# Optimizing a Trainium2 kernel written in Bass

```python
import math
import jax, jax.numpy as jnp
from jax import lax
import numpy as np

D_MODEL = 1024
BATCH = 1
SEQ = 256
DEPTH = 2
DEC_BATCH = 8
DEC_SEQ = 1
PAST_LEN = 1024
PAGE_SIZE = 128

N_META = 16
N_EVEN = (DEPTH + 1) // 2
N_ODD = DEPTH // 2
CHUNK = 128
RET_HEADS = 4
RET_DK = 64
RET_DV = 128
S5_WIDTH = 512
S5_GROUP = 16
S5_GROUPS = S5_WIDTH // S5_GROUP
S5_STATE = 64
RWKV_HEAD = 64
RWKV_WIDTH = 512
RWKV_HEADS = RWKV_WIDTH // RWKV_HEAD
LORA_W = 64
LORA_A = 64
LORA_G = 128
RWKV_PROJ = 3 * RWKV_WIDTH + LORA_W + LORA_A + LORA_G
RWKV_GN_EPS = 64e-5
MLA_HEADS = 8
Q_LORA = 384
KV_LORA = 256
QK_NOPE = 64
QK_ROPE = 32
V_HEAD = 64
MLA_WIDTH = MLA_HEADS * V_HEAD
MLA_SCALE = (QK_NOPE + QK_ROPE) ** -0.5
ROPE_THETA = 10000.0
N_EGROUPS = 4
E_PER_GROUP = 4
N_EXPERTS = N_EGROUPS * E_PER_GROUP
FINE_TOPK = 2
D_EXPERT = 256
DN_ALPHA = (2 * DEPTH) ** 0.25
DN_BETA = (8 * DEPTH) ** -0.25
EVEN_IN = 2 * RET_HEADS * RET_DK + 2 * RET_HEADS * RET_DV + S5_WIDTH
EVEN_OUT = RET_HEADS * RET_DV + S5_WIDTH
ODD_IN = RWKV_PROJ + Q_LORA + KV_LORA + QK_ROPE
ODD_OUT = RWKV_WIDTH + MLA_WIDTH

kernel_name = 'hybrid_retention_s5_rwkv7_mla_hmoe_step'

def layer_norm(x, g, b, eps=1e-5):
    xf = x.astype(jnp.float32)
    mu = jnp.mean(xf, -1, keepdims=True)
    var = jnp.mean(jnp.square(xf - mu), -1, keepdims=True)
    return ((xf - mu) * lax.rsqrt(var + eps)).astype(x.dtype) * g + b

def rms_norm(x, g, eps=1e-6):
    xf = x.astype(jnp.float32)
    return (xf * lax.rsqrt(jnp.mean(jnp.square(xf), -1, keepdims=True) + eps)).astype(x.dtype) * g

def head_norm(x, g, b, eps):
    xf = x.astype(jnp.float32)
    mu = jnp.mean(xf, -1, keepdims=True)
    var = jnp.mean(jnp.square(xf - mu), -1, keepdims=True)
    y = ((xf - mu) * lax.rsqrt(var + eps)).astype(g.dtype)
    return y.reshape(*x.shape[:-2], -1) * g + b

def rope(x, pos):
    d = x.shape[-1]
    inv = ROPE_THETA ** (-jnp.arange(0, d, 2, dtype=jnp.float32) / d)
    ang = pos.astype(jnp.float32)[:, None] * inv[None, :]
    shape = (ang.shape[0],) + (1,) * (x.ndim - 3) + (d // 2,)
    cos = jnp.cos(ang).reshape(shape)
    sin = jnp.sin(ang).reshape(shape)
    x1, x2 = x[..., : d // 2], x[..., d // 2:]
    return jnp.concatenate([x1 * cos - x2 * sin, x1 * sin + x2 * cos], -1).astype(x.dtype)

def retention_chunk(S, q, k, v, log_g):
    L = q.shape[1]
    idx = jnp.arange(L, dtype=jnp.float32)
    diff = idx[:, None] - idx[None, :]
    dmask = jnp.where(diff >= 0, jnp.exp(log_g[:, None, None] * jnp.maximum(diff, 0.0)), 0.0)
    scores = jnp.einsum('bihd,bjhd->bhij', q, k) * dmask
    inner = jnp.einsum('bhij,bjhv->bihv', scores, v)
    cross = jnp.einsum('bihd,bhdv->bihv', q, S) * jnp.exp(log_g[None, None, :, None] * (idx + 1.0)[None, :, None, None])
    kdec = k * jnp.exp(log_g[None, None, :, None] * (L - 1.0 - idx)[None, :, None, None])
    S_new = jnp.exp(log_g * L)[None, :, None, None] * S + jnp.einsum('bjhd,bjhv->bhdv', kdec, v)
    return S_new, inner + cross

def retention(q, k, v, S0, n_lead):
    log_g = jnp.log1p(-jnp.exp2(-5.0 - jnp.arange(RET_HEADS, dtype=jnp.float32)))
    S, o_lead = retention_chunk(S0.astype(jnp.float32), q[:, :n_lead], k[:, :n_lead], v[:, :n_lead], log_g)
    B, T = q.shape[:2]
    rest = T - n_lead
    if rest == 0:
        return o_lead, S

    def to_chunks(t):
        return jnp.moveaxis(t[:, n_lead:].reshape(B, rest // CHUNK, CHUNK, *t.shape[2:]), 1, 0)

    S, o = lax.scan(lambda s, qkv: retention_chunk(s, qkv[0], qkv[1], qkv[2], log_g), S,
                    (to_chunks(q), to_chunks(k), to_chunks(v)))
    o = jnp.moveaxis(o, 0, 1).reshape(B, rest, RET_HEADS, RET_DV)
    return jnp.concatenate([o_lead.astype(o.dtype), o], 1), S

def s5_layer(u, h_re0, h_im0, P, i):
    B, T, _ = u.shape
    f32 = jnp.float32
    ug = u.reshape(B, T, S5_GROUPS, S5_GROUP).astype(f32)
    a_re = P['s5_a_re'][i].astype(f32)
    a_im = P['s5_a_im'][i].astype(f32)
    dt = jnp.exp(P['s5_log_dt'][i].astype(f32))[:, None]
    mag = jnp.exp(dt * a_re)
    ab_re = mag * jnp.cos(dt * a_im)
    ab_im = mag * jnp.sin(dt * a_im)
    den = a_re * a_re + a_im * a_im
    n_re = ab_re - 1.0
    f_re = (n_re * a_re + ab_im * a_im) / den
    f_im = (ab_im * a_re - n_re * a_im) / den
    b_re = P['s5_b_re'][i].astype(f32)
    b_im = P['s5_b_im'][i].astype(f32)
    bb_re = f_re[..., None] * b_re - f_im[..., None] * b_im
    bb_im = f_re[..., None] * b_im + f_im[..., None] * b_re
    bu_re = jnp.einsum('btgc,gpc->btgp', ug, bb_re)
    bu_im = jnp.einsum('btgc,gpc->btgp', ug, bb_im)
    h_re0 = h_re0.astype(f32)
    h_im0 = h_im0.astype(f32)
    bu_re = bu_re.at[:, 0].add(ab_re * h_re0 - ab_im * h_im0)
    bu_im = bu_im.at[:, 0].add(ab_re * h_im0 + ab_im * h_re0)
    A_re = jnp.broadcast_to(ab_re, bu_re.shape)
    A_im = jnp.broadcast_to(ab_im, bu_im.shape)

    def combine(e1, e2):
        a1r, a1i, b1r, b1i = e1
        a2r, a2i, b2r, b2i = e2
        return (a1r * a2r - a1i * a2i, a1r * a2i + a1i * a2r,
                a2r * b1r - a2i * b1i + b2r, a2r * b1i + a2i * b1r + b2i)

    _, _, h_re, h_im = lax.associative_scan(combine, (A_re, A_im, bu_re, bu_im), axis=1)
    y = (jnp.einsum('btgp,gcp->btgc', h_re, P['s5_c_re'][i]) - jnp.einsum('btgp,gcp->btgc', h_im, P['s5_c_im'][i])
         + P['s5_d'][i].reshape(S5_GROUPS, S5_GROUP) * ug).reshape(B, T, S5_WIDTH)
    z = jax.nn.gelu(y)
    out = z * jax.nn.sigmoid(z @ P['s5_w_glu'][i] + P['s5_b_glu'][i])
    return out, h_re[:, -1], h_im[:, -1]

def even_mixer(x, pos, n_lead, S0, h_re0, h_im0, P, i):
    B, T, _ = x.shape
    p = x @ P['ev_w_in'][i]
    o1 = RET_HEADS * RET_DK
    o2 = 2 * o1
    o3 = o2 + RET_HEADS * RET_DV
    o4 = o3 + RET_HEADS * RET_DV
    q = rope(p[..., :o1].reshape(B, T, RET_HEADS, RET_DK), pos) * RET_DK ** -0.5
    k = rope(p[..., o1:o2].reshape(B, T, RET_HEADS, RET_DK), pos)
    v = p[..., o2:o3].reshape(B, T, RET_HEADS, RET_DV)
    gate = p[..., o3:o4]
    u = p[..., o4:]
    o, S = retention(q, k, v, S0, n_lead)
    ret = jax.nn.silu(gate) * head_norm(o, P['ret_gn_g'][i], P['ret_gn_b'][i], 1e-5)
    s5_out, h_re, h_im = s5_layer(u, h_re0, h_im0, P, i)
    mix = jnp.concatenate([ret.astype(x.dtype), s5_out.astype(x.dtype)], -1) @ P['ev_w_out'][i]
    return mix, S, h_re, h_im

def wkv7(r, w, k, v, a, b, S0):
    f32 = jnp.float32

    def step(S, inp):
        r_t, w_t, k_t, v_t, a_t, b_t = inp
        sa = jnp.einsum('bhij,bhj->bhi', S, a_t)
        S = S * w_t[:, :, None, :] + sa[..., None] * b_t[:, :, None, :] + v_t[..., None] * k_t[:, :, None, :]
        return S, jnp.einsum('bhij,bhj->bhi', S, r_t)

    xs = tuple(jnp.moveaxis(t.astype(f32), 1, 0) for t in (r, w, k, v, a, b))
    S, ys = lax.scan(step, S0.astype(f32), xs)
    return jnp.moveaxis(ys, 0, 1), S

def mla_block(q_lat, q_rope, q_pos, c, kr, k_pos):
    s = jnp.einsum('bqhc,bkc->bhqk', q_lat, c) + jnp.einsum('bqhr,bkr->bhqk', q_rope, kr)
    s = s.astype(jnp.float32) * MLA_SCALE
    s = jnp.where(k_pos[None, None, None, :] <= q_pos[None, None, :, None], s, -jnp.inf)
    pr = jax.nn.softmax(s, axis=-1).astype(c.dtype)
    return jnp.einsum('bhqk,bkc->bqhc', pr, c)

def mla_attend(q_lat, q_rope, q_pos, c, kr, k_pos):
    B, T = q_lat.shape[:2]
    if T <= CHUNK:
        return mla_block(q_lat, q_rope, q_pos, c, kr, k_pos)
    nb = -(-T // CHUNK)
    pad = nb * CHUNK - T

    def blocks(t):
        t = jnp.pad(t, ((0, 0), (0, pad)) + ((0, 0),) * (t.ndim - 2))
        return jnp.moveaxis(t.reshape(B, nb, CHUNK, *t.shape[2:]), 1, 0)

    pb = jnp.pad(q_pos, (0, pad), mode='edge').reshape(nb, CHUNK)
    o = lax.map(lambda a: mla_block(a[0], a[1], a[2], c, kr, k_pos), (blocks(q_lat), blocks(q_rope), pb))
    return jnp.moveaxis(o, 0, 1).reshape(B, nb * CHUNK, *o.shape[3:])[:, :T]

def odd_mixer(x, pos, S0, shift0, past_c, past_kr, P, i):
    B, T, _ = x.shape
    W = RWKV_WIDTH
    p = x @ P['od_w_in'][i]
    pr = p[..., :RWKV_PROJ]
    qa = p[..., RWKV_PROJ:RWKV_PROJ + Q_LORA]
    ckv = p[..., RWKV_PROJ + Q_LORA:RWKV_PROJ + Q_LORA + KV_LORA]
    kr = p[..., RWKV_PROJ + Q_LORA + KV_LORA:]
    prev = jnp.concatenate([shift0[:, None].astype(pr.dtype), pr[:, :-1]], 1)
    xm = pr + (prev - pr) * P['rwkv_mu'][i]
    r = xm[..., :W]
    k = xm[..., W:2 * W]
    v = xm[..., 2 * W:3 * W]
    xw = xm[..., 3 * W:3 * W + LORA_W]
    xa = xm[..., 3 * W + LORA_W:3 * W + LORA_W + LORA_A]
    xg = xm[..., 3 * W + LORA_W + LORA_A:]
    w = -jax.nn.softplus(-(P['rwkv_w0'][i] + jnp.tanh(xw) @ P['rwkv_w2'][i])) - 0.5
    decay = jnp.exp(-jnp.exp(w.astype(jnp.float32)))
    a = jax.nn.sigmoid(P['rwkv_a0'][i] + xa @ P['rwkv_a2'][i])
    g = jax.nn.sigmoid(xg) @ P['rwkv_g2'][i]

    def hs(t):
        return t.reshape(B, T, RWKV_HEADS, RWKV_HEAD)

    kk = hs((k * P['rwkv_k_k'][i]).astype(jnp.float32))
    kk = kk / jnp.maximum(jnp.sqrt(jnp.sum(kk * kk, -1, keepdims=True)), 1e-12)
    k = k * (1.0 + (a - 1.0) * P['rwkv_k_a'][i])
    y, S = wkv7(hs(r), hs(decay), hs(k), hs(v), -kk, kk * hs(a), S0)
    y = head_norm(y, P['rwkv_gn_g'][i], P['rwkv_gn_b'][i], RWKV_GN_EPS)
    bonus = jnp.sum(hs(r) * hs(k) * P['rwkv_r_k'][i], -1, keepdims=True) * hs(v)
    y_c = (y + bonus.reshape(B, T, W)) * g
    qa = rms_norm(qa, P['mla_q_norm'][i])
    q = (qa @ P['mla_w_qb'][i]).reshape(B, T, MLA_HEADS, QK_NOPE + QK_ROPE)
    q_nope = q[..., :QK_NOPE]
    q_rope = rope(q[..., QK_NOPE:], pos)
    c = rms_norm(ckv, P['mla_kv_norm'][i])
    kr = rope(kr, pos)
    q_lat = jnp.einsum('bthn,chn->bthc', q_nope, P['mla_w_uk'][i])
    if past_c is None:
        c_all, kr_all, k_pos = c, kr, pos
    else:
        c_all = jnp.concatenate([past_c.astype(c.dtype), c], 1)
        kr_all = jnp.concatenate([past_kr.astype(kr.dtype), kr], 1)
        k_pos = jnp.arange(c_all.shape[1], dtype=jnp.int32)
    o_lat = mla_attend(q_lat, q_rope, pos, c_all, kr_all, k_pos)
    y_d = jnp.einsum('bthc,chv->bthv', o_lat, P['mla_w_uv'][i]).reshape(B, T, MLA_WIDTH)
    mix = jnp.concatenate([y_c.astype(x.dtype), y_d.astype(x.dtype)], -1) @ P['od_w_out'][i]
    return mix, S, pr[:, -1], c, kr

def hier_moe(x, P, l):
    B, T, D = x.shape
    xf = x.reshape(B * T, D)
    lc = (xf @ P['moe_w_coarse'][l] + P['moe_b_coarse'][l]).astype(jnp.float32)
    pc = jax.nn.softmax(lc, -1)
    gsel = jnp.argmax(lc, -1)
    gate_c = jnp.take_along_axis(pc, gsel[:, None], 1)
    lf = jnp.einsum('nd,gde->nge', xf, P['moe_w_fine'][l]) + P['moe_b_fine'][l]
    lf = jnp.take_along_axis(lf, gsel[:, None, None], 1)[:, 0].astype(jnp.float32)
    tv, ti = lax.top_k(lf, FINE_TOPK)
    wf = jax.nn.softmax(tv, -1) * gate_c
    eid = gsel[:, None] * E_PER_GROUP + ti
    comb = jnp.sum(jax.nn.one_hot(eid, N_EXPERTS, dtype=jnp.float32) * wf[..., None], 1)
    h = jax.nn.silu(jnp.einsum('nd,edf->nef', xf, P['moe_w_gate'][l])) * jnp.einsum('nd,edf->nef', xf, P['moe_w_up'][l])
    y = jnp.einsum('nef,efd->nd', h * comb[..., None].astype(h.dtype), P['moe_w_down'][l])
    return y.reshape(B, T, D)

def trunk(x, pos, n_lead, ret0, s5re0, s5im0, wkv0, shift0, past, P):
    ret_l, s5re_l, s5im_l, wkv_l, shift_l, kv_l, kr_l = [], [], [], [], [], [], []
    for layer in range(DEPTH):
        i = layer // 2
        if layer % 2 == 0:
            mix, S, h_re, h_im = even_mixer(x, pos, n_lead, ret0[i], s5re0[i], s5im0[i], P, i)
            ret_l.append(S)
            s5re_l.append(h_re)
            s5im_l.append(h_im)
        else:
            if past is None:
                past_c = None
                past_kr = None
            else:
                cache_kv, cache_krope, page_table = past
                nb = page_table.shape[0]
                past_c = cache_kv[page_table, i].reshape(nb, -1, KV_LORA)
                past_kr = cache_krope[page_table, i].reshape(nb, -1, QK_ROPE)
            mix, S, sh, c, kr = odd_mixer(x, pos, wkv0[i], shift0[i], past_c, past_kr, P, i)
            wkv_l.append(S)
            shift_l.append(sh)
            kv_l.append(c)
            kr_l.append(kr)
        x = layer_norm(DN_ALPHA * x + mix.astype(x.dtype), P['ln1_g'][layer], P['ln1_b'][layer])
        x = layer_norm(DN_ALPHA * x + hier_moe(x, P, layer).astype(x.dtype), P['ln2_g'][layer], P['ln2_b'][layer])
    new = (jnp.stack(ret_l), jnp.stack(s5re_l), jnp.stack(s5im_l), jnp.stack(wkv_l), jnp.stack(shift_l),
           jnp.stack(kv_l, 1), jnp.stack(kr_l, 1))
    return x, new

def setup_inputs(seed: int = 0) -> dict:
    key = jax.random.key(seed)
    ks = iter(jax.random.split(key, 80))
    f32 = jnp.float32

    def nrm(shape, scale=1.0):
        return jax.random.normal(next(ks), shape, f32) * scale

    def unif(shape, lo, hi):
        return jax.random.uniform(next(ks), shape, f32, lo, hi)

    n_pages = PAST_LEN // PAGE_SIZE
    n_pool = -(-5 * DEC_BATCH * n_pages // 4)
    NE, NO = N_EVEN, N_ODD
    inp = {}
    inp['x_prompt'] = nrm((BATCH, SEQ, D_MODEL))
    inp['x_sample'] = nrm((DEC_BATCH, DEC_SEQ, D_MODEL))
    inp['state_ret'] = nrm((NE, DEC_BATCH, RET_HEADS, RET_DK, RET_DV), 0.5)
    inp['state_s5_re'] = nrm((NE, DEC_BATCH, S5_GROUPS, S5_STATE), 0.1)
    inp['state_s5_im'] = nrm((NE, DEC_BATCH, S5_GROUPS, S5_STATE), 0.1)
    inp['state_wkv'] = nrm((NO, DEC_BATCH, RWKV_HEADS, RWKV_HEAD, RWKV_HEAD), 0.1)
    inp['state_shift'] = nrm((NO, DEC_BATCH, RWKV_PROJ))
    inp['cache_kv'] = nrm((n_pool, NO, PAGE_SIZE, KV_LORA))
    inp['cache_krope'] = nrm((n_pool, NO, PAGE_SIZE, QK_ROPE))
    inp['page_table'] = jax.random.permutation(next(ks), n_pool)[:DEC_BATCH * n_pages].reshape(DEC_BATCH, n_pages).astype(jnp.int32)
    inp['meta_tokens'] = nrm((N_META, D_MODEL))
    inp['ev_w_in'] = nrm((NE, D_MODEL, EVEN_IN), D_MODEL ** -0.5)
    inp['ret_gn_g'] = 1.0 + nrm((NE, RET_HEADS * RET_DV), 0.02)
    inp['ret_gn_b'] = nrm((NE, RET_HEADS * RET_DV), 0.02)
    inp['s5_a_re'] = -0.5 + nrm((NE, S5_GROUPS, S5_STATE), 0.01)
    inp['s5_a_im'] = jnp.pi * jnp.arange(S5_STATE, dtype=f32) + nrm((NE, S5_GROUPS, S5_STATE), 0.01)
    inp['s5_log_dt'] = unif((NE, S5_GROUPS), math.log(1e-3), math.log(1e-1))
    inp['s5_b_re'] = nrm((NE, S5_GROUPS, S5_STATE, S5_GROUP), (2 * S5_GROUP) ** -0.5)
    inp['s5_b_im'] = nrm((NE, S5_GROUPS, S5_STATE, S5_GROUP), (2 * S5_GROUP) ** -0.5)
    inp['s5_c_re'] = nrm((NE, S5_GROUPS, S5_GROUP, S5_STATE), S5_STATE ** -0.5)
    inp['s5_c_im'] = nrm((NE, S5_GROUPS, S5_GROUP, S5_STATE), S5_STATE ** -0.5)
    inp['s5_d'] = nrm((NE, S5_WIDTH))
    inp['s5_w_glu'] = nrm((NE, S5_WIDTH, S5_WIDTH), S5_WIDTH ** -0.5)
    inp['s5_b_glu'] = nrm((NE, S5_WIDTH), 0.02)
    inp['ev_w_out'] = nrm((NE, EVEN_OUT, D_MODEL), EVEN_OUT ** -0.5 * DN_BETA)
    inp['od_w_in'] = nrm((NO, D_MODEL, ODD_IN), D_MODEL ** -0.5)
    inp['rwkv_mu'] = unif((NO, RWKV_PROJ), 0.0, 1.0)
    inp['rwkv_w0'] = unif((NO, RWKV_WIDTH), -6.0, -1.0)
    inp['rwkv_w2'] = nrm((NO, LORA_W, RWKV_WIDTH), 0.3 * LORA_W ** -0.5)
    inp['rwkv_a0'] = nrm((NO, RWKV_WIDTH), 0.1)
    inp['rwkv_a2'] = nrm((NO, LORA_A, RWKV_WIDTH), LORA_A ** -0.5)
    inp['rwkv_g2'] = nrm((NO, LORA_G, RWKV_WIDTH), LORA_G ** -0.5)
    inp['rwkv_k_k'] = 0.85 + nrm((NO, RWKV_WIDTH), 0.02)
    inp['rwkv_k_a'] = 1.0 + nrm((NO, RWKV_WIDTH), 0.02)
    inp['rwkv_r_k'] = nrm((NO, RWKV_HEADS, RWKV_HEAD), 0.1)
    inp['rwkv_gn_g'] = 1.0 + nrm((NO, RWKV_WIDTH), 0.02)
    inp['rwkv_gn_b'] = nrm((NO, RWKV_WIDTH), 0.02)
    inp['mla_q_norm'] = 1.0 + nrm((NO, Q_LORA), 0.02)
    inp['mla_w_qb'] = nrm((NO, Q_LORA, MLA_HEADS * (QK_NOPE + QK_ROPE)), Q_LORA ** -0.5)
    inp['mla_kv_norm'] = 1.0 + nrm((NO, KV_LORA), 0.02)
    inp['mla_w_uk'] = nrm((NO, KV_LORA, MLA_HEADS, QK_NOPE), KV_LORA ** -0.5)
    inp['mla_w_uv'] = nrm((NO, KV_LORA, MLA_HEADS, V_HEAD), KV_LORA ** -0.5)
    inp['od_w_out'] = nrm((NO, ODD_OUT, D_MODEL), ODD_OUT ** -0.5 * DN_BETA)
    inp['ln1_g'] = 1.0 + nrm((DEPTH, D_MODEL), 0.02)
    inp['ln1_b'] = nrm((DEPTH, D_MODEL), 0.02)
    inp['ln2_g'] = 1.0 + nrm((DEPTH, D_MODEL), 0.02)
    inp['ln2_b'] = nrm((DEPTH, D_MODEL), 0.02)
    inp['moe_w_coarse'] = nrm((DEPTH, D_MODEL, N_EGROUPS), D_MODEL ** -0.5)
    inp['moe_b_coarse'] = nrm((DEPTH, N_EGROUPS), 0.01)
    inp['moe_w_fine'] = nrm((DEPTH, N_EGROUPS, D_MODEL, E_PER_GROUP), D_MODEL ** -0.5)
    inp['moe_b_fine'] = nrm((DEPTH, N_EGROUPS, E_PER_GROUP), 0.01)
    inp['moe_w_gate'] = nrm((DEPTH, N_EXPERTS, D_MODEL, D_EXPERT), D_MODEL ** -0.5)
    inp['moe_w_up'] = nrm((DEPTH, N_EXPERTS, D_MODEL, D_EXPERT), D_MODEL ** -0.5)
    inp['moe_w_down'] = nrm((DEPTH, N_EXPERTS, D_EXPERT, D_MODEL), D_EXPERT ** -0.5 * DN_BETA)
    return inp

def reference(x_prompt, x_sample, state_ret, state_s5_re, state_s5_im, state_wkv, state_shift,
              cache_kv, cache_krope, page_table, meta_tokens,
              ev_w_in, ret_gn_g, ret_gn_b, s5_a_re, s5_a_im, s5_log_dt, s5_b_re, s5_b_im, s5_c_re, s5_c_im,
              s5_d, s5_w_glu, s5_b_glu, ev_w_out,
              od_w_in, rwkv_mu, rwkv_w0, rwkv_w2, rwkv_a0, rwkv_a2, rwkv_g2, rwkv_k_k, rwkv_k_a, rwkv_r_k,
              rwkv_gn_g, rwkv_gn_b, mla_q_norm, mla_w_qb, mla_kv_norm, mla_w_uk, mla_w_uv, od_w_out,
              ln1_g, ln1_b, ln2_g, ln2_b, moe_w_coarse, moe_b_coarse, moe_w_fine, moe_b_fine,
              moe_w_gate, moe_w_up, moe_w_down):
    P = dict(ev_w_in=ev_w_in, ret_gn_g=ret_gn_g, ret_gn_b=ret_gn_b, s5_a_re=s5_a_re, s5_a_im=s5_a_im,
             s5_log_dt=s5_log_dt, s5_b_re=s5_b_re, s5_b_im=s5_b_im, s5_c_re=s5_c_re, s5_c_im=s5_c_im,
             s5_d=s5_d, s5_w_glu=s5_w_glu, s5_b_glu=s5_b_glu, ev_w_out=ev_w_out,
             od_w_in=od_w_in, rwkv_mu=rwkv_mu, rwkv_w0=rwkv_w0, rwkv_w2=rwkv_w2, rwkv_a0=rwkv_a0,
             rwkv_a2=rwkv_a2, rwkv_g2=rwkv_g2, rwkv_k_k=rwkv_k_k, rwkv_k_a=rwkv_k_a, rwkv_r_k=rwkv_r_k,
             rwkv_gn_g=rwkv_gn_g, rwkv_gn_b=rwkv_gn_b, mla_q_norm=mla_q_norm, mla_w_qb=mla_w_qb,
             mla_kv_norm=mla_kv_norm, mla_w_uk=mla_w_uk, mla_w_uv=mla_w_uv, od_w_out=od_w_out,
             ln1_g=ln1_g, ln1_b=ln1_b, ln2_g=ln2_g, ln2_b=ln2_b, moe_w_coarse=moe_w_coarse,
             moe_b_coarse=moe_b_coarse, moe_w_fine=moe_w_fine, moe_b_fine=moe_b_fine,
             moe_w_gate=moe_w_gate, moe_w_up=moe_w_up, moe_w_down=moe_w_down)
    f32 = jnp.float32
    B = x_prompt.shape[0]
    xp = jnp.concatenate([jnp.broadcast_to(meta_tokens[None].astype(x_prompt.dtype), (B, N_META, D_MODEL)), x_prompt], 1)
    pos_p = jnp.arange(xp.shape[1], dtype=jnp.int32)
    ret0 = jnp.zeros((N_EVEN, B, RET_HEADS, RET_DK, RET_DV), f32)
    s50 = jnp.zeros((N_EVEN, B, S5_GROUPS, S5_STATE), f32)
    wkv0 = jnp.zeros((N_ODD, B, RWKV_HEADS, RWKV_HEAD, RWKV_HEAD), f32)
    sh0 = jnp.zeros((N_ODD, B, RWKV_PROJ), x_prompt.dtype)
    yp, (ret_p, s5re_p, s5im_p, wkv_p, shift_p, kv_p, kr_p) = trunk(
        xp, pos_p, N_META, ret0, s50, s50, wkv0, sh0, None, P)
    pos_s = PAST_LEN + jnp.arange(x_sample.shape[1], dtype=jnp.int32)
    ys, (ret_s, s5re_s, s5im_s, wkv_s, shift_s, kv_s, kr_s) = trunk(
        x_sample, pos_s, x_sample.shape[1], state_ret, state_s5_re, state_s5_im, state_wkv, state_shift,
        (cache_kv, cache_krope, page_table), P)
    return (yp[:, N_META:], ys, ret_p, ret_s, s5re_p, s5re_s, s5im_p, s5im_s, wkv_p, wkv_s,
            shift_p, shift_s, kv_p, kv_s, kr_p, kr_s)


_drawn_inputs = setup_inputs


def setup_inputs(seed=0):
    import zlib

    import numpy as np

    out = dict(_drawn_inputs(seed))
    spreads = {}
    factors = {'cache_kv': 4.469,
     'cache_krope': 8.0,
     'ret_gn_g': 6.954,
     'ret_gn_b': 6.035,
     's5_a_re': 59.494,
     's5_c_re': 3.343,
     's5_c_im': 6.156,
     's5_b_glu': 24.997,
     'rwkv_w2': 4.094,
     'rwkv_k_k': 24.976,
     'rwkv_gn_g': 85.093,
     'rwkv_gn_b': 78.724,
     'mla_q_norm': 8.0,
     'mla_kv_norm': 8.453,
     'moe_b_coarse': 8.0,
     'moe_b_fine': 8.0,
     'rwkv_r_k': 6.519}
    for name, (base, spread) in spreads.items():
        noise = np.random.default_rng([zlib.crc32(name.encode()), seed]).standard_normal(out[name].shape)
        drawn = base * np.exp(spread * noise) if base else spread * noise
        out[name] = __import__('jax').numpy.asarray(drawn.astype(out[name].dtype))
    for name, factor in factors.items():
        out[name] = (out[name] * factor).astype(out[name].dtype)
    return out
```

```python
import math
from contextlib import ExitStack

import numpy as np

import concourse.bass as bass
from concourse import mybir

F32 = mybir.dt.float32
I32 = mybir.dt.int32
ALU = mybir.AluOpType
ACT = mybir.ActivationFunctionType
AX = mybir.AxisListType

P = 128
D = 1024
KD = D // P
NM, SEQ, NB = 16, 256, 8
NPR = NM + SEQ
NT = NPR + NB
TT = [(0, 128), (128, 128), (256, NT - 256)]
PT = [(0, 128), (128, 128), (256, NPR - 256)]
PAST, PAGE = 1024, 128
NPG = PAST // PAGE
ALPHA = 4.0 ** 0.25
RH, RDK, RDV = 4, 64, 128
SG_N, SC_N, SP_N = 32, 16, 64
GP = SG_N // 2
CL = 8
NCH = NPR // CL
UCOL = NCH + 2 * NB
HCOL = NCH + NB
W = 512
WH, WD = 8, 64
WC = 32
LORA = 64
RP = 1792
RT_N = RP // P
DECAY = math.exp(-0.5)
MH, NOPE, ROPE, VH = 8, 64, 32, 64
QL, KVL = 384, 256
SCALE = (NOPE + ROPE) ** -0.5
NE, DE = 16, 256
NG, EG = 4, 4
CAP = P
BIG = 1.0e30

CONSTS = [("ident", P), ("ones", P), ("blk", P), ("id64", 64), ("perm64", P), ("perm32", P),
          ("cosd", NT), ("sind", NT), ("cosr", NT), ("sinr", NT),
          ("retmask", RH * NPR), ("kdec", 3 * RH), ("gam", 1), ("selbh", NB * RH),
          ("strictT", P), ("inclT", P), ("m2T", P), ("m2N", P),
          ("off2", P), ("off4", P), ("off8", P), ("off16", P),
          ("scan", NPR), ("causal", P), ("curmask", NB), ("rank", 4), ("eps", 4), ("before", P), ("iota", P)]
COFF = {}
_o = 0
for _n, _w in CONSTS:
    COFF[_n] = (_o, _w)
    _o += _w
NCONST = _o


def const_table():
    c = {n: np.zeros((P, w), np.float64) for n, w in CONSTS}
    i = np.arange(P)
    c["ident"] = np.eye(P)
    c["ones"][:] = 1.0
    c["id64"] = (i[:, None] % 64 == np.arange(64)[None, :]).astype(float)
    c["blk"] = (i[:, None] // 64 == i[None, :] // 64).astype(float)
    for name, d in (("perm64", 64), ("perm32", 32)):
        for m in range(P):
            if m % d < d // 2:
                c[name][m + d // 2, m] = -1.0
            else:
                c[name][m - d // 2, m] = 1.0
    pos = np.concatenate([np.arange(NPR), np.full(NB, PAST)]).astype(np.float32)
    for d, names in ((64, ("cosd", "sind")), (32, ("cosr", "sinr"))):
        inv = (10000.0 ** (-np.arange(0, d, 2, dtype=np.float32) / np.float32(d))).astype(np.float32)
        ang = (pos[None, :] * inv[:, None]).astype(np.float32)[i % (d // 2)]
        c[names[0]], c[names[1]] = np.cos(ang.astype(np.float64)), np.sin(ang.astype(np.float64))
    logg = np.log1p(-np.exp2(-5.0 - np.arange(RH)))
    x = np.arange(NPR)
    diff = x[None, :] - i[:, None]
    c["retmask"] = np.concatenate([np.where(diff >= 0, np.exp(logg[h] * np.maximum(diff, 0)), 0.0) for h in range(RH)], 1)
    c["kdec"] = np.stack([np.exp(logg[h] * np.maximum(NPR - 1 - (128 * t + i), 0)) for t in range(3) for h in range(RH)], 1)
    h_of = (i // 4) % RH
    c["gam"] = np.exp(logg[h_of])[:, None]
    c["selbh"] = ((i[:, None] // 4 // RH == np.arange(RH * NB)[None, :] % NB) &
                  (h_of[:, None] == np.arange(RH * NB)[None, :] // NB)).astype(float)
    a, b = i[:, None], i[None, :]
    blk = a // WC == b // WC
    c["strictT"] = (blk & (a < b)).astype(float)
    c["inclT"] = (blk & (a <= b)).astype(float)
    c["m2T"] = ((a // 2 == b // 2) & (a < b)).astype(float)
    c["m2N"] = ((a // 2 == b // 2) & (b < a)).astype(float)
    for s in (2, 4, 8, 16):
        c[f"off{s}"] = ((a // (2 * s) == b // (2 * s)) & (a // s > b // s)).astype(float)
    c["scan"] = np.broadcast_to((x % WC != 0).astype(float), (P, NPR))
    c["causal"] = np.where(b <= a, 0.0, -BIG)
    c["curmask"] = np.where((i[:, None] // MH) == np.arange(NB)[None, :], 0.0, -BIG)
    c["rank"] = np.broadcast_to(np.array([4.0, 3.0, 2.0, 1.0]), (P, 4))
    c["eps"] = np.broadcast_to(np.array([1e-5, 64e-5, 1e-6, 0.0]), (P, 4))
    c["before"] = (a < b).astype(float)
    c["iota"] = np.broadcast_to(i[None, :].astype(float), (P, P))
    return np.ascontiguousarray(np.concatenate([c[n] for n, _ in CONSTS], 1).astype(np.float32))


VECS = [("ret_gn_g", 4), ("ret_gn_b", 4), ("s5_d", 4), ("s5_b_glu", 4), ("rwkv_mu", 14), ("rwkv_w0", 4),
        ("rwkv_a0", 4), ("rwkv_k_k", 4), ("rwkv_k_a", 4), ("rwkv_r_k", 4), ("rwkv_gn_g", 4), ("rwkv_gn_b", 4),
        ("mla_q_norm", 3), ("mla_kv_norm", 2), ("ln1_g", 16), ("ln1_b", 16), ("ln2_g", 16), ("ln2_b", 16)]
VOFF = {}
_o = 0
for _n, _w in VECS:
    VOFF[_n] = _o
    _o += _w
NVEC = _o

NSLOT = 6
SLOTF = 2048
U0 = 6
EV_ORDER = [6, 7, 0, 1, 2, 3, 4, 5]
S_EV, S_GLU, S_EVO = 0, 8, 9
S_MOE = [13, 78]
S_OD = 61
S_QB, S_UKV, S_ODO = 71, 73, 74


V_GROUP = 16
V_UP, V_DOWN = [1, 2, 5, 8], [4, 7, 10, 16]


class Ring:

    def __init__(self, eng, banks, full, free):
        self.eng, self.banks, self.full, self.free = eng, banks, full, free
        self.n, self.slot, self.deep = 0, 0, len(banks)

    def claim(self):
        if not (isinstance(self.n, int) and self.n < self.deep):
            self.eng.wait_ge(self.free, self.n - (self.deep - 1))
        return self._next()

    def take(self):
        self.eng.wait_ge(self.full, self.n + 1)
        return self._next()

    def _next(self):
        b = self.banks[self.slot]
        self.n, self.slot = self.n + 1, (self.slot + 1) % self.deep
        return b


class Steps:

    def __init__(self, eng, own):
        self.eng, self.own, self.n = eng, own, {}

    def mark(self, ins, sem):
        ins.then_inc(sem, 1)
        self.n[sem.name] = self.n.get(sem.name, 0) + 1

    def do(self, ins, sem=None):
        sem = self.own if sem is None else sem
        self.mark(ins, sem)
        self.eng.wait_ge(sem, self.n[sem.name])


SCRATCH = 30700
M_QK, M_GATE, M_VF, M_UF = 0, 1120, 2240, 3360
M_R1, M_R2, M_R3, M_R4, M_R5 = 4480, 8576, 12672, 17280, 21376
M_INJ, M_HS, M_PW, M_SV, M_BB = 25984, 27584, 28928, 29216, 29280


def SLOT_view(SLOT, n, k, c, o=0):
    return SLOT[:, n % NSLOT, o:o + k * c].rearrange("p (k c) -> p k c", k=k)


def program(nc, a, outs):
    sems = {}

    with ExitStack() as ctx:
        def sb(name, shape, dt=F32):
            return ctx.enter_context(nc.sbuf_tensor(name, shape, dt))

        def sem(name):
            return ctx.enter_context(nc.semaphore(name))

        def ev(name):
            if name not in sems:
                sems[name] = sem(name)
            return sems[name]

        CST = sb("consts", [P, NCONST])
        VC = sb("vec_cols", [P, P])
        RW = sb("router_w", [P, 2, KD, 20])
        RB = sb("router_b", [P, 2, 20])
        XT = sb("x_fm", [P, KD, NT])
        RES = sb("residual", [P, KD, NT])
        SLOT = sb("weight_slots", [P, NSLOT, SLOTF])
        S = sb("scratch", [P, SCRATCH])
        banks = [ctx.enter_context(nc.psum_tensor(f"bank{i}", [P, 512], F32)) for i in range(8)]
        VB, AB = banks[:4], banks[4:]
        v_full, v_free, a_full, a_free = sem("v_full"), sem("v_free"), sem("a_full"), sem("a_free")
        w_in = [sem(f"w_in{i}") for i in range(NSLOT)]
        dve_step, act_step, pool_step = sem("dve_step"), sem("act_step"), sem("pool_step")

        def dram(name, shape):
            return nc.dram_tensor(name, shape, F32, kind="Internal").ap()

        u_dram, y_dram = dram("u_tok_dram", [NT, 512]), dram("y_tok_dram", [NT, 512])
        srow_dram = dram("srow_dram", [NB, 1024])

        def cst(name):
            o, w = COFF[name]
            return CST[:, o:o + w]

        def vec(name, i=0, n=1):
            o = VOFF[name] + i
            return VC[:, o:o + n]

        def part(o, *dims):
            n = int(np.prod(dims))
            assert o + n <= SCRATCH, (o, dims)
            v = S[:, o:o + n]
            if len(dims) == 1:
                return v
            names = "abcd"[:len(dims)]
            return v.rearrange("p (" + " ".join(names) + ") -> p " + " ".join(names), **dict(zip(names[1:], dims[1:])))

        def resv(o, *dims):
            v = RES[:, :, :].rearrange("p k t -> p (k t)")[:, o:o + int(np.prod(dims))]
            if len(dims) == 1:
                return v
            names = "abcd"[:len(dims)]
            return v.rearrange("p (" + " ".join(names) + ") -> p " + " ".join(names), **dict(zip(names[1:], dims[1:])))

        ident = cst("ident")
        eps = {1e-5: cst("eps")[:, 0:1], 64e-5: cst("eps")[:, 1:2], 1e-6: cst("eps")[:, 2:3]}

        QK, GATE, VF, UF = (part(o, 4, NT) for o in (M_QK, M_GATE, M_VF, M_UF))
        XTOK, VROW = part(M_R4, 3, D), part(M_R4 + 3072, P)
        UTOK = part(M_R4, 3, 512)
        BI = part(M_R1, 2, GP, CL, SC_N)
        UC = part(M_R1, CL, 512)
        TP = part(M_R2, 2, GP, CL, SC_N)
        BIT = part(M_R2, 2, GP, P)
        TD = part(M_R3, 2, GP, CL + 1, SC_N)
        KL = part(M_R3, SG_N, P)
        Y = part(M_R3, CL, 512)
        KT_ = part(M_R4, SG_N, P)
        CP = part(M_R5, 2, GP, CL + 1, SC_N)
        UG = resv(0, SG_N, UCOL)
        UCQ = part(M_INJ, 2, 8, CL, SC_N)
        INJ = part(M_INJ, 2, GP, UCOL)
        HS = part(M_HS, 2, GP, HCOL)
        BRAW, CN = part(M_HS, 2, GP, SC_N), part(M_HS + 512, 2, 2, P)
        PW = part(M_PW, 2, CL + 1, GP)
        SV = part(M_SV, 4, GP)
        BB, CTT = part(M_BB, 2, GP, SC_N), part(M_BB + 512, 2, GP, SC_N)
        ROWS = resv(0, 15, P)
        A_RE, A_IM, LDT = ROWS[0:GP, 0, :], ROWS[0:GP, 1, :], ROWS[0:GP, 2, 0:2]
        YTOK, TOUT = part(M_R1, 3, 512), part(M_R1 + 1536, 16, RDV)
        YF, ZF = part(M_R2, 4, NT), part(M_R2 + 1120, 4, NT)
        MIXS, MIXR = part(M_INJ, 4, NT), part(M_HS, 4, NT)
        KTOK, VTOK, KDT = part(M_R4, 3, 256), part(M_R4 + 768, 3, 512), part(M_R4 + 2304, 3, 256)
        SROW = part(M_R4 + 3072, D)
        SCR = part(M_R5, RH, 3, NPR)
        RSTO = part(M_R5 + RH * 3 * NPR, RH, RDV)
        OT, OSQ, OSD = part(M_R3, 4, NT), part(M_R3 + 1120, 4, NT), part(M_R3 + 2240, 4, NT)
        HROW = part(M_R2 + 2240, 4, P)
        H0R = part(30304, 2, P)
        HF = part(M_BB, 2, NB, GP)
        HFP = part(M_BB + 256, 2, GP)
        RETS = resv(0, 16, RDV)
        KS, QS, VS = part(M_BB + 512, 16), part(M_BB + 528, 16), part(M_BB + 544, RDV)
        PARTO = part(M_BB + 672, RDV)
        CB = part(0, EG, NG, CAP)
        SIL, HB = part(2048, 2, 2, CAP), part(2560, 2, 2, CAP)
        TM = part(3072, 2, 2, CAP)
        LG, RT = part(3584, 3, 20), part(3650, 10, 3, 16)
        WGT = part(4136, NG, CAP)
        DSP = part(4648, 3, NG, CAP)
        DSPT = part(6184, NG, NT)
        POS = part(7304, 3, NG)
        PLACE = part(7316, 3)
        CNT = part(7320, NG)
        XTM = part(10752, 3, D)
        XG = part(13824, KD, CAP)
        YG = part(14848, NG, D)
        XW, XSIL, XHB = part(10752, 3, SLOTF), part(16896, 2, NT), part(17456, 2, NT)
        XCT, XC, XROW = part(18016, NT), part(18300, 3, NE), part(18350, NT)
        OVER = ctx.enter_context(nc.sbuf_tensor("over_capacity", [P, 2], I32))
        LSQ, LSD = part(8200, KD, NT), part(10440, NT)

        x_loads = [
            (XTOK[0:NM, 0, :], a["meta_tokens"]),
            (XTOK[NM:P, 0, :], a["x_prompt"][0, 0:P - NM, :]),
            (XTOK[:, 1, :], a["x_prompt"][0, P - NM:2 * P - NM, :]),
            (XTOK[0:NM, 2, :], a["x_prompt"][0, 2 * P - NM:SEQ, :]),
            (XTOK[NM:NM + NB, 2, :], a["x_sample"].rearrange("b s d -> (b s) d")),
            (CST[:, :], a["consts"]),
        ]
        def rows_of(name):
            v = a[name]
            if len(v.shape) == 3:
                v = v.rearrange("l h d -> l (h d)")
            return v.rearrange("l (t p) -> (l t) p", p=P)

        vec_loads = [(VROW[VOFF[n]:VOFF[n] + w, :], rows_of(n)) for n, w in VECS]
        s5_loads = [
            (A_RE, a["s5_a_re"][0].rearrange("(g two) s -> g (two s)", two=2)),
            (A_IM, a["s5_a_im"][0].rearrange("(g two) s -> g (two s)", two=2)),
            (LDT, a["s5_log_dt"].rearrange("l (g two) -> (l g) two", two=2)),
        ]
        for j, n in enumerate(("s5_b_re", "s5_b_im")):
            s5_loads.append((BRAW[:, j], a[n][0].rearrange("(g two) s c -> (two s) g c", two=2)))
        for j, n in enumerate(("s5_c_re", "s5_c_im")):
            for t in range(2):
                for two in range(2):
                    s5_loads.append((CN[:, j, t, two * SP_N:(two + 1) * SP_N],
                                     a[n][0].rearrange("(t g two) c s -> t two g c s", t=2, two=2)[t, two]))
        router_loads = []
        for l in range(2):
            router_loads.append((RW[:, l, :, 0:4], a["moe_w_coarse"][l].rearrange("(k p) g -> p k g", p=P)))
            for g in range(4):
                router_loads.append((RW[:, l, :, 4 + 4 * g:8 + 4 * g], a["moe_w_fine"][l, g].rearrange("(k p) e -> p k e", p=P)))
            router_loads.append((RB[:, l, 0:4], a["moe_b_coarse"][l:l + 1, :].to_broadcast([P, 4])))
            router_loads.append((RB[:, l, 4:20], a["moe_b_fine"][l:l + 1].rearrange("l g e -> l (g e)").to_broadcast([P, 16])))

        fills, od9 = {}, []
        for j, s in enumerate(EV_ORDER):
            fills[S_EV + j] = [(SLOT_view(SLOT, S_EV + j, KD, 256), a["ev_w_in"][0].rearrange("(k p) c -> p k c", p=P)[:, :, 256 * s:256 * s + 256])]
        w9 = SLOT_view(SLOT, S_OD + 9, KD, 256)
        odw = a["od_w_in"][0].rearrange("(k p) c -> p k c", p=P)
        for i in range(4):
            od9.append((w9[:, :, P + ROPE * i:P + ROPE * i + ROPE], odw[:, :, 2432:2464]))
        od9.append((w9[:, :, 0:P], odw[:, :, 2304:2432]))
        fills[S_GLU] = [(SLOT_view(SLOT, S_GLU, 4, 512), a["s5_w_glu"][0].rearrange("(k p) c -> p k c", p=P))]
        for j in range(4):
            fills[S_EVO + j] = [(SLOT_view(SLOT, S_EVO + j, KD, 256), a["ev_w_out"][0].rearrange("(k p) c -> p k c", p=P)[:, :, 256 * j:256 * j + 256])]
        for l in range(2):
            for e in range(NE):
                n = S_MOE[l] + 3 * e
                fills[n] = [(SLOT_view(SLOT, n, KD, DE), a["moe_w_gate"][l, e].rearrange("(k p) c -> p k c", p=P))]
                fills[n + 1] = [(SLOT_view(SLOT, n + 1, KD, DE), a["moe_w_up"][l, e].rearrange("(k p) c -> p k c", p=P))]
                fills[n + 2] = [(SLOT_view(SLOT, n + 2, 2, D), a["moe_w_down"][l, e].rearrange("(k p) c -> p k c", p=P))]
        fills[S_OD + 9] = od9
        for j in range(9):
            w = 256
            fills[S_OD + j] = [(SLOT_view(SLOT, S_OD + j, KD, w), a["od_w_in"][0].rearrange("(k p) c -> p k c", p=P)[:, :, 256 * j:256 * j + w])]
        for j in range(2):
            fills[S_QB + j] = [(SLOT_view(SLOT, S_QB + j, 3, 384), a["mla_w_qb"][0].rearrange("(k p) c -> p k c", p=P)[:, :, 384 * j:384 * j + 384])]
        fills[S_UKV] = [(SLOT_view(SLOT, S_UKV, 2, 512), a["mla_w_uk"][0].rearrange("(k p) h n -> p k (h n)", p=P)),
                        (SLOT_view(SLOT, S_UKV, 2, 512, 1024), a["mla_w_uv"][0].rearrange("(k p) h n -> p k (h n)", p=P))]
        for j in range(4):
            fills[S_ODO + j] = [(SLOT_view(SLOT, S_ODO + j, KD, 256), a["od_w_out"][0].rearrange("(k p) c -> p k c", p=P)[:, :, 256 * j:256 * j + 256])]

        def landed(n):
            return sum(16 * len(fills[m]) for m in range(n % NSLOT, n + 1, NSLOT))

        slot_done = {}
        mark = {}

        block = ctx.enter_context(nc.Block())

        PR, QA, CKV, KRF = part(0, RT_N, NT), part(3920, 3, NT), part(4760, 2, NT), part(5320, NT)
        XM = part(5600, RT_N, NT)
        XR, XK, XV = XM[:, 0:4], XM[:, 4:8], XM[:, 8:12]
        DIF = part(9520, RT_N, NT)
        SW, AS, KK = (part(9520 + 1120 * i, 4, NT) for i in range(3))
        TW, GX = part(12880, NT), part(13160, NT)
        GG, K2, CS, RTF, ATF, KTF, BTF, KLF, BLF, BON = (part(13440 + 1120 * i, 4, NT) for i in range(10))
        YW = CS
        E1, E2, E3 = (part(1120 * i, 4, NT) for i in range(3))
        LW, G2 = part(24640, 512), part(25152, 512)
        SSH, SHO = part(25664, RP), part(27456, RP)
        SROW2 = part(25664, 6 * 512)
        SMP = part(29248, 6, 4, NB)
        PL = part(24640, 4, 9)
        WKS = resv(0, 32, WD)
        SV5, SVV = part(30272, 5, WD), part(30592, 32)
        SAS, SYS = part(30624, 32), part(30656, 32)
        NTM, TM_, TTM, XX = (part(25664 + 1024 * i, 2, 4, P) for i in range(4))
        ST = part(29760, 2, 4, WD)
        AKT, RBT, RKT = (part(1024 * i, 2, 4, P) for i in range(3))
        TA = part(3072, 512)
        ATK, BLK, KLK, VTK = (part(5600 + 512 * i, 512) for i in range(4))
        AK, TV, RE, GTM, CCM = part(9520, 512), part(10032, 512), part(10544, 4, P), part(11056, 4, 4, WD), part(12080, 4, 4, WD)
        SWO = part(3072, WH, WD)
        TS = part(9520, 32, WD)
        YR8 = part(11600, 512)
        OSQ1, OSD1 = E1, E2
        MIXR1, MIXS1 = part(28460, 4, NT), part(29580, 4, NT)
        CK = part(0, NB, NPG, 288)
        WUKT, QAN, MSQ, MSD = part(0, MH, KVL), part(2048, 3, NT), part(2888, 3, NT), part(5600, 2, NT)
        KRR, RT1, RT2 = part(6160, NT), part(6440, NT), part(6720, NT)
        Q96, K96 = part(18432, MH, NT), part(20672, MH, NT)
        VM, CT9, CNF = part(22912, 3, 512), part(24448, 3, 288), part(25312, 2, NT)
        PTS = part(25872, 3, NPR)
        SCM = part(26688, 2, 3, NPR)
        STAT = part(28320, 2, 3, 4)
        QLP, QLF, CS8, C8T = resv(0, NB, 3, 64), resv(1536, 3, 64), resv(1728, 288), resv(2016, 3, NB)
        KT3 = part(18432, 2, 3, 1024)
        SCS, P8, PC, OLT = part(24600, 1032), part(25632, NPG, 64), part(26144, 64), part(26208, 2, 64)
        STS = part(26336, 4)
        YOUT = part(12000, 3, D)
        PTAB = ctx.enter_context(nc.sbuf_tensor("page_ids", [1, NB * NPG], I32))
        srow2_dram, yrow_dram = dram("srow2_dram", [NB, 3072]), dram("yrow_dram", [NB, 512])

        od_loads = [
            (LW[0:LORA], a["rwkv_w2"][0]),
            (LW[LORA:P], a["rwkv_a2"][0]),
            (G2, a["rwkv_g2"][0]),
            (SSH[0:NB], a["state_shift"][0]),
            (PTAB[0:1, :], a["page_table"].rearrange("(o b) n -> o (b n)", o=1)),
        ]

        def odd_pe(pe, V, A, close, until, slot, used, to_fm, project, fm_sums, out_and_moe):
            pe.wait_ge(ev("ln_done"), 2)
            for j in range(10):
                slot(S_OD + j)
                for m2 in range(2):
                    project(S_OD + j, m2, 256, XT, KD, A, f"od{j}")
                used(S_OD + j, A)
            until("od6")
            for q in range(0, RT_N, 4):
                b = V.claim()
                for m in range(q, min(q + 4, RT_N)):
                    ins = pe.transpose(b[0:NB + 1, P * (m - q):P * (m - q) + P], PR[:, m, NPR - 1:NT], ident)
                close(V, ins, "sho")
            pe.wait_ge(ev("od_in"), 16 * len(od_loads))
            b = V.claim()
            for m in range(RT_N):
                ins = pe.transpose(b[:, NB * m:NB * m + NB], SSH[0:NB, P * m:P * m + P], ident[:NB, :NB])
            close(V, ins, "prev")
            pe.wait_ge(ev("lora_in"), 2)
            for m in range(4):
                b = A.claim()
                close(A, pe.matmul(b[:, 0:NT], LW[0:LORA, P * m:P * m + P], TW[0:LORA, :], start=True, stop=True), "sw")
            for m in range(4):
                b = A.claim()
                close(A, pe.matmul(b[:, 0:NT], LW[LORA:P, P * m:P * m + P], XM[LORA:P, 12, :], start=True, stop=True), "as")
            for m in range(4):
                b = A.claim()
                close(A, pe.matmul(b[:, 0:NT], G2[:, P * m:P * m + P], GX, start=True, stop=True), "gg")
            fm_sums(E1, cst("blk"), 4, False, "kk_sq", "kk_sq_in", A)
            fm_sums(E1, cst("blk"), 4, False, "bonus", "bonus_in")
            pe.wait_ge(ev("smp_cols"), 1)
            for q in range(6):
                b = V.claim()
                for m in range(4):
                    ins = pe.transpose(b[0:NB, P * m:P * m + P], SMP[:, q, m, :], ident)
                close(V, ins, "srow2")
            pe.wait_ge(ev("wkv_in"), 1)
            n_st = 0
            for tt, (c0, r) in enumerate(PT):
                for src in (ATF, BLF, KLF, XV):
                    b = V.claim()
                    for m in range(4):
                        ins = pe.transpose(b[:r, P * m:P * m + P], src[:, m, c0:c0 + r], ident)
                    close(V, ins, "wkv_tok")

                def heads(b, n):
                    return b[:, 0:4 * n].rearrange("p (h x) -> p h x", h=4)

                for par in range(2):
                    lo = 64 * par
                    for lt, rt in ((BTF, ATF), (ATF, BTF), (KTF, ATF), (BTF, RTF), (KTF, RTF)):
                        b = V.claim()
                        for hp in range(4):
                            ins = pe.matmul(heads(b, r)[:r, hp, :], lt[lo:lo + 64, hp, c0:c0 + r], rt[lo:lo + 64, hp, c0:c0 + r], start=True, stop=True)
                        close(V, ins, f"prod{par}")
                for par in range(2):
                    pe.wait_ge(ev("t_init"), 2 * tt + par + 1)
                for lev in range(4):
                    for par in range(2):
                        if lev > 0:
                            until(f"t{par}")
                        b = V.claim()
                        for hp in range(4):
                            ins = pe.matmul(heads(b, r)[:r, hp, :], NTM[:r, par, hp, 0:r], TM_[:r, par, hp, 0:r], start=True, stop=True)
                        close(V, ins, f"x{par}")
                    for par in range(2):
                        until(f"x{par}")
                        if lev < 3:
                            b = V.claim()
                            for hp in range(4):
                                ins = pe.matmul(heads(b, r)[:r, hp, :], TTM[:r, par, hp, 0:r], XX[:r, par, hp, 0:r], start=True, stop=True)
                            close(V, ins)
                        b = V.claim()
                        for hp in range(4):
                            ins = pe.matmul(heads(b, r)[:r, hp, :], XX[:r, par, hp, 0:r], TTM[:r, par, hp, 0:r], start=True, stop=True)
                        close(V, ins, f"t{par}")
                b = V.claim()
                for h in range(WH):
                    ins = pe.matmul(b[:r, WD * h:WD * h + WD], AKT[:r, h % 2, h // 2, 0:r], VTK[:r, WD * h:WD * h + WD], start=True, stop=True)
                close(V, ins, "ak")
                until("t1")
                for src, name in ((ATK, "ta"), (AK, "tv")):
                    if name == "tv":
                        until("ak")
                    b = V.claim()
                    for h in range(WH):
                        ins = pe.matmul(b[:r, WD * h:WD * h + WD], TTM[:r, h % 2, h // 2, 0:r], src[:r, WD * h:WD * h + WD], start=True, stop=True)
                    close(V, ins, name)
                until("ta")
                b = V.claim()
                for h in range(WH):
                    ins = pe.matmul(heads(b, r)[64 * (h % 2):64 * (h % 2) + 64, h // 2, :], TA[:r, WD * h:WD * h + WD], RBT[:r, h % 2, h // 2, 0:r], start=True, stop=True)
                close(V, ins, "re")
                until("tv")
                nch = max(1, r // WC)
                rc = min(r, WC)
                for c in range(nch):
                    b = V.claim()
                    k = slice(WC * c, WC * c + rc)
                    for h in range(WH):
                        o, hs = slice(64 * (h % 2), 64 * (h % 2) + 64), slice(WD * h, WD * h + WD)
                        pe.matmul(b[o, WD * (h // 2):WD * (h // 2) + WD], TA[k, hs], BLK[k, hs], start=True, stop=True)
                        q = b[o, 256 + WD * (h // 2):256 + WD * (h // 2) + WD]
                        pe.matmul(q, BLK[k, hs], TV[k, hs], start=True, stop=False)
                        ins = pe.matmul(q, KLK[k, hs], VTK[k, hs], start=False, stop=True)
                    close(V, ins, "gc")
                by = A.claim()
                until("re")
                for h in range(WH):
                    o, hs = slice(64 * (h % 2), 64 * (h % 2) + 64), slice(WD * h, WD * h + WD)
                    q = heads(by, r)[o, h // 2, :]
                    pe.matmul(q, TV[:r, hs], RBT[:r, h % 2, h // 2, 0:r], start=(h < 2), stop=False, skip_group_check=True)
                    pe.matmul(q, VTK[:r, hs], RKT[:r, h % 2, h // 2, 0:r], start=False, stop=True, skip_group_check=True)
                until("gc")
                for c in range(nch):
                    if n_st == 0:
                        pe.wait_ge(ev("state0"), 1)
                    else:
                        until("state")
                    b = V.claim()
                    for h in range(WH):
                        o = slice(64 * (h % 2), 64 * (h % 2) + 64)
                        ins = pe.matmul(b[o, WD * (h // 2):WD * (h // 2) + WD], GTM[o, c, h // 2, :], ST[o, n_st % 2, h // 2, :], start=True, stop=True)
                    close(V, ins, "state")
                    for h in range(WH):
                        o = slice(64 * (h % 2), 64 * (h % 2) + 64)
                        ins = pe.matmul(heads(by, r)[o, h // 2, WC * c:WC * c + rc], ST[o, n_st % 2, h // 2, :], RE[o, h // 2, WC * c:WC * c + rc],
                                        start=False, stop=True, skip_group_check=True)
                    n_st += 1
                close(A, ins, "yw")
            until("state")
            b = V.claim()
            for hp in range(4):
                ins = pe.transpose(b[0:WD, P * hp:P * hp + P], ST[:, n_st % 2, hp, :], ident)
            close(V, ins, "swo")
            pe.wait_ge(ev("yr8_in"), 16)
            b = V.claim()
            for m in range(4):
                ins = pe.transpose(b[:, NB * m:NB * m + NB], YR8[0:NB, P * m:P * m + P], ident[:NB, :NB])
            close(V, ins, "yw_smp")
            until("yw")
            until("yw_smp")
            fm_sums(YW, cst("blk"), 4, False, "hn_mean", None)
            fm_sums(OSQ1, cst("blk"), 4, False, "hn_var1", "hn_sq", A)

            fm_sums(MSQ, cst("ones"), 3, True, "qa_var", "qa_sq", A)
            fm_sums(MSQ, cst("ones"), 2, True, "kv_var", "kv_sq", A)
            b = V.claim()
            close(V, pe.matmul(b[:, 0:NT], cst("perm32"), KRF, start=True, stop=True), "kr_rope")
            ukv = S_UKV
            uk, uv = SLOT_view(SLOT, ukv, 2, 512), SLOT_view(SLOT, ukv, 2, 512, 1024)
            slot(S_QB)
            slot(S_QB + 1)
            slot(ukv)
            for q in range(4):
                b = V.claim()
                for i in range(2):
                    for k in range(2):
                        ins = pe.transpose(b[0:64, 256 * i + P * k:256 * i + P * k + P], uk[:, k, 64 * (2 * q + i):64 * (2 * q + i) + 64], ident)
                close(V, ins, "wukt")
            pe.wait_ge(ev("qan_ready"), 1)
            for h in range(MH):
                b = A.claim()
                w = SLOT_view(SLOT, S_QB + h // 4, 3, 384)
                for k in range(3):
                    ins = pe.matmul(b[0:96, 0:NT], w[:, k, 96 * (h % 4):96 * (h % 4) + 96], QAN[:, k, :], start=(k == 0), stop=(k == 2))
                close(A, ins, f"q{h}")
                if h == 3:
                    used(S_QB, A)
            used(S_QB + 1, A)
            for h in range(MH):
                until(f"q{h}")
                b = V.claim()
                close(V, pe.matmul(b[0:96, 0:NT], cst("perm32")[0:96, 0:96], Q96[0:96, h, :], start=True, stop=True), f"qr{h}")
            pe.wait_ge(ev("cnf_ready"), 1)
            for h in range(MH):
                b = A.claim()
                for k in range(2):
                    ins = pe.matmul(b[0:64, 0:NT], uk[:, k, 64 * h:64 * h + 64], CNF[:, k, :], start=(k == 0), stop=(k == 1))
                close(A, ins, "k96")
            for t, (c0, r) in enumerate(TT):
                b = V.claim()
                for k in range(2):
                    ins = pe.matmul(b[:r, :], CNF[:, k, c0:c0 + r], uv[:, k, :], start=(k == 0), stop=(k == 1))
                close(V, ins, "vm")
            pe.wait_ge(ev("krr_ready"), 1)
            for t, (c0, r) in enumerate(TT):
                b = V.claim()
                for k in range(2):
                    pe.transpose(b[:r, P * k:P * k + P], CNF[:, k, c0:c0 + r], ident)
                ins = pe.transpose(b[:r, 256:384], KRR[:, c0:c0 + r], ident)
                close(V, ins, "ct9")
            b = V.claim()
            for k in range(2):
                pe.transpose(b[:NB, P * k:P * k + P], CNF[:, k, NPR:NT], ident)
            close(V, pe.transpose(b[:NB, 256:384], KRR[:, NPR:NT], ident), "cs8")
            until("cs8")
            b = V.claim()
            for k in range(3):
                ins = pe.transpose(b[0:96, NB * k:NB * k + NB], CS8[0:NB, 96 * k:96 * k + 96], ident[:NB, :NB])
            close(V, ins, "c8t")
            until("qr7")
            until("wukt")
            b = V.claim()
            for k in range(3):
                for h in range(MH):
                    m = min(96, KVL - 96 * k)
                    o = b[0:m, 64 * k + h:64 * k + 64:MH]
                    ins = pe.matmul(o, WUKT[0:64, h, 96 * k:96 * k + m], Q96[0:64, h, NPR:NT], start=True, stop=True)
            close(V, ins, "qlat")

            def scores(h):
                for t, (c0, r) in enumerate(PT):
                    b = V.claim()
                    close(V, pe.matmul(b[:r, 0:c0 + r], Q96[0:96, h, c0:c0 + r], K96[0:96, h, 0:c0 + r], start=True, stop=True), "scm")

            until("k96")
            pe.wait_ge(ev("k96_rope"), 1)
            scores(0)
            for h in range(MH):
                if h < MH - 1:
                    scores(h + 1)
                pe.wait_ge(ev("p_ready"), h + 1)
                for j, (j0, rj) in enumerate(PT):
                    b = V.claim()
                    for t in range(j, 3):
                        c0, r = PT[t]
                        ins = pe.transpose(b[:rj, c0:c0 + r], SCM[:r, h % 2, t, j0:j0 + rj], ident[:r, :r])
                    close(V, ins, f"pts{h}")
                until(f"pts{h}")
                b = A.claim()
                o = 64 * (h % 2)
                for j, (j0, rj) in enumerate(PT):
                    ins = pe.matmul(b[o:o + 64, j0:NPR], VM[:rj, j, VH * h:VH * h + VH], PTS[:rj, j, j0:NPR], start=(j == 0), stop=(j == 2))
                close(A, ins, f"yd{h}")
            pe.wait_ge(ev("qlp_ready"), 1)
            pe.wait_ge(ev("cache_krope_in"), 16 * NPG * NB)
            for sm in range(NB):
                pe.wait_ge(ev(f"cache_kv_in{sm}"), 16 * NPG)
                if sm >= 2:
                    until(f"scs{sm - 2}")
                for half in range(2):
                    for k in range(3):
                        b = A.claim()
                        for i in range(4):
                            ins = pe.transpose(b[0:96, P * i:P * i + P], CK[:, sm, 4 * half + i, 96 * k:96 * k + 96], ident)
                        close(A, ins, "kt3")
                until("kt3")
                for half in range(2):
                    b = V.claim()
                    for k in range(3):
                        ins = pe.matmul(b[0:64, :], QLP[0:96, sm, k, :], KT3[0:96, sm % 2, k, 512 * half:512 * half + 512], start=(k == 0), stop=(k == 2))
                    close(V, ins, f"scs{sm}")
            b = V.claim()
            for k in range(3):
                ins = pe.matmul(b[0:64, 0:NB], QLF[0:96, k, :], C8T[0:96, k, :], start=(k == 0), stop=(k == 2))
            close(V, ins, "scur")
            pe.wait_ge(ev("ps_ready"), 1)
            b = V.claim()
            for pg in range(NPG):
                ins = pe.transpose(b[:, 64 * pg:64 * pg + 64], SCS[0:64, PAGE * pg:PAGE * pg + PAGE], ident[:64, :64])
            close(V, ins, "p8")
            b = V.claim()
            close(V, pe.transpose(b[0:NB, 0:64], SCS[0:64, PAST:PAST + NB], ident[:64, :64]), "pc")
            until("pc")
            for k in range(2):
                b = V.claim()
                pe.matmul(b[:, 0:64], CS8[0:NB, P * k:P * k + P], PC[0:NB, :], start=True, stop=False, skip_group_check=True)
                for sm in range(NB):
                    for pg in range(NPG):
                        ins = pe.matmul(b[:, 8 * sm:8 * sm + 8], CK[:, sm, pg, P * k:P * k + P], P8[:, pg, 8 * sm:8 * sm + 8],
                                        start=False, stop=(pg == NPG - 1), skip_group_check=True)
                close(V, ins, "olt")
            until("olt")
            b = V.claim()
            for h in range(MH):
                o = slice(64 * (h % 2), 64 * (h % 2) + 64)
                for k in range(2):
                    ins = pe.matmul(b[o, NB * (h // 2):NB * (h // 2) + NB], uv[:, k, VH * h:VH * h + VH], OLT[:, k, h:64:MH], start=(k == 0), stop=(k == 1))
            close(V, ins, "yd_smp")
            used(ukv, V)
            until(f"yd{MH - 1}")
            out_and_moe(1, S_ODO)
            pe.wait_ge(ev("ln_done"), 4)
            for t, (c0, r) in enumerate(TT):
                for h in range(2):
                    b = V.claim()
                    for i in range(4):
                        ins = pe.transpose(b[:r, P * i:P * i + P], XT[:, 4 * h + i, c0:c0 + r], ident)
                    close(V, ins, "y_rows")

        def odd_dve(dve, V, s, until, empty, mul, add, sub, bc, head_norm, out_and_moe):
            dve.wait_ge(ev("od_in"), 16 * len(od_loads))
            for q in range(0, RT_N, 4):
                n = min(4, RT_N - q)
                b = V.take()
                s.do(dve.tensor_copy(SHO[0:NB + 1, P * q:P * q + P * n], b[0:NB + 1, 0:P * n]), v_free)
            s.mark(sub(DIF[:, :, 1:NPR], PR[:, :, 0:NPR - 1], PR[:, :, 1:NPR]), dve_step)
            s.mark(dve.tensor_scalar(DIF[:, :, 0], PR[:, :, 0], -1.0, None, ALU.mult), dve_step)
            b = V.take()
            s.do(sub(DIF[:, :, NPR:NT], b[:, 0:RT_N * NB].rearrange("p (m b) -> p m b", m=RT_N), PR[:, :, NPR:NT]), v_free)
            dve.wait_ge(dve_step, s.n["dve_step"])
            s.do(mul(DIF, DIF, bc(vec("rwkv_mu", 0, RT_N), [P, RT_N, NT], 2)))
            s.do(add(XM, DIF, PR), ev("xm_ready"))
            v4 = lambda name, w=NT: bc(vec(name, 0, 4), [P, 4, w], 2)
            until("as")
            s.do(mul(KK, XK, v4("rwkv_k_k")))
            s.do(mul(E1, KK, KK), ev("kk_sq_in"))
            s.do(dve.tensor_scalar(E3, AS, -1.0, None, ALU.add))
            s.do(mul(E3, E3, v4("rwkv_k_a")))
            s.do(dve.scalar_tensor_tensor(K2, E3, 1.0, XK, ALU.add, ALU.mult))
            for m in range(4):
                ins = dve.tensor_tensor_scan(CS[:, m, 0:NPR], cst("scan"), SW[:, m, 0:NPR], 0.0, ALU.mult, ALU.add)
                s.do(ins, ev("cs_ready") if m == 3 else None)
            s.do(sub(ATF[:, :, 0:NPR], CS[:, :, 0:NPR], SW[:, :, 0:NPR]))
            nf = NPR // WC
            chunks = lambda v: v[:, :, 0:nf * WC].rearrange("p m (c l) -> p m c l", l=WC)
            s.do(sub(chunks(KLF), chunks(CS), chunks(CS)[:, :, :, WC - 1:WC].to_broadcast([P, 4, nf, WC])))
            s.do(sub(KLF[:, :, nf * WC:NPR], CS[:, :, nf * WC:NPR], CS[:, :, NPR - 1:NPR].to_broadcast([P, 4, NPR - nf * WC])), ev("exp_in"))
            until("kk_sq")
            s.do(dve.tensor_scalar(E2, E2, 1e-12, None, ALU.max))
            s.do(dve.reciprocal(E2, E2))
            s.do(mul(KK, KK, E2))
            s.do(mul(E1, XR, v4("rwkv_r_k")))
            s.do(mul(E1, E1, K2), ev("bonus_in"))
            s.do(mul(BTF, KK, AS))
            cols = slice(NPR, NT)
            s.mark(dve.tensor_scalar(SMP[:, 0], KK[:, :, cols], -1.0, None, ALU.mult), dve_step)
            s.mark(dve.tensor_copy(SMP[:, 2], BTF[:, :, cols]), dve_step)
            s.mark(dve.tensor_copy(SMP[:, 3], K2[:, :, cols]), dve_step)
            s.mark(dve.tensor_copy(SMP[:, 4], XR[:, :, cols]), dve_step)
            dve.wait_ge(ev("exps"), 6)
            s.do(dve.tensor_copy(SMP[:, 5], XV[:, :, cols]), ev("smp_cols"))
            for m in range(4):
                b = V.take()
                s.do(mul(BON[:, m, :], b[:, 0:NT], XV[:, m, :]), v_free)
            pc_ = slice(0, NPR)
            s.do(mul(RTF[:, :, pc_], RTF[:, :, pc_], XR[:, :, pc_]))
            s.do(dve.scalar_tensor_tensor(ATF[:, :, pc_], ATF[:, :, pc_], -1.0, KK[:, :, pc_], ALU.mult, ALU.mult))
            s.do(mul(BLF[:, :, pc_], BTF[:, :, pc_], KLF[:, :, pc_]))
            s.do(mul(KLF[:, :, pc_], K2[:, :, pc_], KLF[:, :, pc_]))
            s.do(mul(BTF[:, :, pc_], BTF[:, :, pc_], KTF[:, :, pc_]))
            s.do(mul(KTF[:, :, pc_], K2[:, :, pc_], KTF[:, :, pc_]), ev("wkv_in"))
            dve.wait_ge(ev("stores"), 16 * 8)
            for q in range(6):
                empty(SROW2[0:NB, 512 * q:512 * q + 512], 512, NB)
            dve.wait_ge(ev("srow2_out"), 16)
            s.do(dve.memset(ST[:, 0], 0.0), ev("state0"))
            n_st = 0
            for tt, (c0, r) in enumerate(PT):
                for dst in (ATK, BLK, KLK, VTK):
                    empty(dst[:r, :], 512, r)

                def heads(b, n):
                    return b[:n, 0:4 * n].rearrange("p (h x) -> p h x", h=4)

                def mk(name):
                    return bc(cst(name)[:r, 0:r], [r, 4, r], 1)

                for par in range(2):
                    m_ = lambda v: v[:r, par, :, 0:r]
                    b = V.take()
                    s.do(mul(m_(NTM), heads(b, r), mk("strictT")), v_free)
                    b = V.take()
                    s.do(mul(m_(TM_), heads(b, r), mk("m2N")), v_free)
                    for dst, name in ((AKT, "strictT"), (RBT, "inclT"), (RKT, "inclT")):
                        b = V.take()
                        s.do(mul(m_(dst), heads(b, r), mk(name)), v_free)
                    s.do(add(m_(TM_), m_(TM_), mk("ident")))
                    s.do(mul(m_(TTM), m_(NTM), mk("m2T")))
                    s.do(add(m_(TTM), m_(TTM), mk("ident")), ev("t_init"))
                for lev in range(4):
                    for par in range(2):
                        b = V.take()
                        s.do(mul(XX[:r, par, :, 0:r], heads(b, r), mk(f"off{2 << lev}")), v_free)
                    for par in range(2):
                        if lev < 3:
                            b = V.take()
                            s.do(add(TM_[:r, par, :, 0:r], TM_[:r, par, :, 0:r], heads(b, r)), v_free)
                        b = V.take()
                        s.do(add(TTM[:r, par, :, 0:r], TTM[:r, par, :, 0:r], heads(b, r)), v_free)
                empty(AK[:r, :], 512, r)
                empty(TA[:r, :], 512, r)
                empty(TV[:r, :], 512, r)
                b = V.take()
                s.do(add(RE[:, :, 0:r], RTF[:, :, c0:c0 + r], b[:, 0:4 * r].rearrange("p (h x) -> p h x", h=4)), v_free)
                nch = max(1, r // WC)
                for c in range(nch):
                    s.do(mul(GTM[:, c], bc(cst("id64"), [P, 4, WD], 1), bc(PL[:, :, 4 * tt + c], [P, 4, WD], 2)))
                    b = V.take()
                    s.do(dve.tensor_copy(CCM[:, c], b[:, 256:512].rearrange("p (h x) -> p h x", h=4)))
                    s.do(add(GTM[:, c], GTM[:, c], b[:, 0:256].rearrange("p (h x) -> p h x", h=4)), v_free)
                for c in range(nch):
                    b = V.take()
                    s.do(add(ST[:, (n_st + 1) % 2], b[:, 0:256].rearrange("p (h x) -> p h x", h=4), CCM[:, c]), v_free)
                    n_st += 1
            b = V.take()
            s.do(dve.tensor_copy(SWO[0:WD], b[0:WD, :].rearrange("p (h x) -> p h x", h=WH)), v_free)
            dve.wait_ge(ev("smp2_in"), 16 * 12)
            sh = [P, 32, WD]
            q_ = [bc(SV5[:, q, :], sh, 1) for q in range(5)]
            s.do(mul(TS, WKS, q_[0]))
            s.do(dve.tensor_reduce(SAS, TS, AX.X, ALU.add))
            s.do(mul(WKS, WKS, q_[1]))
            s.do(mul(TS, bc(SAS, sh, 2), q_[2]))
            s.do(add(WKS, WKS, TS))
            s.do(mul(TS, bc(SVV, sh, 2), q_[3]))
            s.do(add(WKS, WKS, TS), ev("wks_ready"))
            s.do(mul(TS, WKS, q_[4]))
            s.do(dve.tensor_reduce(SYS, TS, AX.X, ALU.add), ev("sys_ready"))
            b = V.take()
            s.do(dve.tensor_copy(YW[:, :, NPR:NT], b[:, 0:4 * NB].rearrange("p (m b) -> p m b", m=4)), v_free)
            until("yw")
            head_norm(YW, OSQ1, OSD1, WD, "rwkv_gn_g", "rwkv_gn_b", YW, "hn_var1")
            s.do(add(YW, YW, BON))
            s.do(mul(MIXR1, YW, GG), ev("mix_ready"))

            dve.wait_ge(ev("stores"), 16 * 10)
            s.do(mul(MSQ, QA, QA), ev("qa_sq"))
            until("qa_var")
            s.do(mul(MSQ[:, 0:2], CKV, CKV), ev("kv_sq"))
            s.do(dve.reciprocal(MSD[:, 0], MSD[:, 0]))
            for m in range(3):
                s.do(dve.scalar_tensor_tensor(QAN[:, m, :], QA[:, m, :], vec("mla_q_norm", m), MSD[:, 0], ALU.mult, ALU.mult), ev("qan_ready") if m == 2 else None)
            until("kv_var")
            s.do(dve.reciprocal(MSD[:, 1], MSD[:, 1]))
            for m in range(2):
                s.do(dve.scalar_tensor_tensor(CNF[:, m, :], CKV[:, m, :], vec("mla_kv_norm", m), MSD[:, 1], ALU.mult, ALU.mult), ev("cnf_ready") if m == 1 else None)
            b = V.take()
            s.do(mul(RT2, b[:, 0:NT], cst("sinr")), v_free)
            s.do(mul(RT1, KRF, cst("cosr")))
            s.do(add(KRR, RT1, RT2), ev("krr_ready"))
            for q in range(4):
                b = V.take()
                s.do(dve.tensor_copy(WUKT[0:64, 2 * q:2 * q + 2, :], b[0:64, :].rearrange("p (h c) -> p h c", h=2)), v_free)
            ro = slice(64, 96)
            for h in range(MH):
                b = V.take()
                s.do(mul(RT2[ro], b[ro, 0:NT], cst("sinr")[ro]))
                s.do(mul(RT1[ro], Q96[ro, h, :], cst("cosr")[ro]))
                s.do(add(Q96[ro, h, :], RT1[ro], RT2[ro]), v_free)
            s.do(dve.tensor_copy(K96[ro], bc(KRR[ro], [32, MH, NT], 1)), ev("k96_rope"))
            for t, (c0, r) in enumerate(TT):
                empty(VM[:r, t, :], 512, r)
            for t, (c0, r) in enumerate(TT):
                empty(CT9[:r, t, :], 288, r)
            dve.wait_ge(ev("stores"), 16 * 10)
            empty(CS8[0:NB, :], 288, NB)
            b = V.take()
            s.do(dve.tensor_copy(C8T[0:96], b[0:96, 0:3 * NB].rearrange("p (k b) -> p k b", k=3)), v_free)
            b = V.take()
            s.do(dve.memset(QLP[0:96], 0.0))
            s.do(dve.tensor_copy(QLF[0:96, 0:2, :], b[0:96, 0:128].rearrange("p (k f) -> p k f", k=2)))
            s.do(dve.tensor_copy(QLF[0:64, 2, :], b[0:64, 128:192]), v_free)
            s.do(dve.tensor_copy(QLF[ro, 2, :].rearrange("p (b h) -> p b h", b=NB), Q96[ro, :, NPR:NT].rearrange("p h b -> p b h")))
            for sm in range(NB):
                s.do(dve.tensor_copy(QLP[0:96, sm, :, 8 * sm:8 * sm + 8], QLF[0:96, :, 8 * sm:8 * sm + 8]), ev("qlp_ready") if sm == NB - 1 else None)

            def take_scores(h):
                for t, (c0, r) in enumerate(PT):
                    b = V.take()
                    if c0:
                        s.do(dve.tensor_scalar(SCM[:r, h % 2, t, 0:c0], b[:r, 0:c0], SCALE, None, ALU.mult))
                    s.do(dve.scalar_tensor_tensor(SCM[:r, h % 2, t, c0:c0 + r], b[:r, c0:c0 + r], SCALE, cst("causal")[:r, 0:r], ALU.mult, ALU.add), v_free)
                    s.do(dve.tensor_reduce(STAT[:r, h % 2, t, 0:1], SCM[:r, h % 2, t, 0:c0 + r], AX.X, ALU.max, negate=True), ev("s_ready"))

            take_scores(0)
            for h in range(MH):
                if h < MH - 1:
                    take_scores(h + 1)
                for t, (c0, r) in enumerate(PT):
                    dve.wait_ge(ev("p_exp"), 3 * h + t + 1)
                    st = STAT[:r, h % 2, t, :]
                    s.do(dve.reciprocal(st[:, 2:3], st[:, 1:2]))
                    p = SCM[:r, h % 2, t, 0:c0 + r]
                    s.do(dve.tensor_scalar(p, p, st[:, 2:3], None, ALU.mult), ev("p_ready") if t == 2 else None)
                for j, (j0, rj) in enumerate(PT):
                    b = V.take()
                    s.do(dve.tensor_copy(PTS[:rj, j, j0:NPR], b[:rj, j0:NPR]), v_free)
            dve.wait_ge(ev("stores"), 16 * 18)
            for sm in range(NB):
                for half in range(2):
                    b = V.take()
                    o = SCS[0:64, 512 * half:512 * half + 512]
                    s.do(dve.tensor_copy(o, b[0:64, :]) if sm == 0 else add(o, o, b[0:64, :]), v_free)
            b = V.take()
            s.do(add(SCS[0:64, PAST:PAST + NB], b[0:64, 0:NB], cst("curmask")[0:64, :]), v_free)
            s.do(dve.tensor_reduce(STS[0:64, 0:1], SCS[0:64, :], AX.X, ALU.max, negate=True))
            s.do(dve.tensor_scalar(STS[0:64, 0:1], STS[0:64, 0:1], SCALE, None, ALU.mult), ev("ss_ready"))
            dve.wait_ge(ev("ps_exp"), 1)
            s.do(dve.reciprocal(STS[0:64, 2:3], STS[0:64, 1:2]))
            s.do(dve.tensor_scalar(SCS[0:64, :], SCS[0:64, :], STS[0:64, 2:3], None, ALU.mult), ev("ps_ready"))
            b = V.take()
            s.do(dve.tensor_copy(P8, b[:, :].rearrange("p (g f) -> p g f", g=NPG)), v_free)
            b = V.take()
            s.do(dve.tensor_copy(PC[0:NB, :], b[0:NB, 0:64]), v_free)
            for k in range(2):
                b = V.take()
                s.do(dve.tensor_copy(OLT[:, k, :], b[:, 0:64]), v_free)
            b = V.take()
            s.do(dve.tensor_copy(MIXS1[:, :, NPR:NT], b[:, 0:4 * NB].rearrange("p (m b) -> p m b", m=4)))
            s.do(dve.tensor_copy(STS[:, 3:4], b[:, 0:1]), v_free)
            s.do(dve.tensor_copy(STS[:, 3:4], MIXS1[:, 0, NPR:NPR + 1]), ev("mix_ready"))
            out_and_moe(1)
            for t, (c0, r) in enumerate(TT):
                for h in range(2):
                    empty(YOUT[:r, t, 512 * h:512 * h + 512], 512, r)

        def odd_act(act, A, s, empty, std, moe):
            for m in range(RT_N):
                empty(PR[:, m, :], NT)
            for m in range(3):
                empty(QA[:, m, :], NT)
            for m in range(2):
                empty(CKV[:, m, :], NT)
            empty(KRF, NT)
            act.wait_ge(ev("xm_ready"), 1)
            act.activation(TW[0:LORA, :], XM[0:LORA, 12, :], ACT.Tanh).then_inc(ev("lora_in"), 1)
            act.activation(GX, XM[:, 13, :], ACT.Sigmoid).then_inc(ev("lora_in"), 1)
            for m in range(4):
                empty(SW[:, m, :], NT, ACT.Sigmoid, bias=vec("rwkv_w0", m))
            for m in range(4):
                empty(AS[:, m, :], NT, ACT.Sigmoid, bias=vec("rwkv_a0", m))
            for m in range(4):
                empty(GG[:, m, :], NT)
            for m in range(4):
                empty(E2[:, m, :], NT, ACT.Sqrt)
            act.wait_ge(ev("exp_in"), 1)
            act.activation(ATF[:, :, 0:NPR], ATF[:, :, 0:NPR], ACT.Exp, scale=-DECAY).then_inc(ev("exps"), 1)
            act.activation(KLF[:, :, 0:NPR], KLF[:, :, 0:NPR], ACT.Exp, scale=DECAY).then_inc(ev("exps"), 1)
            act.activation(RTF[:, :, 0:NPR], CS[:, :, 0:NPR], ACT.Exp, scale=-DECAY).then_inc(ev("exps"), 1)
            act.activation(KTF[:, :, 0:NPR], CS[:, :, 0:NPR], ACT.Exp, scale=DECAY).then_inc(ev("exps"), 1)
            act.activation(PL[:, :, 0:8], CS[:, :, WC - 1:8 * WC:WC], ACT.Exp, scale=-DECAY)
            act.activation(PL[:, :, 8], CS[:, :, NPR - 1], ACT.Exp, scale=-DECAY).then_inc(ev("exps"), 1)
            act.activation(SMP[:, 1], SW[:, :, NPR:NT], ACT.Exp, scale=-DECAY).then_inc(ev("exps"), 1)
            for tt, (c0, r) in enumerate(PT):
                b = A.take()
                act.activation(YW[:, :, c0:c0 + r], b[:, 0:4 * r].rearrange("p (h x) -> p h x", h=4), ACT.Copy).then_inc(a_free, 1)
            std(OSD1, WD, 64e-5, 4)
            empty(MSD[:, 0, :], NT, ACT.Sqrt, scale=1.0 / QL, bias=eps[1e-6])
            empty(MSD[:, 1, :], NT, ACT.Sqrt, scale=1.0 / KVL, bias=eps[1e-6])
            for h in range(MH):
                empty(Q96[0:96, h, :], NT, rows=96)
            for h in range(MH):
                empty(K96[0:64, h, :], NT, rows=64)

            def exps(h):
                for t, (c0, r) in enumerate(PT):
                    act.wait_ge(ev("s_ready"), 3 * h + t + 1)
                    p = SCM[:r, h % 2, t, 0:c0 + r]
                    act.activation(p, p, ACT.Exp, bias=STAT[:r, h % 2, t, 0:1], accum_out=STAT[:r, h % 2, t, 1:2]).then_inc(ev("p_exp"), 1)

            exps(0)
            for h in range(MH):
                if h < MH - 1:
                    exps(h + 1)
                b = A.take()
                o = 64 * (h % 2)
                act.activation(MIXS1[o:o + 64, h // 2, 0:NPR], b[o:o + 64, 0:NPR], ACT.Copy).then_inc(a_free, 1)
            act.wait_ge(ev("stores"), 16 * 18)
            for sm in range(NB):
                for half in range(2):
                    for k in range(3):
                        empty(KT3[0:96, sm % 2, k, 512 * half:512 * half + 512], 512, rows=96)
            act.wait_ge(ev("ss_ready"), 1)
            act.activation(SCS[0:64, :], SCS[0:64, :], ACT.Exp, bias=STS[0:64, 0:1], scale=SCALE, accum_out=STS[0:64, 1:2]).then_inc(ev("ps_exp"), 1)
            moe(1)

        def odd_pool(pool, s):
            pool.wait_ge(*mark["out0"])
            for dst, src in od_loads:
                pool.dma_start(dst, src).then_inc(ev("od_in"), 16)
            pool.wait_ge(ev("ln_done"), 2)
            pool.dma_start(WKS, a["state_wkv"][0].rearrange("b h (two i) j -> (b h two) i j", two=2)).then_inc(ev("smp2_in"), 16)
            pool.wait_ge(*mark["srow2"])
            pool.dma_start(srow2_dram, SROW2[0:NB, :]).then_inc(ev("srow2_out"), 16)
            pool.wait_ge(ev("srow2_out"), 16)
            for q in range(5):
                for ih in range(2):
                    pool.dma_start(SV5[ih:P:2, q, :], srow2_dram[:, 512 * q:512 * q + 512].rearrange("b (h d) -> b h d", d=WD)).then_inc(ev("smp2_in"), 16)
            pool.dma_start(SVV, srow2_dram[:, 2560:3072].rearrange("b (x i) -> b x i", i=32)).then_inc(ev("smp2_in"), 16)
            pool.wait_ge(ev("sys_ready"), 1)
            pool.dma_start(yrow_dram.rearrange("b (x i) -> b x i", i=32), SYS).then_inc(ev("yrow_out"), 16)
            pool.wait_ge(ev("yrow_out"), 16)
            pool.dma_start(YR8[0:NB, :], yrow_dram).then_inc(ev("yr8_in"), 16)
            pool.wait_ge(*mark["qlat"])
            for sm in range(NB):
                for pg in range(NPG):
                    i = NPG * sm + pg
                    page = pool.value_load(PTAB[0:1, i:i + 1], min_val=0, max_val=a["cache_krope"].shape[0] - 1)
                    pool.dma_start(CK[:, sm, pg, 256:288], a["cache_krope"][bass.ds(page, 1), 0].rearrange("o p c -> p (o c)")).then_inc(ev("cache_krope_in"), 16)

        def odd_sp(sp, store, fill, over_capacity_sp):
            for n in range(S_OD + NSLOT, S_ODO):
                fill(n)
            sp.wait_ge(*mark["sho"])
            store(outs[10][0], SHO[0:1, :])
            store(outs[11][0], SHO[1:NB + 1, :])
            sp.wait_ge(ev("wks_ready"), 1)
            store(outs[9][0].rearrange("b h (two i) j -> (b h two) i j", two=2), WKS)
            sp.wait_ge(*mark["swo"])
            store(outs[8][0, 0].rearrange("h i j -> i h j"), SWO[0:WD])
            for n in range(S_ODO, S_MOE[1] + 1):
                fill(n)
            sp.wait_ge(*mark["ct9"])
            for t, (c0, r) in enumerate(PT):
                store(outs[12][0, 0, c0:c0 + r, :], CT9[:r, t, 0:256])
                store(outs[14][0, 0, c0:c0 + r, :], CT9[:r, t, 256:288])
            sp.wait_ge(*mark["cs8"])
            store(outs[13].rearrange("b l s c -> (b l s) c"), CS8[0:NB, 0:256])
            store(outs[15].rearrange("b l s c -> (b l s) c"), CS8[0:NB, 256:288])
            sp.wait_ge(*mark["qlat"])
            for sm in range(NB):
                for pg in range(NPG):
                    i = NPG * sm + pg
                    page = sp.value_load(PTAB[0:1, i:i + 1], min_val=0, max_val=a["cache_kv"].shape[0] - 1)
                    sp.dma_start(CK[:, sm, pg, 0:256], a["cache_kv"][bass.ds(page, 1), 0].rearrange("o p c -> p (o c)")).then_inc(ev(f"cache_kv_in{sm}"), 16)
            for n in range(S_MOE[1] + 1, S_MOE[1] + 3 * NE):
                fill(n)
            over_capacity_sp(1)
            sp.wait_ge(*mark["y_rows"])
            store(outs[0][0, 0:P - NM, :], YOUT[NM:P, 0, :])
            store(outs[0][0, P - NM:2 * P - NM, :], YOUT[:, 1, :])
            store(outs[0][0, 2 * P - NM:SEQ, :], YOUT[0:NM, 2, :])
            store(outs[1].rearrange("b s d -> (b s) d"), YOUT[NM:NM + NB, 2, :])

        @block.tensor
        def _(pe):
            V, A = Ring(pe, VB, v_full, v_free), Ring(pe, AB, a_full, a_free)

            def close(ring, ins, name=None):
                ins.then_inc(ring.full, 1)
                if name:
                    mark[name] = (ring.free, ring.n)

            def until(name):
                pe.wait_ge(*mark[name])

            def slot(n):
                pe.wait_ge(w_in[n % NSLOT], landed(n))

            def used(n, ring):
                slot_done[n] = (ring.full, ring.n)

            def to_fm(src, name, r_of=TT, tiles=4):
                for m in range(tiles):
                    b = V.claim()
                    for t, (c0, r) in enumerate(r_of):
                        ins = pe.transpose(b[:, c0:c0 + r], src[:r, t, P * m:P * m + P], ident[:r, :r])
                    close(V, ins, name)

            def project(n, m2, width, src, kt, ring, name, cols=None):
                b = ring.claim()
                w = SLOT_view(SLOT, n, kt, width)
                for k in range(kt):
                    ins = pe.matmul(b[:, 0:NT], w[:, k, P * m2:P * m2 + P], src[:, k, :], start=(k == 0), stop=(k == kt - 1))
                close(ring, ins, name)

            pe.wait_ge(ev("x_in"), 16 * len(x_loads))
            to_fm(XTOK, "x_fm", tiles=KD)
            pe.wait_ge(ev("vec_in"), 16 * len(vec_loads))
            b = V.claim()
            close(V, pe.transpose(b[:, 0:NVEC], VROW[:NVEC, :], ident[:NVEC, :NVEC]), "vec_cols")
            pe.wait_ge(ev("s5_in"), 16 * len(s5_loads))
            b = V.claim()
            for j in range(2):
                for t in range(2):
                    ins = pe.transpose(b[:, P * (2 * j + t):P * (2 * j + t) + P], CN[:, j, t, :], ident)
            close(V, ins, "c_turned")
            until("x_fm")
            for j in range(8):
                if j == 2:
                    until("proj1")
                    for t, (c0, r) in enumerate(TT):
                        b = V.claim()
                        for m in range(4):
                            ins = pe.transpose(b[:r, P * m:P * m + P], UF[:, m, c0:c0 + r], ident)
                        close(V, ins, "u_tok")
                    pe.wait_ge(ev("s5_rows"), 1)
                    b = V.claim()
                    for j2 in range(4):
                        ins = pe.transpose(b[:, GP * j2:GP * j2 + GP], ROWS[0:GP, 11 + j2, :], ident[:GP, :GP])
                    close(V, ins, "s5_vecs")
                slot(S_EV + j)
                for m2 in range(2):
                    project(S_EV + j, m2, 256, XT, KD, A, f"proj{j}")
                used(S_EV + j, A)
            until("proj3")
            for m in range(4):
                b = V.claim()
                close(V, pe.matmul(b[:, 0:NT], cst("perm64"), QK[:, m, :], start=True, stop=True), f"rope{m}")
            pe.wait_ge(ev("bi_ready"), 1)
            for j in range(2):
                for g in range(0, GP, 4):
                    b = A.claim()
                    for i in range(4):
                        ins = pe.transpose(b[:, P * i:P * i + P], BI[:, j, g + i, :, :].rearrange("p t c -> p (t c)"), ident)
                    close(A, ins, "bit")
            pe.wait_ge(ev("cp_ready"), 1)
            for q in range(8):
                b = V.claim()
                for i in range(4):
                    g = 8 * (q // 2) + 2 * i + q % 2
                    lo = SP_N * (g % 2)
                    for j in range(2):
                        ins = pe.matmul(b[0:SC_N, P * i:P * i + P], BB[lo:lo + SP_N, j, g // 2, :],
                                        CP[lo:lo + SP_N, j, g // 2, 0:CL, :].rearrange("p l c -> p (l c)"),
                                        start=(j == 0), stop=(j == 1))
                close(V, ins, "kl")
            for q in range(4):
                pe.wait_ge(ev("ucq_ready"), q + 1)
                b = V.claim()
                for i in range(8):
                    ins = pe.transpose(b[:, UCOL * i:UCOL * i + UCOL], UCQ[:UCOL, q % 2, i, :, :].rearrange("p t c -> p (t c)"), ident[:UCOL, :UCOL])
                close(V, ins, f"ug{q}")
            pe.wait_ge(ev("h0_in"), 32)
            b = V.claim()
            for j in range(2):
                ins = pe.transpose(b[:, P * j:P * j + P], H0R[:, j, :], ident)
            close(V, ins, "h0")
            until("bit")
            until("ug3")
            for j in range(2):
                for h in range(2):
                    b = V.claim()
                    for i in range(8):
                        g = 8 * h + i
                        for two in range(2):
                            lo = SP_N * two
                            ins = pe.matmul(b[lo:lo + SP_N, UCOL * i:UCOL * i + UCOL], BIT[:, j, g, lo:lo + SP_N],
                                            UG[:, 2 * g + two, :], start=True, stop=True)
                    close(V, ins, "inj")
            pe.wait_ge(ev("k_ready"), 16 * CL)
            pe.wait_ge(ev("hs_ready"), 1)
            for q in range(8):
                b = A.claim()
                for i in range(4):
                    g = 8 * (q // 2) + 2 * i + q % 2
                    lo = SP_N * (g % 2)
                    o = b[0:HCOL, P * i:P * i + P]
                    pe.matmul(o, UG[:, g, 0:HCOL], KT_[:, g, :], start=True, stop=False)
                    for j in range(2):
                        ins = pe.matmul(o, HS[lo:lo + SP_N, j, g // 2, :], CP[lo:lo + SP_N, j, g // 2, 1:CL + 1, :].rearrange("p l c -> p (l c)"),
                                        start=False, stop=(j == 1))
                close(A, ins, "y_chunk")
            b = V.claim()
            for j in range(2):
                pe.transpose(b[:, P * j:P * j + P], HF[:, j].rearrange("p b g -> p (b g)"), ident)
            for j in range(2):
                ins = pe.transpose(b[0:GP, P * (2 + j):P * (3 + j)], HFP[:, j, :], ident)
            close(V, ins, "h_rows")
            pe.wait_ge(ev("ytok_in"), 48)
            to_fm(YTOK, "y_fm")
            slot(S_GLU)
            pe.wait_ge(ev("z_ready"), 1)
            for m in range(4):
                project(S_GLU, m, 512, ZF, 4, A, "glu")
            used(S_GLU, A)
            until("rope3")
            for t, (c0, r) in enumerate(TT):
                b = V.claim()
                for m in range(2):
                    ins = pe.transpose(b[:r, P * m:P * m + P], QK[:, 2 + m, c0:c0 + r], ident)
                close(V, ins, "k_tok")
            until("proj5")
            for t, (c0, r) in enumerate(TT):
                b = V.claim()
                for m in range(4):
                    ins = pe.transpose(b[:r, P * m:P * m + P], VF[:, m, c0:c0 + r], ident)
                close(V, ins, "v_tok")
            for h in range(2):
                b = V.claim()
                for m in range(4):
                    src = QK if h == 0 else VF
                    ins = pe.transpose(b[:NB, P * m:P * m + P], src[:, m, NPR:NT], ident)
                close(V, ins, "srow")
            for h in range(RH):
                lo, m = 64 * (h % 2), h // 2
                for t, (c0, r) in enumerate(PT):
                    b = V.claim()
                    close(V, pe.matmul(b[:r, 0:NPR - c0], QK[lo:lo + 64, 2 + m, c0:c0 + r], QK[lo:lo + 64, m, c0:NPR],
                                       start=True, stop=True), f"scr{h}")
            for h in range(RH):
                until(f"scr{h}")
                b = A.claim()
                for t, (c0, r) in enumerate(PT):
                    ins = pe.matmul(b[:, c0:NPR], VTOK[:r, t, P * h:P * h + P], SCR[:r, h, t, c0:NPR], start=(t == 0), stop=(t == 2))
                close(A, ins, "o_fm")
            pe.wait_ge(ev("kdec_ready"), 1)
            b = V.claim()
            for h in range(RH):
                for t, (c0, r) in enumerate(PT):
                    ins = pe.matmul(b[0:RDK, RDV * h:RDV * h + RDV], KDT[:r, t, RDK * h:RDK * h + RDK], VTOK[:r, t, RDV * h:RDV * h + RDV],
                                    start=(t == 0), stop=(t == 2))
            close(V, ins, "ret_state")
            pe.wait_ge(ev("parto_ready"), 1)
            b = V.claim()
            close(V, pe.matmul(b[:, 0:RH * NB], PARTO, cst("selbh"), start=True, stop=True), "o_smp")

            def fm_sums(src, kmat, tiles, together, name, ready, ring=V):
                if ready:
                    pe.wait_ge(ev(ready), fm_sums.n.setdefault(ready, 0) + 1)
                    fm_sums.n[ready] += 1
                for m in range(tiles):
                    if m == 0 or not together:
                        b = ring.claim()
                    ins = pe.matmul(b[:, 0:NT], kmat, src[:, m, :], start=(m == 0 or not together), stop=(m == tiles - 1 or not together))
                    if m == tiles - 1 or not together:
                        close(ring, ins, name)
            fm_sums.n = {}

            until("o_fm")
            until("o_smp")
            fm_sums(OT, cst("ones"), 4, False, "hn_mean", None)
            fm_sums(OSQ, cst("ones"), 4, False, "hn_var", "hn_sq", A)

            def over_capacity_pe(l):
                pe.wait_ge(ev("over_known"), l + 1)
                over = pe.value_load(OVER[0:1, l:l + 1], min_val=0, max_val=1)
                with pe.If(over > 0):
                    pe.wait_ge(ev(f"x_comb{l}"), 1)
                    for t, (c0, r) in enumerate(TT):
                        ins = pe.transpose(banks[7][0:NE, c0:c0 + r], XC[:r, t, :], ident[:r, :r])
                    ins.then_inc(ev(f"x_full{l}"), 1)
                    pe.wait_ge(ev(f"x_comb{l}"), 2)
                    with pe.Fori(0, NE) as e:
                        pe.wait_ge(ev(f"x_w{l}"), e * 48 + 48)
                        pe.wait_ge(ev(f"x_row{l}"), e + 1)
                        for f in range(2):
                            for bank, j in ((4, 0), (0, 1)):
                                w = XW[:, j, :].rearrange("p (k c) -> p k c", k=KD)
                                for k in range(KD):
                                    pe.matmul(banks[bank + f][:, 0:NT], w[:, k, P * f:P * f + P], XT[:, k, :], start=(k == 0), stop=(k == KD - 1))
                        pe.matmul(banks[6][:, 0:NT], cst("ones")[0:NE, :], XROW[0:NE, :], start=True, stop=True).then_inc(ev(f"x_full{l}"), 1)
                        pe.wait_ge(ev(f"x_h{l}"), e * 2 + 2)
                        w = XW[:, 2, :].rearrange("p (k c) -> p k c", k=2)
                        for m in range(KD):
                            for f in range(2):
                                ins = pe.matmul(banks[m][:, 0:NT], w[:, f, P * m:P * m + P], XHB[:, f, :], start=(f == 0), stop=(f == 1))
                        ins.then_inc(ev(f"x_sums{l}"), 1)
                    pe.wait_ge(ev(f"x_dve{l}"), 2 * NE + 2)

            def out_and_moe(l, s_out):
                mixr, mixs = ((MIXR, MIXS), (MIXR1, MIXS1))[l]
                pe.wait_ge(ev("mix_ready"), 2 * (l + 1))
                for j in range(4):
                    slot(s_out + j)
                    w = SLOT_view(SLOT, s_out + j, KD, 256)
                    for m2 in range(2):
                        b = V.claim()
                        for k in range(KD):
                            src = mixr[:, k, :] if k < 4 else mixs[:, k - 4, :]
                            ins = pe.matmul(b[:, 0:NT], w[:, k, P * m2:P * m2 + P], src, start=(k == 0), stop=(k == KD - 1))
                        close(V, ins, f"out{l}")
                    used(s_out + j, V)
                until(f"out{l}")
                fm_sums(RES, cst("ones"), KD, True, "ln_mean", None)
                fm_sums(LSQ, cst("ones"), KD, True, "ln_var", "ln_sq", A)
                pe.wait_ge(ev("router_in"), 16 * len(router_loads))
                pe.wait_ge(ev("ln_done"), 2 * l + 1)
                for t, (c0, r) in enumerate(TT):
                    b = V.claim()
                    for k in range(KD):
                        ins = pe.matmul(b[:r, 0:20], XT[:, k, c0:c0 + r], RW[:, l, k, :], start=(k == 0), stop=(k == KD - 1))
                    close(V, ins, "logits")
                for t, (c0, r) in enumerate(TT):
                    for h in range(2):
                        b = A.claim()
                        for i in range(4):
                            ins = pe.transpose(b[:r, P * i:P * i + P], XT[:, 4 * h + i, c0:c0 + r], ident)
                        close(A, ins, f"x_tok{l}")
                pe.wait_ge(ev("group_ready"), l + 1)
                b = V.claim()
                one = lambda t: RT[:TT[t][1], 0, t, 0:NG]
                for t, (c0, r) in enumerate(TT):
                    for u in range(t):
                        pe.matmul(b[:, NG * t:NG * t + NG], cst("ones"), one(u), start=(u == 0), stop=False)
                    pe.matmul(b[:, NG * t:NG * t + NG], cst("before")[:r, :], one(t), start=(t == 0), stop=True)
                for t, (c0, r) in enumerate(TT):
                    ins = pe.matmul(b[:, 12:16], cst("ones")[:r, :], one(t), start=(t == 0), stop=(t == 2))
                close(V, ins, "places")
                pe.wait_ge(ev("dispatch_ready"), l + 1)
                until(f"x_tok{l}")

                def pack(g):
                    for kh in range(4):
                        b = V.claim()
                        for k2 in range(2):
                            k = 2 * kh + k2
                            for t, (c0, r) in enumerate(TT):
                                sel = DSP[:r, t, g, :] if isinstance(g, int) else DSP[:r, t, bass.ds(g, 1), :].rearrange("p a c -> p (a c)")
                                ins = pe.matmul(b[:, CAP * k2:CAP * k2 + CAP], XTM[:r, t, P * k:P * k + P], sel, start=(t == 0), stop=(t == 2))
                        close(V, ins)

                pack(0)
                for g in range(NG):
                    b = A.claim()
                    for t, (c0, r) in enumerate(TT):
                        ins = pe.transpose(b[:, c0:c0 + r], DSP[:r, t, g, :], ident[:r, :r])
                    close(A, ins, f"dspt{l}")
                pe.wait_ge(ev("comb_ready"), l + 1)
                b = V.claim()
                for t, (c0, r) in enumerate(TT):
                    ins = pe.matmul(b[0:EG, :], RT[:r, 4, t, 0:EG], DSP[:r, t, :, :].rearrange("p g c -> p (g c)"), start=(t == 0), stop=(t == 2))
                close(V, ins, "wgt")
                until("wgt")
                for e in range(EG):
                    b = A.claim()
                    close(A, pe.matmul(b[:, :], ident[0:EG, e:e + 1].to_broadcast([EG, P]), WGT[0:EG, :, :].rearrange("p g c -> p (g c)"), start=True, stop=True), f"gates{l}")
                s0 = S_MOE[l]
                va, aa = V.n, A.n
                mark[f"moe{l}"] = (va, aa)
                for e in range(NE):
                    g, j = e // EG, e % EG
                    slot_done[s0 + 3 * e] = (a_full, aa + e + 1)
                    slot_done[s0 + 3 * e + 1] = (v_full, va + V_GROUP * g + V_UP[j])
                    slot_done[s0 + 3 * e + 2] = (v_full, va + V_GROUP * g + (V_DOWN[j] if e < NE - 1 else V_GROUP - 4))

                def wait_fill(e, what, i):
                    n = s0 + 3 * e + what
                    pe.wait_ge(w_in[n % NSLOT], landed(n) + 16 * (3 * EG // NSLOT) * i)

                def gate_up(e, i):
                    wait_fill(e, 0, i)
                    wait_fill(e, 1, i)
                    n = s0 + 3 * e
                    for ring, w in ((A, SLOT_view(SLOT, n, KD, DE)), (V, SLOT_view(SLOT, n + 1, KD, DE))):
                        b = ring.claim()
                        for f in range(2):
                            for k in range(KD):
                                ins = pe.matmul(b[:, CAP * f:CAP * f + CAP], w[:, k, P * f:P * f + P], XG[:, k, :], start=(k == 0), stop=(k == KD - 1))
                        close(ring, ins)

                def down(e, i, h0):
                    wait_fill(e, 2, i)
                    pe.wait_ge(ev("h_ready"), h0 + e + 1)
                    w = SLOT_view(SLOT, s0 + 3 * e + 2, 2, D)
                    for h in range(2):
                        b = V.claim()
                        for f in range(2):
                            ins = pe.matmul(b[:, :], HB[:, e % 2, f, :], w[:, f, 512 * h:512 * h + 512], start=(f == 0), stop=(f == 1))
                        close(V, ins)

                def group(i, last):
                    h0 = NE * l + EG * i
                    pe.wait_ge(v_free, V.n - 2)
                    gate_up(0, i)
                    gate_up(1, i)
                    down(0, i, h0)
                    gate_up(2, i)
                    down(1, i, h0)
                    gate_up(3, i)
                    down(2, i, h0)
                    if not last:
                        pack(i + 1)
                    down(3, i, h0)

                with pe.Fori(0, NG - 1) as i:
                    vn, an = V.n, A.n
                    V.n, A.n = va + i * V_GROUP, aa + i * EG
                    group(i, False)
                V.n, A.n = va + V_GROUP * (NG - 1), aa + EG * (NG - 1)
                group(NG - 1, True)
                assert V.n == va + V_GROUP * NG - 4 and A.n == aa + NE
                pe.wait_ge(v_free, V.n)
                for m in range(KD):
                    b = V.claim()
                    for g in range(NG):
                        ins = pe.matmul(b[:, 0:NT], YG[:, g, P * m:P * m + P], DSPT[:, g, :], start=(g == 0), stop=(g == NG - 1))
                    close(V, ins, f"moe_out{l}")
                until(f"moe_out{l}")
                over_capacity_pe(l)
                fm_sums(RES, cst("ones"), KD, True, "ln_mean", None)
                fm_sums(LSQ, cst("ones"), KD, True, "ln_var", "ln_sq", A)

            out_and_moe(0, S_EVO)
            odd_pe(pe, V, A, close, until, slot, used, to_fm, project, fm_sums, out_and_moe)

        @block.vector
        def _(dve):
            V = Ring(dve, VB, v_full, v_free)
            s = Steps(dve, dve_step)

            def until(name):
                dve.wait_ge(*mark[name])

            def empty(dst, width=None, rows=P):
                b = V.take()
                src = b[:rows, 0:width or int(np.prod(dst.shape[1:]))]
                s.do(dve.tensor_copy(dst, src if len(dst.shape) == 2 else src.rearrange("p (a b) -> p a b", a=dst.shape[1])), v_free)

            def mul(o, x, y):
                return dve.tensor_tensor(o, x, y, ALU.mult)

            def add(o, x, y):
                return dve.tensor_tensor(o, x, y, ALU.add)

            def sub(o, x, y):
                return dve.tensor_tensor(o, x, y, ALU.subtract)

            def bc(v, shape, at):
                return v.unsqueeze(at).to_broadcast(shape)

            for k in range(KD):
                empty(XT[:, k, :])
            empty(VC[:, 0:NVEC])
            b = V.take()
            s.do(dve.tensor_copy(CTT.rearrange("p j g c -> p (j g c)"), b[:, 0:512]), v_free)

            dve.wait_ge(ev("s5_in"), 16 * len(s5_loads))
            row = [ROWS[0:GP, i, :] for i in range(15)]
            are, aim, _, t0, t1, t2, t3, sn, cs, mag, t4, abr, abi, fr, fi = row
            dve.wait_ge(ev("dt_ready"), 1)
            dt = bc(row[2][:, 4:6], [GP, 2, SP_N], 2)
            v2 = lambda r: r.rearrange("p (a b) -> p a b", a=2)
            s.do(mul(v2(t0), v2(are), dt), ev("mag_arg"))
            s.do(mul(v2(t1), v2(aim), dt))
            MAGIC = 12582912.0
            s.do(dve.tensor_scalar(t2, t1, 1.0 / (2 * math.pi), None, ALU.mult))
            s.do(dve.tensor_scalar(t2, t2, MAGIC, None, ALU.add))
            s.do(dve.tensor_scalar(t2, t2, -MAGIC, None, ALU.add))
            c1, c2 = 6.28125, 0.0019350051879882812
            for c in (c1, c2, 2 * math.pi - c1 - c2):
                s.do(dve.scalar_tensor_tensor(t1, t2, -c, t1, ALU.mult, ALU.add))
            PI = 3.1415925
            s.do(dve.tensor_scalar(t2, t1, math.pi / 2, None, ALU.add))
            s.do(dve.tensor_scalar(t3, t2, PI, -2 * math.pi, ALU.is_gt, ALU.mult))
            s.do(add(t2, t2, t3))
            s.do(dve.tensor_scalar(t2, t2, PI, -PI, ALU.min, ALU.max))
            s.do(dve.tensor_scalar(t1, t1, PI, -PI, ALU.min, ALU.max), ev("sin_arg"))
            dve.wait_ge(ev("sin_ready"), 3)
            s.do(mul(abr, mag, cs))
            s.do(mul(abi, mag, sn))
            s.do(mul(t0, are, are))
            s.do(mul(t1, aim, aim))
            s.do(add(t0, t0, t1))
            s.do(dve.reciprocal(t4, t0))
            s.do(dve.tensor_scalar(t3, abr, -1.0, None, ALU.add))
            s.do(mul(t0, t3, are))
            s.do(mul(t1, abi, aim))
            s.do(add(t0, t0, t1))
            s.do(mul(fr, t0, t4))
            s.do(mul(t0, abi, are))
            s.do(mul(t1, t3, aim))
            s.do(sub(t0, t0, t1))
            s.do(mul(fi, t0, t4), ev("s5_rows"))
            for t, (c0, r) in enumerate(TT):
                empty(UTOK[:r, t, :], 512, r)
            b = V.take()
            s.do(dve.tensor_copy(SV.rearrange("p j g -> p (j g)"), b[:, 0:4 * GP]), v_free)
            q1, q2 = TD[:, 0].rearrange("p g l c -> p (g l c)"), TD[:, 1].rearrange("p g l c -> p (g l c)")
            s.do(dve.memset(PW[:, 0, 0, :], 1.0))
            s.do(dve.memset(PW[:, 1, 0, :], 0.0))
            s.do(dve.tensor_copy(PW[:, :, 1, :], SV[:, 0:2, :]))

            def cmul(ore, oim, xr, xi, yr, yi, last=None, q1=q1, q2=q2):
                n, sh = int(np.prod(xr.shape[1:])), xr.shape
                def shaped(q):
                    q = q[:, 0:n]
                    if len(sh) == 3:
                        return q.rearrange("p (a b) -> p a b", a=sh[1])
                    return q.rearrange("p (a b c) -> p a b c", a=sh[1], b=sh[2])
                w1, w2 = shaped(q1), shaped(q2)
                s.do(mul(w1, xr, yr))
                s.do(mul(w2, xi, yi))
                s.do(sub(ore, w1, w2))
                s.do(mul(w1, xr, yi))
                s.do(mul(w2, xi, yr))
                s.do(add(oim, w1, w2), last)

            for lo, n in ((1, 1), (1, 2), (1, 4)):
                step = [bc(PW[:, j, n, :], [P, n, GP], 1) for j in range(2)]
                cmul(PW[:, 0, n + 1:2 * n + 1, :], PW[:, 1, n + 1:2 * n + 1, :], PW[:, 0, 1:n + 1, :], PW[:, 1, 1:n + 1, :], *step)
            fb = [bc(SV[:, 2 + j, :], [P, GP, SC_N], 2) for j in range(2)]
            cmul(BB[:, 0], BB[:, 1], BRAW[:, 0], BRAW[:, 1], *fb, ev("bb_ready"))
            sh = [P, GP, CL + 1, SC_N]
            cc = [bc(CTT[:, j], sh, 2) for j in range(2)]
            pw = [bc(PW[:, j].rearrange("p l g -> p g l"), sh, 3) for j in range(2)]
            w1, w2 = TD[:, 0], TD[:, 1]
            s.do(mul(w1, cc[0], pw[0]))
            s.do(mul(w2, cc[1], pw[1]))
            s.do(sub(CP[:, 0], w1, w2))
            s.do(mul(w1, cc[0], pw[1]))
            s.do(mul(w2, cc[1], pw[0]))
            s.do(add(w1, w1, w2))
            s.do(dve.tensor_scalar(CP[:, 1], w1, -1.0, None, ALU.mult), ev("cp_ready"))
            rt1, rt2 = q1[:, 0:NT], q2[:, 0:NT]
            for m in range(4):
                scale = RDK ** -0.5 if m < 2 else 1.0
                b = V.take()
                s.do(dve.scalar_tensor_tensor(rt2, b[:, 0:NT], scale, cst("sind"), ALU.mult, ALU.mult))
                s.do(dve.scalar_tensor_tensor(rt1, QK[:, m, :], scale, cst("cosd"), ALU.mult, ALU.mult))
                s.do(add(QK[:, m, :], rt1, rt2), v_free)
            dve.wait_ge(ev("u_out"), 48)
            s.do(dve.memset(KT_, 0.0), ev("k_zero"))
            for q in range(8):
                b = V.take()
                g0 = 8 * (q // 2) + q % 2
                s.do(dve.tensor_copy(KL[0:SC_N, g0:g0 + 7:2, :], b[0:SC_N, :].rearrange("p (g f) -> p g f", g=4)), v_free)
            for q in range(4):
                b = V.take()
                s.do(dve.tensor_copy(UG[:, 8 * q:8 * q + 8, :], b[:, 0:8 * UCOL].rearrange("p (g f) -> p g f", g=8)), v_free)
            b = V.take()
            s.do(dve.tensor_copy(HS[:, :, :, NCH:HCOL], b[:, 0:256].rearrange("p (j b g) -> p j g b", j=2, g=GP)), v_free)
            for j in range(2):
                for h in range(2):
                    b = V.take()
                    s.do(dve.tensor_copy(INJ[:, j, 8 * h:8 * h + 8, :], b[:, 0:8 * UCOL].rearrange("p (g f) -> p g f", g=8)), v_free)
            s.do(dve.memset(HS[:, :, :, 0], 0.0))
            ar = bc(PW[:, 0, CL, :], [P, 2, GP], 1)
            ai = bc(PW[:, 1, CL, :], [P, 2, GP], 1)
            q1, q2 = part(M_BB + 512, 256), part(M_BB + 768, 256)
            w1, w2 = q1[:, 0:2 * GP].rearrange("p (j g) -> p j g", j=2), q2[:, 0:2 * GP].rearrange("p (j g) -> p j g", j=2)
            for c in range(NCH):
                h, nxt = HS[:, :, :, c], (HS[:, :, :, c + 1] if c < NCH - 1 else HFP[:, :, :])
                s.mark(mul(w1, h, ar), dve_step)
                s.do(mul(w2, h, ai))
                s.do(add(w1, w1, INJ[:, :, :, c]))
                s.mark(sub(nxt[:, 0], w1[:, 0], w2[:, 1]), dve_step)
                s.do(add(nxt[:, 1], w1[:, 1], w2[:, 0]))
            h0 = [HS[:, j, :, NCH:HCOL].rearrange("p g b -> p b g") for j in range(2)]
            ab = [bc(SV[:, j, :], [P, NB, GP], 1) for j in range(2)]
            cmul(HF[:, 0], HF[:, 1], h0[0], h0[1], *ab, None, q1, q2)
            s.do(add(HF[:, :, :, :], HF[:, :, :, :], INJ[:, :, :, HCOL:UCOL].rearrange("p j g b -> p j b g")), ev("hs_ready"))
            b = V.take()
            s.do(dve.tensor_copy(HROW[:, 0:2, :], b[:, 0:256].rearrange("p (j f) -> p j f", j=2)))
            s.do(dve.tensor_copy(HROW[0:GP, 2:4, :], b[0:GP, 256:512].rearrange("p (j f) -> p j f", j=2)), v_free)
            for m in range(4):
                b = V.take()
                s.do(dve.scalar_tensor_tensor(YF[:, m, :], UF[:, m, :], vec("s5_d", m), b[:, 0:NT], ALU.mult, ALU.add), v_free)
            until("glu")
            s.do(mul(MIXS, ZF, YF), ev("mix_ready"))
            for t, (c0, r) in enumerate(TT):
                empty(KTOK[:r, t, :], 256, r)
            for t, (c0, r) in enumerate(TT):
                empty(VTOK[:r, t, :], 512, r)
            for h in range(2):
                empty(SROW[:NB, 512 * h:512 * h + 512], 512, NB)
            kd = cst("kdec").rearrange("p (t h) -> p t h", t=3)
            for t, (c0, r) in enumerate(PT):
                ins = mul(KDT[:r, t, :].rearrange("p (h d) -> p h d", h=RH), KTOK[:r, t, :].rearrange("p (h d) -> p h d", h=RH),
                          bc(kd[:r, t, :], [r, RH, RDK], 2))
                s.do(ins, ev("kdec_ready") if t == 2 else None)
            msk = cst("retmask").rearrange("p (h x) -> p h x", h=RH)
            for h in range(RH):
                for t, (c0, r) in enumerate(PT):
                    b = V.take()
                    s.do(mul(SCR[:r, h, t, c0:NPR], b[:r, 0:NPR - c0], msk[:r, h, 0:NPR - c0]), v_free)
            dve.wait_ge(ev("smp_in"), 16 * 7)
            s.do(mul(TOUT, bc(KS, [P, 16, RDV], 2), bc(VS, [P, 16, RDV], 1)))
            s.do(dve.scalar_tensor_tensor(RETS, RETS, cst("gam"), TOUT, ALU.mult, ALU.add), ev("rets_ready"))
            s.do(mul(TOUT, RETS, bc(QS, [P, 16, RDV], 2)))
            s.do(dve.tensor_reduce(PARTO, TOUT.rearrange("p d v -> p v d"), AX.X, ALU.add), ev("parto_ready"))
            b = V.take()
            s.do(dve.tensor_copy(RSTO[0:RDK], b[0:RDK, :].rearrange("p (h v) -> p h v", h=RH)), v_free)
            b = V.take()
            s.do(dve.tensor_copy(OT[:, :, NPR:NT], b[:, 0:RH * NB].rearrange("p (h b) -> p h b", h=RH)), v_free)

            def head_norm(x, sq, sd, n, g, bias, out, last):
                for m in range(4):
                    b = V.take()
                    s.do(dve.scalar_tensor_tensor(x[:, m, :], b[:, 0:NT], -1.0 / n, x[:, m, :], ALU.mult, ALU.add), v_free)
                s.do(mul(sq, x, x), ev("hn_sq"))
                until(last)
                s.do(dve.reciprocal(sd, sd))
                s.do(mul(x, x, sd))
                for m in range(4):
                    s.do(dve.tensor_scalar(out[:, m, :], x[:, m, :], vec(g, m), vec(bias, m), ALU.mult, ALU.add))

            until("o_fm")
            head_norm(OT, OSQ, OSD, RDV, "ret_gn_g", "ret_gn_b", OT, "hn_var")
            until("proj7")
            s.do(mul(MIXR, OT, GATE), ev("mix_ready"))

            def layer_norm(g, bias, l, tag):
                b = V.take()
                s.do(dve.scalar_tensor_tensor(RES[:, :, :], bc(b[:, 0:NT], [P, KD, NT], 1), -1.0 / D, RES[:, :, :], ALU.mult, ALU.add), v_free)
                s.do(mul(LSQ, RES[:, :, :], RES[:, :, :]), ev("ln_sq"))
                dve.wait_ge(ev("lsd_ready"), layer_norm.n + 1)
                layer_norm.n += 1
                s.do(dve.reciprocal(LSD, LSD))
                s.do(mul(RES[:, :, :], RES[:, :, :], bc(LSD, [P, KD, NT], 1)))
                for m in range(KD):
                    ins = dve.tensor_scalar(XT[:, m, :], RES[:, m, :], vec(g, KD * l + m), vec(bias, KD * l + m), ALU.mult, ALU.add)
                    s.do(ins, ev("ln_done") if m == KD - 1 else None)
            layer_norm.n = 0

            def out_and_moe(l):
                for m in range(KD):
                    b = V.take()
                    s.do(dve.scalar_tensor_tensor(RES[:, m, :], XT[:, m, :], ALPHA, b[:, 0:NT], ALU.mult, ALU.add), v_free)
                layer_norm("ln1_g", "ln1_b", l, f"ln1_{l}")
                s.do(dve.tensor_scalar(RES[:, :, :], XT[:, :, :], ALPHA, None, ALU.mult))
                s.do(dve.memset(LG, 0.0))
                dve.wait_ge(ev("router_in"), 16 * len(router_loads))
                for t, (c0, r) in enumerate(TT):
                    b = V.take()
                    s.do(add(LG[:r, t, :], b[:r, 0:20], RB[:r, l, :]), v_free)
                R = [RT[:, i, :, 0:4] for i in range(10)]
                r1 = [RT[:, i, :, 8:9] for i in range(10)]
                rank = bc(cst("rank"), [P, 3, 4], 1)
                b4 = lambda v: v.to_broadcast([P, 3, 4])

                def pack_taken():
                    for kh in range(4):
                        b = V.take()
                        s.do(dve.tensor_copy(XG[:, 2 * kh:2 * kh + 2, :], b[:, 0:2 * CAP].rearrange("p (k c) -> p k c", k=2)), v_free)

                def first_max(x, onehot, mx, tmp, tmp1, sem=None):
                    s.do(dve.tensor_reduce(mx, x, AX.X, ALU.max))
                    s.do(dve.tensor_tensor(tmp, x, b4(mx), ALU.is_equal))
                    s.do(mul(tmp, tmp, rank))
                    s.do(dve.tensor_reduce(tmp1, tmp, AX.X, ALU.max))
                    s.do(dve.tensor_tensor(onehot, tmp, b4(tmp1), ALU.is_equal), sem)

                lc = LG[:, :, 0:4]
                first_max(lc, R[0], r1[0], R[1], r1[1], ev("group_ready"))
                s.do(sub(R[2], lc, b4(r1[0])), ev("lc_shift"))
                dve.wait_ge(ev("lc_exp"), 2 * l + 1)
                s.do(dve.tensor_reduce(r1[2], R[2], AX.X, ALU.add))
                s.do(dve.reciprocal(r1[2], r1[2]))
                b = V.take()
                s.do(mul(POS, R[0], b[:, 0:12].rearrange("p (t g) -> p t g", t=3)))
                s.do(dve.tensor_copy(CNT, b[:, 12:16]), v_free)
                s.do(dve.tensor_reduce(PLACE, POS, AX.X, ALU.add))
                s.do(dve.tensor_reduce(CNT[:, 0:1], CNT, AX.X, ALU.max))
                s.do(dve.tensor_scalar(OVER[:, l:l + 1], CNT[:, 0:1], CAP + 0.5, None, ALU.is_gt), ev("over_known"))
                for g in range(NG):
                    for t in range(3):
                        ins = dve.tensor_scalar(DSP[:, t, g, :], cst("iota"), PLACE[:, t:t + 1], R[0][:, t, g:g + 1], ALU.is_equal, ALU.mult)
                s.do(ins, ev("dispatch_ready"))
                pack_taken()
                w16 = RT[:, 9, :, :]
                g4 = lambda v: v.rearrange("p t (g e) -> p t g e", g=4)
                s.do(mul(g4(w16), g4(LG[:, :, 4:20]), bc(R[0], [P, 3, 4, 4], 3)))
                s.do(dve.tensor_reduce(R[3], w16.rearrange("p t (g e) -> p t e g", g=4), AX.X, ALU.add))
                first_max(R[3], R[4], r1[3], R[1], r1[1])
                s.do(dve.scalar_tensor_tensor(R[5], R[4], -BIG, R[3], ALU.mult, ALU.add))
                first_max(R[5], R[6], r1[4], R[1], r1[1])
                s.do(sub(r1[5], r1[4], r1[3]), ev("lf_diff"))
                dve.wait_ge(ev("lc_exp"), 2 * l + 2)
                s.do(dve.tensor_scalar(r1[6], r1[5], 1.0, None, ALU.add))
                s.do(dve.reciprocal(r1[6], r1[6]))
                s.do(mul(r1[6], r1[6], r1[2]))
                s.do(mul(r1[7], r1[6], r1[5]))
                s.do(mul(R[4], R[4], b4(r1[6])))
                s.do(mul(R[6], R[6], b4(r1[7])))
                s.do(add(R[4], R[4], R[6]), ev("comb_ready"))
                b = V.take()
                s.do(dve.tensor_copy(WGT[0:EG, :, :], b[0:EG, :].rearrange("p (g c) -> p g c", g=NG)), v_free)
                va, aa = mark[f"moe{l}"]
                assert V.n == va
                until(f"gates{l}")

                def at(v, g):
                    return v[:, g, :] if isinstance(g, int) else v[:, bass.ds(g, 1), :].rearrange("p a c -> p (a c)")

                def gated(e, i):
                    b = V.take()
                    dve.wait_ge(a_free, aa + e + 1 + EG * i)
                    s.do(mul(TM[:, e % 2], b[:, 0:2 * CAP].rearrange("p (f c) -> p f c", f=2), SIL[:, e % 2, :, :]), v_free)
                    s.mark(mul(HB[:, e % 2, :, :], TM[:, e % 2], bc(at(CB[:, e], i), [P, 2, CAP], 1)), ev("h_ready"))

                def down_taken(e, i):
                    for h in range(2):
                        b = V.take()
                        y = at(YG, i)[:, 512 * h:512 * h + 512]
                        s.do(dve.tensor_copy(y, b[:, :]) if e == 0 else add(y, y, b[:, :]), v_free)

                def group(i, last):
                    gated(0, i)
                    gated(1, i)
                    down_taken(0, i)
                    gated(2, i)
                    down_taken(1, i)
                    gated(3, i)
                    down_taken(2, i)
                    if not last:
                        pack_taken()
                    down_taken(3, i)

                free0, h0 = s.n["v_free"], s.n.get("h_ready", 0)
                with dve.Fori(0, NG - 1) as i:
                    V.n = va + i * V_GROUP
                    s.n["v_free"] = free0 + i * V_GROUP
                    group(i, False)
                V.n, s.n["v_free"] = va + V_GROUP * (NG - 1), free0 + V_GROUP * (NG - 1)
                group(NG - 1, True)
                s.n["h_ready"] = h0 + NE
                for m in range(KD):
                    b = V.take()
                    s.do(add(RES[:, m, :], RES[:, m, :], b[:, 0:NT]), v_free)
                over = dve.value_load(OVER[0:1, l:l + 1], min_val=0, max_val=1)
                with dve.If(over > 0):
                    mine = ev(f"x_dve{l}")
                    t34 = [P, 3, 4]
                    dve.tensor_scalar(PLACE, PLACE, CAP - 0.5, None, ALU.is_gt).then_inc(mine, 1)
                    dve.wait_ge(mine, 1)
                    dve.tensor_tensor(R[4], R[4], bc(PLACE, t34, 2), ALU.mult).then_inc(mine, 1)
                    dve.wait_ge(mine, 2)
                    mul(g4(XC), bc(R[0], [P, 3, 4, 4], 3), bc(R[4], [P, 3, 4, 4], 2)).then_inc(ev(f"x_comb{l}"), 1)
                    dve.wait_ge(ev(f"x_full{l}"), 1)
                    dve.tensor_copy(XCT[0:NE, :], banks[7][0:NE, 0:NT]).then_inc(ev(f"x_comb{l}"), 1)
                    dve.wait_ge(ev(f"x_comb{l}"), 2)
                    with dve.Fori(0, NE) as e:
                        mul(XROW[0:NE, :], XCT[0:NE, :], ident[0:NE, bass.ds(e, 1)].to_broadcast([NE, NT])).then_inc(ev(f"x_row{l}"), 1)
                        dve.wait_ge(ev(f"x_sil{l}"), e + 1)
                        for f in range(2):
                            ins = mul(XSIL[:, f, :], banks[f][:, 0:NT], XSIL[:, f, :])
                        ins.then_inc(mine, 1)
                        dve.wait_ge(mine, e * 2 + 3)
                        for f in range(2):
                            mul(XHB[:, f, :], banks[6][:, 0:NT], XSIL[:, f, :]).then_inc(ev(f"x_h{l}"), 1)
                        dve.wait_ge(ev(f"x_sums{l}"), e + 1)
                        for m in range(KD):
                            ins = add(RES[:, m, :], RES[:, m, :], banks[m][:, 0:NT])
                        ins.then_inc(mine, 1)
                        dve.wait_ge(mine, e * 2 + 4)
                layer_norm("ln2_g", "ln2_b", l, f"ln2_{l}")

            dve.wait_ge(ev("stores"), 16 * 6)
            out_and_moe(0)
            odd_dve(dve, V, s, until, empty, mul, add, sub, bc, head_norm, out_and_moe)

        @block.scalar
        def _(act):
            A = Ring(act, AB, a_full, a_free)
            s = Steps(act, act_step)

            for dst, src in x_loads:
                act.dma_start(dst, src).then_inc(ev("x_in"), 16)
            for dst, src in s5_loads:
                act.dma_start(dst, src).then_inc(ev("s5_in"), 16)
            for dst, src in vec_loads:
                act.dma_start(dst, src).then_inc(ev("vec_in"), 16)

            def empty(dst, width, f=ACT.Copy, rows=P, **kw):
                b = A.take()
                return act.activation(dst, b[:rows, 0:width], f, **kw).then_inc(a_free, 1)

            for m in range(4):
                empty(UF[:, m, :], NT)
            act.wait_ge(ev("s5_in"), 16 * len(s5_loads))
            act.activation(ROWS[0:GP, 2, 4:6], LDT, ACT.Exp).then_inc(ev("dt_ready"), 1)
            act.wait_ge(ev("mag_arg"), 1)
            act.activation(ROWS[0:GP, 9, :], ROWS[0:GP, 3, :], ACT.Exp).then_inc(ev("sin_ready"), 1)
            act.wait_ge(ev("sin_arg"), 1)
            act.activation(ROWS[0:GP, 7, :], ROWS[0:GP, 4, :], ACT.Sin).then_inc(ev("sin_ready"), 1)
            act.activation(ROWS[0:GP, 8, :], ROWS[0:GP, 5, :], ACT.Sin).then_inc(ev("sin_ready"), 1)
            for m in range(4):
                empty(QK[:, m, :], NT)
            for m in range(4):
                empty(VF[:, m, :], NT)
            for m in range(4):
                empty(GATE[:, m, :], NT, ACT.Silu)
            act.wait_ge(ev("bi_ready"), 1)
            for j in range(2):
                for g in range(0, GP, 4):
                    b = A.take()
                    act.activation(BIT[:, j, g:g + 4, :], b[:, :].rearrange("p (g f) -> p g f", g=4), ACT.Copy).then_inc(a_free, 1)
            act.wait_ge(ev("uc_in"), 48)
            for q in range(4):
                if q >= 2:
                    act.wait_ge(*mark[f"ug{q - 2}"])
                act.activation(UCQ[0:UCOL, q % 2], UC[0:UCOL, :, P * q:P * q + P].rearrange("p t (g c) -> p g t c", g=8), ACT.Copy).then_inc(ev("ucq_ready"), 1)
            act.wait_ge(ev("k_ready"), 16 * CL)
            for q in range(8):
                b = A.take()
                act.activation(Y[0:HCOL, :, P * (q // 2):P * (q // 2) + P].rearrange("p t (g two c) -> p two g t c", two=2, c=SC_N)[:, q % 2],
                               b[0:HCOL, :].rearrange("p (g t c) -> p g t c", g=4, t=CL), ACT.Copy).then_inc(a_free, 1)
            act.wait_ge(*mark["y_fm"])
            act.activation(ZF, YF, ACT.Gelu_apprx_tanh).then_inc(ev("z_ready"), 1)
            act.wait_ge(ev("z_ready"), 1)
            for m in range(4):
                empty(YF[:, m, :], NT, ACT.Sigmoid, bias=vec("s5_b_glu", m))
            act.wait_ge(ev("y_out"), 32)
            for h in range(RH):
                empty(OT[:, h, 0:NPR], NPR)

            def std(sd, n, e, ring_tiles):
                for m in range(ring_tiles):
                    empty(sd[:, m, :], NT, ACT.Sqrt, scale=1.0 / n, bias=eps[e])

            std(OSD, RDV, 1e-5, 4)

            def ln_std():
                b = A.take()
                act.activation(LSD, b[:, 0:NT], ACT.Sqrt, scale=1.0 / D, bias=eps[1e-5]).then_inc(ev("lsd_ready"), 1)
                act.wait_ge(ev("lsd_ready"), ln_std.n + 1)
                ln_std.n += 1
                act.nop().then_inc(a_free, 1)
            ln_std.n = 0

            def moe(l):
                ln_std()
                for t, (c0, r) in enumerate(TT):
                    for h in range(2):
                        empty(XTM[:r, t, 512 * h:512 * h + 512], 512, rows=r)
                act.wait_ge(ev("lc_shift"), l + 1)
                act.activation(RT[:, 2, :, 0:4], RT[:, 2, :, 0:4], ACT.Exp).then_inc(ev("lc_exp"), 1)
                act.wait_ge(ev("lf_diff"), l + 1)
                act.activation(RT[:, 5, :, 8:9], RT[:, 5, :, 8:9], ACT.Exp).then_inc(ev("lc_exp"), 1)
                for g in range(NG):
                    empty(DSPT[:, g, :], NT)
                for e in range(EG):
                    empty(CB[:, e, :, :].rearrange("p g c -> p (g c)"), 512)
                va, aa = mark[f"moe{l}"]
                assert A.n == aa

                def silu(e, i):
                    if not (e < 2 and isinstance(i, int) and i == 0):
                        act.wait_ge(v_free, (va - V_GROUP + V_UP[e + 2] if e < 2 else va + V_UP[e - 2]) + i * V_GROUP)
                    b = A.take()
                    act.activation(SIL[:, e % 2, :, :].rearrange("p f c -> p (f c)"), b[:, 0:2 * CAP], ACT.Silu).then_inc(a_free, 1)

                with act.Fori(0, NG) as i:
                    A.n = aa + i * EG
                    for e in range(EG):
                        silu(e, i)
                A.n = aa + NE
                act.wait_ge(ev("over_known"), l + 1)
                over = act.value_load(OVER[0:1, l:l + 1], min_val=0, max_val=1)
                with act.If(over > 0):
                    with act.Fori(0, NE) as e:
                        act.wait_ge(ev(f"x_full{l}"), e + 2)
                        act.activation(XSIL[:, 0, :], banks[4][:, 0:NT], ACT.Silu)
                        act.activation(XSIL[:, 1, :], banks[5][:, 0:NT], ACT.Silu).then_inc(ev(f"x_sil{l}"), 1)
                ln_std()

            moe(0)
            odd_act(act, A, s, empty, std, moe)

        @block.gpsimd
        def _(pool):
            s = Steps(pool, pool_step)
            for dst, src in router_loads:
                pool.dma_start(dst, src).then_inc(ev("router_in"), 16)
            for j, n in enumerate(("state_s5_re", "state_s5_im")):
                pool.dma_start(H0R[:, j, :], a[n][0].rearrange("b (g two) s -> (b g) (two s)", two=2)).then_inc(ev("h0_in"), 16)
            pool.wait_ge(ev("bb_ready"), 1)
            sh = [P, GP, CL, SC_N]
            bb = [BB[:, j].unsqueeze(2).to_broadcast(sh) for j in range(2)]
            w1, w2 = TP[:, 0], TP[:, 1]

            def powers(j):
                return PW[:, j, CL - 1::-1, :].rearrange("p l g -> p g l").unsqueeze(3).to_broadcast(sh)

            for o, (x, y, op) in enumerate(((0, 0, ALU.subtract), (0, 1, ALU.add))):
                for h in range(0, GP, 8):
                    g = slice(h, h + 8)
                    s.mark(pool.tensor_tensor(w1[:, g], bb[0][:, g], powers(x if o == 0 else 1)[:, g], ALU.mult), pool_step)
                    s.do(pool.tensor_tensor(w2[:, g], bb[1][:, g], powers(1 if o == 0 else 0)[:, g], ALU.mult))
                    last = o == 1 and h == 8
                    s.do(pool.tensor_tensor(BI[:, o, g], w1[:, g], w2[:, g], op), ev("bi_ready") if last else None)
            pool.wait_ge(*mark["bit"])
            s.mark(pool.memset(UC[0:UCOL], 0.0), ev("uc_zero"))
            pool.wait_ge(*mark["srow"])
            pool.dma_start(srow_dram, SROW[0:NB, :]).then_inc(ev("srow_out"), 16)
            pool.wait_ge(ev("srow_out"), 16)
            pool.dma_start(QS, srow_dram[:, 0:256].rearrange("b (x d) -> b x d", d=16)).then_inc(ev("smp_in"), 16)
            pool.dma_start(KS, srow_dram[:, 256:512].rearrange("b (x d) -> b x d", d=16)).then_inc(ev("smp_in"), 16)
            for q in range(4):
                pool.dma_start(VS[q:P:4, :], srow_dram[:, 512:1024].rearrange("b (h v) -> b h v", v=RDV)).then_inc(ev("smp_in"), 16)
            pool.wait_ge(*mark["y_chunk"])
            pool.dma_start(RETS, a["state_ret"][0].rearrange("b h (q d) v -> (b h q) d v", q=4)).then_inc(ev("smp_in"), 16)
            odd_pool(pool, s)

        @block.sync
        def _(sp):
            out_n = [0]

            def store(dst, src):
                sp.dma_start(dst, src).then_inc(ev("stores"), 16)
                out_n[0] += 16

            def fill(n):
                if n >= NSLOT:
                    sp.wait_ge(*slot_done[n - NSLOT])
                for dst, src in fills[n]:
                    sp.dma_start(dst, src).then_inc(w_in[n % NSLOT], 16)

            def over_capacity_sp(l):
                sp.wait_ge(*mark[f"moe_out{l}"])
                sp.wait_ge(ev("over_known"), l + 1)
                over = sp.value_load(OVER[0:1, l:l + 1], min_val=0, max_val=1)
                with sp.If(over > 0):
                    for e in range(NE):
                        if e:
                            sp.wait_ge(ev(f"x_sums{l}"), e)
                        for j, name in enumerate(("moe_w_gate", "moe_w_up", "moe_w_down")):
                            sp.dma_start(XW[:, j, :].rearrange("p (k c) -> p k c", k=2 if j == 2 else KD), a[name][l, e].rearrange("(k p) c -> p k c", p=P)).then_inc(ev(f"x_w{l}"), 16)
                    sp.wait_ge(ev(f"x_w{l}"), 48 * NE)

            for n in range(NSLOT):
                fill(n)
            sp.wait_ge(*mark["u_tok"])
            for t, (c0, r) in enumerate(TT):
                sp.dma_start(u_dram[c0:c0 + r, :], UTOK[:r, t, :]).then_inc(ev("u_out"), 16)
            for n in (6, 7, 8):
                fill(n)
            sp.wait_ge(ev("uc_zero"), 1)
            sp.wait_ge(ev("u_out"), 48)
            sp.dma_start(UC[0:NCH], u_dram[0:NPR, :].rearrange("(k t) f -> k t f", t=CL)).then_inc(ev("uc_in"), 16)
            sp.dma_start(UC[NCH:HCOL, 0, :], u_dram[NPR:NT, :]).then_inc(ev("uc_in"), 16)
            sp.dma_start(UC[HCOL:UCOL, CL - 1, :], u_dram[NPR:NT, :]).then_inc(ev("uc_in"), 16)
            sp.wait_ge(ev("k_zero"), 1)
            sp.wait_ge(*mark["kl"])
            for t in range(CL):
                sp.dma_start(KT_[SC_N * t:SC_N * t + SC_N, :, SC_N * t:P], KL[0:SC_N, :, 0:P - SC_N * t]).then_inc(ev("k_ready"), 16)
            sp.wait_ge(*mark["y_chunk"])
            sp.dma_start(y_dram[0:NPR, :].rearrange("(k t) f -> k t f", t=CL), Y[0:NCH]).then_inc(ev("y_out"), 16)
            sp.dma_start(y_dram[NPR:NT, :], Y[NCH:HCOL, 0, :]).then_inc(ev("y_out"), 16)
            sp.wait_ge(ev("y_out"), 32)
            for t, (c0, r) in enumerate(TT):
                sp.dma_start(YTOK[:r, t, :], y_dram[c0:c0 + r, :]).then_inc(ev("ytok_in"), 16)
            for n in range(9, S_MOE[0] + 1):
                fill(n)
            sp.wait_ge(*mark["h_rows"])
            for j, n in enumerate((5, 7)):
                store(outs[n][0].rearrange("b (g two) s -> (b g) (two s)", two=2), HROW[:, j, :])
                store(outs[n - 1][0, 0].rearrange("(g two) s -> g (two s)", two=2), HROW[0:GP, 2 + j, :])
            sp.wait_ge(ev("rets_ready"), 1)
            store(outs[3][0].rearrange("b h (q d) v -> (b h q) d v", q=4), RETS)
            sp.wait_ge(*mark["ret_state"])
            store(outs[2][0, 0].rearrange("h d v -> d h v"), RSTO[0:RDK])
            for n in range(S_MOE[0] + 1, S_OD):
                fill(n)
            for n in range(S_OD, S_OD + NSLOT):
                fill(n)
            over_capacity_sp(0)
            odd_sp(sp, store, fill, over_capacity_sp)
            sp.wait_ge(ev("stores"), out_n[0])


_INS = ["x_prompt", "x_sample", "state_ret", "state_s5_re", "state_s5_im", "state_wkv", "state_shift", "cache_kv",
        "cache_krope", "page_table", "meta_tokens", "ev_w_in", "ret_gn_g", "ret_gn_b", "s5_a_re", "s5_a_im",
        "s5_log_dt", "s5_b_re", "s5_b_im", "s5_c_re", "s5_c_im", "s5_d", "s5_w_glu", "s5_b_glu", "ev_w_out",
        "od_w_in", "rwkv_mu", "rwkv_w0", "rwkv_w2", "rwkv_a0", "rwkv_a2", "rwkv_g2", "rwkv_k_k", "rwkv_k_a",
        "rwkv_r_k", "rwkv_gn_g", "rwkv_gn_b", "mla_q_norm", "mla_w_qb", "mla_kv_norm", "mla_w_uk", "mla_w_uv",
        "od_w_out", "ln1_g", "ln1_b", "ln2_g", "ln2_b", "moe_w_coarse", "moe_b_coarse", "moe_w_fine",
        "moe_b_fine", "moe_w_gate", "moe_w_up", "moe_w_down"]
_OUTS = [(1, SEQ, D), (NB, 1, D), (1, 1, RH, RDK, RDV), (1, NB, RH, RDK, RDV), (1, 1, SG_N, SP_N), (1, NB, SG_N, SP_N),
         (1, 1, SG_N, SP_N), (1, NB, SG_N, SP_N), (1, 1, WH, WD, WD), (1, NB, WH, WD, WD), (1, 1, RP), (1, NB, RP),
         (1, 1, NPR, KVL), (NB, 1, 1, KVL), (1, 1, NPR, ROPE), (NB, 1, 1, ROPE)]


def kernel(**inputs):
    import concourse.bacc as _bacc
    from concourse import mybir as _mybir
    from concourse.bass_utils import run_bass_kernel_spmd as _run

    nc = _bacc.Bacc("TRN2", target_bir_lowering=False, num_devices=1)
    arrays, args = {}, {}
    for name in _INS + ["consts"]:
        v = np.ascontiguousarray(inputs[name]) if name != "consts" else const_table()
        arrays[f"in_{name}"] = v
        args[name] = nc.dram_tensor(f"in_{name}", v.shape, _mybir.dt.from_np(v.dtype), kind="ExternalInput").ap()
    shapes = list(_OUTS)
    outs = [nc.dram_tensor(f"out_{i}", sh, F32, kind="ExternalOutput").ap() for i, sh in enumerate(shapes)]
    program(nc, args, outs)
    r = _run(nc, [arrays], core_ids=[0])
    return tuple(r.results[0][f"out_{i}"] for i in range(len(_OUTS)))
```

```python
import math
from contextlib import ExitStack

import numpy as np

import concourse.bass as bass
from concourse import mybir

F32 = mybir.dt.float32
I32 = mybir.dt.int32
ALU = mybir.AluOpType
ACT = mybir.ActivationFunctionType
AX = mybir.AxisListType

P = 128
D = 1024
KD = D // P
NM, SEQ, NB = 16, 256, 8
NPR = NM + SEQ
NT = NPR + NB
TT = [(0, 128), (128, 128), (256, NT - 256)]
PT = [(0, 128), (128, 128), (256, NPR - 256)]
PAST, PAGE = 1024, 128
NPG = PAST // PAGE
ALPHA = 4.0 ** 0.25
RH, RDK, RDV = 4, 64, 128
SG_N, SC_N, SP_N = 32, 16, 64
GP = SG_N // 2
CL = 8
NCH = NPR // CL
UCOL = NCH + 2 * NB
HCOL = NCH + NB
WH, WD = 8, 64
WC = 32
LORA = 64
RP = 1792
RT_N = RP // P
DECAY = math.exp(-0.5)
MH, NOPE, ROPE, VH = 8, 64, 32, 64
QL, KVL = 384, 256
SCALE = (NOPE + ROPE) ** -0.5
NE, DE = 16, 256
NG, EG = 4, 4
CAP = P
BIG = 1.0e30

CONSTS = [("ident", P), ("ones", P), ("blk", P), ("id64", 64), ("perm64", P), ("perm32", P),
          ("cosd", NT), ("sind", NT), ("cosr", NT), ("sinr", NT),
          ("retmask", RH * NPR), ("kdec", 3 * RH), ("gam", 1), ("selbh", NB * RH),
          ("strictT", P), ("inclT", P), ("m2T", P), ("m2N", P),
          ("off2", P), ("off4", P), ("off8", P), ("off16", P),
          ("scan", NPR), ("causal", P), ("curmask", NB), ("rank", 4), ("eps", 4), ("before", P), ("iota", P)]
COFF = {}
_o = 0
for _n, _w in CONSTS:
    COFF[_n] = (_o, _w)
    _o += _w
NCONST = _o


def const_table():
    c = {n: np.zeros((P, w), np.float64) for n, w in CONSTS}
    i = np.arange(P)
    c["ident"] = np.eye(P)
    c["ones"][:] = 1.0
    c["id64"] = (i[:, None] % 64 == np.arange(64)[None, :]).astype(float)
    c["blk"] = (i[:, None] // 64 == i[None, :] // 64).astype(float)
    for name, d in (("perm64", 64), ("perm32", 32)):
        for m in range(P):
            if m % d < d // 2:
                c[name][m + d // 2, m] = -1.0
            else:
                c[name][m - d // 2, m] = 1.0
    pos = np.concatenate([np.arange(NPR), np.full(NB, PAST)]).astype(np.float32)
    for d, names in ((64, ("cosd", "sind")), (32, ("cosr", "sinr"))):
        inv = (10000.0 ** (-np.arange(0, d, 2, dtype=np.float32) / np.float32(d))).astype(np.float32)
        ang = (pos[None, :] * inv[:, None]).astype(np.float32)[i % (d // 2)]
        c[names[0]], c[names[1]] = np.cos(ang.astype(np.float64)), np.sin(ang.astype(np.float64))
    logg = np.log1p(-np.exp2(-5.0 - np.arange(RH)))
    x = np.arange(NPR)
    diff = x[None, :] - i[:, None]
    c["retmask"] = np.concatenate([np.where(diff >= 0, np.exp(logg[h] * np.maximum(diff, 0)), 0.0) for h in range(RH)], 1)
    c["kdec"] = np.stack([np.exp(logg[h] * np.maximum(NPR - 1 - (128 * t + i), 0)) for t in range(3) for h in range(RH)], 1)
    h_of = (i // 4) % RH
    c["gam"] = np.exp(logg[h_of])[:, None]
    c["selbh"] = ((i[:, None] // 4 // RH == np.arange(RH * NB)[None, :] % NB) &
                  (h_of[:, None] == np.arange(RH * NB)[None, :] // NB)).astype(float)
    a, b = i[:, None], i[None, :]
    blk = a // WC == b // WC
    c["strictT"] = (blk & (a < b)).astype(float)
    c["inclT"] = (blk & (a <= b)).astype(float)
    c["m2T"] = ((a // 2 == b // 2) & (a < b)).astype(float)
    c["m2N"] = ((a // 2 == b // 2) & (b < a)).astype(float)
    for s in (2, 4, 8, 16):
        c[f"off{s}"] = ((a // (2 * s) == b // (2 * s)) & (a // s > b // s)).astype(float)
    c["scan"] = np.broadcast_to((x % WC != 0).astype(float), (P, NPR))
    c["causal"] = np.where(b <= a, 0.0, -BIG)
    c["curmask"] = np.where((i[:, None] // MH) == np.arange(NB)[None, :], 0.0, -BIG)
    c["rank"] = np.broadcast_to(np.array([4.0, 3.0, 2.0, 1.0]), (P, 4))
    c["eps"] = np.broadcast_to(np.array([1e-5, 64e-5, 1e-6, 0.0]), (P, 4))
    c["before"] = (a < b).astype(float)
    c["iota"] = np.broadcast_to(i[None, :].astype(float), (P, P))
    return np.ascontiguousarray(np.concatenate([c[n] for n, _ in CONSTS], 1).astype(np.float32))


VECS = [("ret_gn_g", 4), ("ret_gn_b", 4), ("s5_d", 4), ("s5_b_glu", 4), ("rwkv_mu", 14), ("rwkv_w0", 4),
        ("rwkv_a0", 4), ("rwkv_k_k", 4), ("rwkv_k_a", 4), ("rwkv_r_k", 4), ("rwkv_gn_g", 4), ("rwkv_gn_b", 4),
        ("mla_q_norm", 3), ("mla_kv_norm", 2), ("ln1_g", 16), ("ln1_b", 16), ("ln2_g", 16), ("ln2_b", 16)]
VOFF = {}
_o = 0
for _n, _w in VECS:
    VOFF[_n] = _o
    _o += _w
NVEC = _o

NSLOT = 6
SLOTF = 2048
EV_ORDER = [6, 7, 0, 1, 2, 3, 4, 5]
S_EV, S_GLU, S_EVO = 0, 8, 9
S_MOE = [13, 78]
S_OD = 61
S_QB, S_UKV, S_ODO = 71, 73, 74


V_GROUP = 16
V_UP, V_DOWN = [-1, 0, 3, 6], [2, 5, 8, 14]
A_GATE = [-1, 0, 1, 2]


class Ring:

    def __init__(self, eng, banks, full, free):
        self.eng, self.banks, self.full, self.free = eng, banks, full, free
        self.n, self.slot, self.deep = 0, 0, len(banks)

    def claim(self):
        if not (isinstance(self.n, int) and self.n < self.deep):
            self.eng.wait_ge(self.free, self.n - (self.deep - 1))
        return self._next()

    def take(self):
        self.eng.wait_ge(self.full, self.n + 1)
        return self._next()

    def _next(self):
        b = self.banks[self.slot]
        self.n, self.slot = self.n + 1, (self.slot + 1) % self.deep
        return b


class Steps:

    def __init__(self, eng, own):
        self.eng, self.own, self.n = eng, own, {}

    def mark(self, ins, sem):
        ins.then_inc(sem, 1)
        self.n[sem.name] = self.n.get(sem.name, 0) + 1

    def do(self, ins, sem=None):
        sem = self.own if sem is None else sem
        self.mark(ins, sem)
        self.eng.wait_ge(sem, self.n[sem.name])


SCRATCH = 30700
M_QK, M_GATE, M_VF, M_UF = 0, 1120, 2240, 3360
M_R1, M_R2, M_R3, M_R4, M_R5 = 4480, 8576, 12672, 17280, 21376
M_INJ, M_HS, M_PW, M_SV, M_BB = 25984, 27584, 28928, 29216, 29280


def slot_view(SLOT, n, k, c, o=0):
    return SLOT[:, n % NSLOT, o:o + k * c].rearrange("p (k c) -> p k c", k=k)


def program(nc, a, outs):
    sems = {}

    with ExitStack() as ctx:
        def sb(name, shape, dt=F32):
            return ctx.enter_context(nc.sbuf_tensor(name, shape, dt))

        def sem(name):
            return ctx.enter_context(nc.semaphore(name))

        def ev(name):
            if name not in sems:
                sems[name] = sem(name)
            return sems[name]

        CST = sb("consts", [P, NCONST])
        VC = sb("vec_cols", [P, P])
        RW = sb("router_w", [P, 2, KD, 20])
        RB = sb("router_b", [P, 2, 20])
        XT = sb("x_fm", [P, KD, NT])
        RES = sb("residual", [P, KD, NT])
        SLOT = sb("weight_slots", [P, NSLOT, SLOTF])
        S = sb("scratch", [P, SCRATCH])
        banks = [ctx.enter_context(nc.psum_tensor(f"bank{i}", [P, 512], F32)) for i in range(8)]
        VB, AB = banks[:4], banks[4:]
        v_full, v_free, a_full, a_free = sem("v_full"), sem("v_free"), sem("a_full"), sem("a_free")
        w_in = [sem(f"w_in{i}") for i in range(NSLOT)]
        dve_step, act_step, pool_step = sem("dve_step"), sem("act_step"), sem("pool_step")

        def dram(name, shape):
            return nc.dram_tensor(name, shape, F32, kind="Internal").ap()

        u_dram, y_dram = dram("u_tok_dram", [NT, 512]), dram("y_tok_dram", [NT, 512])
        srow_dram = dram("srow_dram", [NB, 1024])

        def cst(name):
            o, w = COFF[name]
            return CST[:, o:o + w]

        def vec(name, i=0, n=1):
            o = VOFF[name] + i
            return VC[:, o:o + n]

        def part(o, *dims):
            n = int(np.prod(dims))
            assert o + n <= SCRATCH, (o, dims)
            v = S[:, o:o + n]
            if len(dims) == 1:
                return v
            names = "abcd"[:len(dims)]
            return v.rearrange("p (" + " ".join(names) + ") -> p " + " ".join(names), **dict(zip(names[1:], dims[1:])))

        def resv(o, *dims):
            v = RES[:, :, :].rearrange("p k t -> p (k t)")[:, o:o + int(np.prod(dims))]
            if len(dims) == 1:
                return v
            names = "abcd"[:len(dims)]
            return v.rearrange("p (" + " ".join(names) + ") -> p " + " ".join(names), **dict(zip(names[1:], dims[1:])))

        ident = cst("ident")
        eps = {1e-5: cst("eps")[:, 0:1], 64e-5: cst("eps")[:, 1:2], 1e-6: cst("eps")[:, 2:3]}

        QK, GATE, VF, UF = (part(o, 4, NT) for o in (M_QK, M_GATE, M_VF, M_UF))
        XTOK, VROW = part(M_R4, 3, D), part(M_R4 + 3072, P)
        UTOK = part(M_R4, 3, 512)
        BI = part(M_R1, 2, GP, CL, SC_N)
        UC = part(M_R1, CL, 512)
        TP = part(M_R2, 2, GP, CL, SC_N)
        BIT = part(M_R2, 2, GP, P)
        TD = part(M_R3, 2, GP, CL + 1, SC_N)
        KL = part(M_R3, SG_N, P)
        Y = part(M_R3, CL, 512)
        KT_ = part(M_R4, SG_N, P)
        CP = part(M_R5, 2, GP, CL + 1, SC_N)
        UG = resv(0, SG_N, UCOL)
        UCQ = part(M_INJ, 2, 8, CL, SC_N)
        INJ = part(M_INJ, 2, GP, UCOL)
        HS = part(M_HS, 2, GP, HCOL)
        BRAW, CN = part(M_HS, 2, GP, SC_N), part(M_HS + 512, 2, 2, P)
        PW = part(M_PW, 2, CL + 1, GP)
        SV = part(M_SV, 4, GP)
        BB, CTT = part(M_BB, 2, GP, SC_N), part(M_BB + 512, 2, GP, SC_N)
        ROWS = resv(0, 15, P)
        A_RE, A_IM, LDT = ROWS[0:GP, 0, :], ROWS[0:GP, 1, :], ROWS[0:GP, 2, 0:2]
        YTOK, TOUT = part(M_R1, 3, 512), part(M_R1 + 1536, 16, RDV)
        YF, ZF = part(M_R2, 4, NT), part(M_R2 + 1120, 4, NT)
        MIXS, MIXR = part(M_INJ, 4, NT), part(M_HS, 4, NT)
        KTOK, VTOK, KDT = part(M_R4, 3, 256), part(M_R4 + 768, 3, 512), part(M_R4 + 2304, 3, 256)
        SROW = part(M_R4 + 3072, D)
        SCR = part(M_R5, RH, 3, NPR)
        RSTO = part(M_R5 + RH * 3 * NPR, RH, RDV)
        OT, OSQ, OSD = part(M_R3, 4, NT), part(M_R3 + 1120, 4, NT), part(M_R3 + 2240, 4, NT)
        HROW = part(M_R2 + 2240, 4, P)
        H0R = part(30304, 2, P)
        HF = part(M_BB, 2, NB, GP)
        HFP = part(M_BB + 256, 2, GP)
        HALF = NCH // 2
        PX = resv(SG_N * UCOL, 2, HALF, GP)
        TX = part(M_R1, 2, 2, GP, HALF - 1)
        RETS = resv(0, 16, RDV)
        KS, QS, VS = part(M_BB + 512, 16), part(M_BB + 528, 16), part(M_BB + 544, RDV)
        PARTO = part(M_BB + 672, RDV)
        SIL, HB = part(2048, 2, 2, CAP), part(2560, 2, 2, CAP)
        LG, RT = part(3584, 3, 20), part(3650, 10, 3, 16)
        WG = part(4136, NG, EG)
        DSP = part(4648, 3, NG, CAP)
        DSPT = part(6184, NG, NT)
        POS = part(7304, 3, NG)
        PLACE = part(7316, 3)
        CNT = part(7320, NG)
        XTM = part(10752, 3, D)
        XG = part(13824, KD, CAP)
        YG = part(14848, NG, D)
        XW, XSIL, XHB = part(10752, 3, SLOTF), part(16896, 2, NT), part(17456, 2, NT)
        XCT, XC, XROW = part(18016, NT), part(18300, 3, NE), part(18350, NT)
        OVER = ctx.enter_context(nc.sbuf_tensor("over_capacity", [P, 2], I32))
        LSQ, LSD = part(8200, KD, NT), part(10440, NT)

        x_loads = [
            (XTOK[0:NM, 0, :], a["meta_tokens"]),
            (XTOK[NM:P, 0, :], a["x_prompt"][0, 0:P - NM, :]),
            (XTOK[:, 1, :], a["x_prompt"][0, P - NM:2 * P - NM, :]),
            (XTOK[0:NM, 2, :], a["x_prompt"][0, 2 * P - NM:SEQ, :]),
            (XTOK[NM:NM + NB, 2, :], a["x_sample"].rearrange("b s d -> (b s) d")),
            (ident, a["consts"][:, 0:P]),
        ]
        const_load = (CST[:, P:NCONST], a["consts"][:, P:NCONST])
        def rows_of(name):
            v = a[name]
            if len(v.shape) == 3:
                v = v.rearrange("l h d -> l (h d)")
            return v.rearrange("l (t p) -> (l t) p", p=P)

        vec_loads = [(VROW[VOFF[n]:VOFF[n] + w, :], rows_of(n)) for n, w in VECS]
        s5_loads = [
            (A_RE, a["s5_a_re"][0].rearrange("(g two) s -> g (two s)", two=2)),
            (A_IM, a["s5_a_im"][0].rearrange("(g two) s -> g (two s)", two=2)),
            (LDT, a["s5_log_dt"].rearrange("l (g two) -> (l g) two", two=2)),
        ]
        for j, n in enumerate(("s5_b_re", "s5_b_im")):
            s5_loads.append((BRAW[:, j], a[n][0].rearrange("(g two) s c -> (two s) g c", two=2)))
        for j, n in enumerate(("s5_c_re", "s5_c_im")):
            for t in range(2):
                for two in range(2):
                    s5_loads.append((CN[:, j, t, two * SP_N:(two + 1) * SP_N],
                                     a[n][0].rearrange("(t g two) c s -> t two g c s", t=2, two=2)[t, two]))
        router_loads = []
        for l in range(2):
            router_loads.append((RW[:, l, :, 0:4], a["moe_w_coarse"][l].rearrange("(k p) g -> p k g", p=P)))
            for g in range(4):
                router_loads.append((RW[:, l, :, 4 + 4 * g:8 + 4 * g], a["moe_w_fine"][l, g].rearrange("(k p) e -> p k e", p=P)))
            router_loads.append((RB[:, l, 0:4], a["moe_b_coarse"][l:l + 1, :].to_broadcast([P, 4])))
            router_loads.append((RB[:, l, 4:20], a["moe_b_fine"][l:l + 1].rearrange("l g e -> l (g e)").to_broadcast([P, 16])))

        fills, od9 = {}, []
        for j, s in enumerate(EV_ORDER):
            fills[S_EV + j] = [(slot_view(SLOT, S_EV + j, KD, 256), a["ev_w_in"][0].rearrange("(k p) c -> p k c", p=P)[:, :, 256 * s:256 * s + 256])]
        w9 = slot_view(SLOT, S_OD + 9, KD, 256)
        odw = a["od_w_in"][0].rearrange("(k p) c -> p k c", p=P)
        for i in range(4):
            od9.append((w9[:, :, P + ROPE * i:P + ROPE * i + ROPE], odw[:, :, 2432:2464]))
        od9.append((w9[:, :, 0:P], odw[:, :, 2304:2432]))
        fills[S_GLU] = [(slot_view(SLOT, S_GLU, 4, 512), a["s5_w_glu"][0].rearrange("(k p) c -> p k c", p=P))]
        for j in range(4):
            fills[S_EVO + j] = [(slot_view(SLOT, S_EVO + j, KD, 256), a["ev_w_out"][0].rearrange("(k p) c -> p k c", p=P)[:, :, 256 * j:256 * j + 256])]
        for l in range(2):
            for e in range(NE):
                n = S_MOE[l] + 3 * e
                fills[n] = [(slot_view(SLOT, n, KD, DE), a["moe_w_gate"][l, e].rearrange("(k p) c -> p k c", p=P))]
                fills[n + 1] = [(slot_view(SLOT, n + 1, KD, DE), a["moe_w_up"][l, e].rearrange("(k p) c -> p k c", p=P))]
                fills[n + 2] = [(slot_view(SLOT, n + 2, 2, D), a["moe_w_down"][l, e].rearrange("(k p) c -> p k c", p=P))]
        fills[S_OD + 9] = od9
        for j in range(9):
            w = 256
            fills[S_OD + j] = [(slot_view(SLOT, S_OD + j, KD, w), a["od_w_in"][0].rearrange("(k p) c -> p k c", p=P)[:, :, 256 * j:256 * j + w])]
        for j in range(2):
            fills[S_QB + j] = [(slot_view(SLOT, S_QB + j, 3, 384), a["mla_w_qb"][0].rearrange("(k p) c -> p k c", p=P)[:, :, 384 * j:384 * j + 384])]
        fills[S_UKV] = [(slot_view(SLOT, S_UKV, 2, 512), a["mla_w_uk"][0].rearrange("(k p) h n -> p k (h n)", p=P)),
                        (slot_view(SLOT, S_UKV, 2, 512, 1024), a["mla_w_uv"][0].rearrange("(k p) h n -> p k (h n)", p=P))]
        for j in range(4):
            fills[S_ODO + j] = [(slot_view(SLOT, S_ODO + j, KD, 256), a["od_w_out"][0].rearrange("(k p) c -> p k c", p=P)[:, :, 256 * j:256 * j + 256])]

        def landed(n):
            return sum(16 * len(fills[m]) for m in range(n % NSLOT, n + 1, NSLOT))

        kt_read = {}
        slot_done = {}
        mark = {}

        def bc(v, shape, at):
            return v.unsqueeze(at).to_broadcast(shape)

        block = ctx.enter_context(nc.Block())

        PR, QA, CKV, KRF = part(0, RT_N, NT), part(3920, 3, NT), part(4760, 2, NT), part(5320, NT)
        XM = part(5600, RT_N, NT)
        XR, XK, XV = XM[:, 0:4], XM[:, 4:8], XM[:, 8:12]
        DIF = part(9520, RT_N, NT)
        SW, AS, KK = (part(9520 + 1120 * i, 4, NT) for i in range(3))
        TW, GX = part(12880, NT), part(13160, NT)
        GG, K2, CS, RTF, ATF, KTF, BTF, KLF, BLF, BON = (part(13440 + 1120 * i, 4, NT) for i in range(10))
        YW = CS
        E1, E2, E3 = (part(1120 * i, 4, NT) for i in range(3))
        LW, G2 = part(24640, 512), part(25152, 512)
        SSH, SHO = part(25664, RP), part(27456, RP)
        SROW2 = part(25664, 6 * 512)
        SMP = part(29248, 6, 4, NB)
        PL = part(24640, 4, 9)
        WKS = resv(0, 32, WD)
        SV5, SVV = part(30272, 5, WD), part(30592, 32)
        SAS, SYS = part(30624, 32), part(30656, 32)
        NTM, TM_, TTM, XX = (part(25664 + 1024 * i, 2, 4, P) for i in range(4))
        ST = part(29760, 2, 4, WD)
        AKT, RBT, RKT = (part(1024 * i, 2, 4, P) for i in range(3))
        TA = part(3072, 512)
        ATK, BLK, KLK, VTK = (part(5600 + 512 * i, 512) for i in range(4))
        AK, TV, RE, GTM, CCM = part(9520, 512), part(10032, 512), part(10544, 4, P), part(11056, 4, 4, WD), part(12080, 4, 4, WD)
        SWO = part(15072, WH, WD)
        TS = part(14560, 16, WD)
        YR8 = part(14560, 512)
        OSQ1, OSD1 = part(25872, 4, NT), part(26992, 4, NT)
        MIXR1, MIXS1 = part(28460, 4, NT), part(29580, 4, NT)
        CK = part(0, NB, NPG, 288)
        WUKT, QAN, MSQ, MSD = part(0, MH, KVL), part(2048, 3, NT), part(2888, 3, NT), part(5600, 2, NT)
        KRR, RT1, RT2 = part(6160, NT), part(6440, NT), part(6720, NT)
        Q96, K96 = part(18432, MH, NT), part(20672, MH, NT)
        VM, CT9, CNF = part(22912, 3, 512), part(24448, 3, 288), part(25312, 2, NT)
        PTS = part(25872, 3, NPR)
        SCM = part(26688, 2, 3, NPR)
        STAT = part(28320, 2, 3, 4)
        QLP, QLF, CS8, C8T = resv(0, NB, 3, 64), resv(1536, 3, 64), resv(1728, 288), resv(2016, 3, NB)
        KTB = SLOT[:, S_MOE[1] % NSLOT, :]
        SCB = SLOT[:, (S_ODO + 3) % NSLOT, :]
        SCS = SCB[:, 0:PAST + NB]
        KT3 = [[KTB[:, 512 * k:512 * k + 512] for k in range(3)],
               [KTB[:, 1536:2048], SCB[:, 1040:1552], CNF.rearrange("p m t -> p (m t)")[:, 0:512]]]
        P8, PC, OLT = part(25632, NPG, 64), part(26144, 64), part(26208, 2, 64)
        STS, O8 = part(26336, 4), part(18432, NB, KVL)
        YOUT = part(12000, 3, D)
        PTAB = ctx.enter_context(nc.sbuf_tensor("page_ids", [1, NB * NPG], I32))
        srow2_dram, yrow_dram = dram("srow2_dram", [NB, 3072]), dram("yrow_dram", [NB, 512])

        od_loads = [
            (LW[0:LORA], a["rwkv_w2"][0]),
            (LW[LORA:P], a["rwkv_a2"][0]),
            (G2, a["rwkv_g2"][0]),
            (SSH[0:NB], a["state_shift"][0]),
            (PTAB[0:1, :], a["page_table"].rearrange("(o b) n -> o (b n)", o=1)),
        ]

        def odd_pe(pe, V, A, close, until, slot, used, to_fm, project, fm_sums, out_and_moe):
            pe.wait_ge(ev("od_in"), 16 * len(od_loads))
            b = V.claim()
            for m in range(RT_N):
                ins = pe.transpose(b[:, NB * m:NB * m + NB], SSH[0:NB, P * m:P * m + P], ident[:NB, :NB])
            close(V, ins, "prev")
            for j in range(10):
                slot(S_OD + j)
                for m2 in range(2):
                    project(S_OD + j, m2, 256, XT, KD, A, f"od{2 * j + m2}", (ev("ln_done"), KD + 1) if j == m2 == 0 else None)
                used(S_OD + j, A)
            until("od13")
            for q in range(0, RT_N, 4):
                b = V.claim()
                for m in range(q, min(q + 4, RT_N)):
                    ins = pe.transpose(b[0:NB + 1, P * (m - q):P * (m - q) + P], PR[:, m, NPR - 1:NT], ident)
                close(V, ins, "sho")
            pe.wait_ge(ev("lora_in"), 2)
            for m in range(4):
                b = A.claim()
                close(A, pe.matmul(b[:, 0:NT], LW[0:LORA, P * m:P * m + P], TW[0:LORA, :], start=True, stop=True), "sw")
            for m in range(4):
                b = A.claim()
                close(A, pe.matmul(b[:, 0:NT], LW[LORA:P, P * m:P * m + P], XM[LORA:P, 12, :], start=True, stop=True), "as")
            for m in range(4):
                b = A.claim()
                close(A, pe.matmul(b[:, 0:NT], G2[:, P * m:P * m + P], GX, start=True, stop=True), "gg")
            fm_sums(E1, cst("blk"), 4, False, "kk_sq", "kk_sq_in", A)
            fm_sums(E1, cst("blk"), 4, False, "bonus", "bonus_in")
            pe.wait_ge(ev("smp_cols"), 1)
            for q in range(6):
                b = A.claim()
                for m in range(4):
                    ins = pe.transpose(b[0:NB, P * m:P * m + P], SMP[:, q, m, :], ident)
                close(A, ins, "srow2")
            pe.wait_ge(ev("wkv_in"), 1)
            n_st = 0
            for tt, (c0, r) in enumerate(PT):
                for src in (ATF, BLF, KLF, XV):
                    b = V.claim()
                    for m in range(4):
                        ins = pe.transpose(b[:r, P * m:P * m + P], src[:, m, c0:c0 + r], ident)
                    close(V, ins, "wkv_tok")

                def heads(b, n):
                    return b[:, 0:4 * n].rearrange("p (h x) -> p h x", h=4)

                for par in range(2):
                    lo = 64 * par
                    for lt, rt in ((BTF, ATF), (ATF, BTF), (KTF, ATF), (BTF, RTF), (KTF, RTF)):
                        b = V.claim()
                        for hp in range(4):
                            ins = pe.matmul(heads(b, r)[:r, hp, :], lt[lo:lo + 64, hp, c0:c0 + r], rt[lo:lo + 64, hp, c0:c0 + r], start=True, stop=True)
                        close(V, ins, f"prod{par}")
                for par in range(2):
                    pe.wait_ge(ev("t_init"), 2 * tt + par + 1)
                for lev in range(4):
                    for par in range(2):
                        if lev > 0:
                            until(f"t{par}")
                        b = V.claim()
                        for hp in range(4):
                            ins = pe.matmul(heads(b, r)[:r, hp, :], NTM[:r, par, hp, 0:r], TM_[:r, par, hp, 0:r], start=True, stop=True)
                        close(V, ins, f"x{par}")
                    for par in range(2):
                        until(f"x{par}")
                        if lev < 3:
                            b = V.claim()
                            for hp in range(4):
                                ins = pe.matmul(heads(b, r)[:r, hp, :], TTM[:r, par, hp, 0:r], XX[:r, par, hp, 0:r], start=True, stop=True)
                            close(V, ins)
                        b = V.claim()
                        for hp in range(4):
                            ins = pe.matmul(heads(b, r)[:r, hp, :], XX[:r, par, hp, 0:r], TTM[:r, par, hp, 0:r], start=True, stop=True)
                        close(V, ins, f"t{par}")
                b = V.claim()
                for h in range(WH):
                    ins = pe.matmul(b[:r, WD * h:WD * h + WD], AKT[:r, h % 2, h // 2, 0:r], VTK[:r, WD * h:WD * h + WD], start=True, stop=True)
                close(V, ins, "ak")
                until("t1")
                for src, name in ((ATK, "ta"), (AK, "tv")):
                    if name == "tv":
                        until("ak")
                    b = V.claim()
                    for h in range(WH):
                        ins = pe.matmul(b[:r, WD * h:WD * h + WD], TTM[:r, h % 2, h // 2, 0:r], src[:r, WD * h:WD * h + WD], start=True, stop=True)
                    close(V, ins, name)
                until("ta")
                b = V.claim()
                for h in range(WH):
                    ins = pe.matmul(heads(b, r)[64 * (h % 2):64 * (h % 2) + 64, h // 2, :], TA[:r, WD * h:WD * h + WD], RBT[:r, h % 2, h // 2, 0:r], start=True, stop=True)
                close(V, ins, "re")
                until("tv")
                nch = max(1, r // WC)
                rc = min(r, WC)
                for c in range(nch):
                    b = V.claim()
                    k = slice(WC * c, WC * c + rc)
                    for h in range(WH):
                        o, hs = slice(64 * (h % 2), 64 * (h % 2) + 64), slice(WD * h, WD * h + WD)
                        pe.matmul(b[o, WD * (h // 2):WD * (h // 2) + WD], TA[k, hs], BLK[k, hs], start=True, stop=True)
                        q = b[o, 256 + WD * (h // 2):256 + WD * (h // 2) + WD]
                        pe.matmul(q, BLK[k, hs], TV[k, hs], start=True, stop=False)
                        ins = pe.matmul(q, KLK[k, hs], VTK[k, hs], start=False, stop=True)
                    close(V, ins, "gc")
                by = A.claim()
                until("re")
                for h in range(WH):
                    o, hs = slice(64 * (h % 2), 64 * (h % 2) + 64), slice(WD * h, WD * h + WD)
                    q = heads(by, r)[o, h // 2, :]
                    pe.matmul(q, TV[:r, hs], RBT[:r, h % 2, h // 2, 0:r], start=(h < 2), stop=False, skip_group_check=True)
                    pe.matmul(q, VTK[:r, hs], RKT[:r, h % 2, h // 2, 0:r], start=False, stop=True, skip_group_check=True)
                until("gc")
                for c in range(nch):
                    if n_st == 0:
                        pe.wait_ge(ev("state0"), 1)
                    else:
                        until("state")
                    b = V.claim()
                    for h in range(WH):
                        o = slice(64 * (h % 2), 64 * (h % 2) + 64)
                        ins = pe.matmul(b[o, WD * (h // 2):WD * (h // 2) + WD], GTM[o, c, h // 2, :], ST[o, n_st % 2, h // 2, :], start=True, stop=True)
                    close(V, ins, "state")
                    for h in range(WH):
                        o = slice(64 * (h % 2), 64 * (h % 2) + 64)
                        ins = pe.matmul(heads(by, r)[o, h // 2, WC * c:WC * c + rc], ST[o, n_st % 2, h // 2, :], RE[o, h // 2, WC * c:WC * c + rc],
                                        start=False, stop=True, skip_group_check=True)
                    n_st += 1
                close(A, ins, "yw")
            until("state")
            b = V.claim()
            for hp in range(4):
                ins = pe.transpose(b[0:WD, P * hp:P * hp + P], ST[:, n_st % 2, hp, :], ident)
            close(V, ins, "swo")
            pe.wait_ge(ev("yr8_in"), 16)
            b = V.claim()
            for m in range(4):
                ins = pe.transpose(b[:, NB * m:NB * m + NB], YR8[0:NB, P * m:P * m + P], ident[:NB, :NB])
            close(V, ins, "yw_smp")
            until("yw")
            until("yw_smp")
            fm_sums(YW, cst("blk"), 4, False, "hn_mean", None)

            fm_sums(MSQ, cst("ones"), 3, True, "qa_var", "qa_sq", A)
            fm_sums(OSQ1, cst("blk"), 4, False, "hn_var1", "hn_sq", A)
            fm_sums(MSQ, cst("ones"), 2, True, "kv_var", "kv_sq", A)
            b = V.claim()
            close(V, pe.matmul(b[:, 0:NT], cst("perm32"), KRF, start=True, stop=True), "kr_rope")
            ukv = S_UKV
            uk, uv = slot_view(SLOT, ukv, 2, 512), slot_view(SLOT, ukv, 2, 512, 1024)
            slot(S_QB)
            slot(S_QB + 1)
            slot(ukv)
            for q in range(4):
                b = V.claim()
                for i in range(2):
                    for k in range(2):
                        ins = pe.transpose(b[0:64, 256 * i + P * k:256 * i + P * k + P], uk[:, k, 64 * (2 * q + i):64 * (2 * q + i) + 64], ident)
                close(V, ins, "wukt")
            pe.wait_ge(ev("qan_ready"), 1)
            for h in range(MH):
                b = A.claim()
                w = slot_view(SLOT, S_QB + h // 4, 3, 384)
                for k in range(3):
                    ins = pe.matmul(b[0:96, 0:NT], w[:, k, 96 * (h % 4):96 * (h % 4) + 96], QAN[:, k, :], start=(k == 0), stop=(k == 2))
                close(A, ins, f"q{h}")
                if h == 3:
                    used(S_QB, A)
            used(S_QB + 1, A)
            for h in range(MH):
                until(f"q{h}")
                b = V.claim()
                close(V, pe.matmul(b[0:96, 0:NT], cst("perm32")[0:96, 0:96], Q96[0:96, h, :], start=True, stop=True), f"qr{h}")
            pe.wait_ge(ev("cnf_ready"), 1)
            for h in range(MH):
                b = A.claim()
                for k in range(2):
                    ins = pe.matmul(b[0:64, 0:NT], uk[:, k, 64 * h:64 * h + 64], CNF[:, k, :], start=(k == 0), stop=(k == 1))
                close(A, ins, "k96")
            for t, (c0, r) in enumerate(TT):
                b = V.claim()
                for k in range(2):
                    ins = pe.matmul(b[:r, :], CNF[:, k, c0:c0 + r], uv[:, k, :], start=(k == 0), stop=(k == 1))
                close(V, ins, "vm")
            pe.wait_ge(ev("krr_ready"), 1)
            for t, (c0, r) in enumerate(TT):
                b = V.claim()
                for k in range(2):
                    pe.transpose(b[:r, P * k:P * k + P], CNF[:, k, c0:c0 + r], ident)
                ins = pe.transpose(b[:r, 256:384], KRR[:, c0:c0 + r], ident)
                close(V, ins, "ct9")
            b = V.claim()
            for k in range(2):
                pe.transpose(b[:NB, P * k:P * k + P], CNF[:, k, NPR:NT], ident)
            close(V, pe.transpose(b[:NB, 256:384], KRR[:, NPR:NT], ident), "cs8")
            until("cs8")
            b = V.claim()
            for k in range(3):
                ins = pe.transpose(b[0:96, NB * k:NB * k + NB], CS8[0:NB, 96 * k:96 * k + 96], ident[:NB, :NB])
            close(V, ins, "c8t")
            until("qr7")
            until("wukt")
            b = V.claim()
            for k in range(3):
                for h in range(MH):
                    m = min(96, KVL - 96 * k)
                    o = b[0:m, 64 * k + h:64 * k + 64:MH]
                    ins = pe.matmul(o, WUKT[0:64, h, 96 * k:96 * k + m], Q96[0:64, h, NPR:NT], start=True, stop=True)
            close(V, ins, "qlat")

            def scores(h):
                for t, (c0, r) in enumerate(PT):
                    b = V.claim()
                    close(V, pe.matmul(b[:r, 0:c0 + r], Q96[0:96, h, c0:c0 + r], K96[0:96, h, 0:c0 + r], start=True, stop=True), "scm")

            def sample_scores(sm):
                pe.wait_ge(ev(f"cache_kv_in{sm}"), 16 * NPG)
                pe.wait_ge(ev(f"cache_krope_in{sm}"), 16 * NPG)
                for half in range(2):
                    for k in range(3):
                        b = A.claim()
                        for i in range(4):
                            ins = pe.transpose(b[0:96, P * i:P * i + P], CK[:, sm, 4 * half + i, 96 * k:96 * k + 96], ident)
                        close(A, ins, f"kt{sm}{half}")
                for half in range(2):
                    until(f"kt{sm}{half}")
                    b = V.claim()
                    for k in range(3):
                        ins = pe.matmul(b[0:64, :], QLP[0:96, sm, k, :], KT3[half][k][0:96, :], start=(k == 0), stop=(k == 2))
                    close(V, ins, "scs")
                    kt_read[sm, half] = (v_full, V.n)

            until("k96")
            pe.wait_ge(ev("k96_rope"), 1)
            pe.wait_ge(ev("qlp_ready"), 1)
            scores(0)
            for h in range(MH):
                if h < MH - 1:
                    scores(h + 1)
                pe.wait_ge(ev("p_ready"), h + 1)
                for j, (j0, rj) in enumerate(PT):
                    b = V.claim()
                    for t in range(j, 3):
                        c0, r = PT[t]
                        ins = pe.transpose(b[:rj, c0:c0 + r], SCM[:r, h % 2, t, j0:j0 + rj], ident[:r, :r])
                    close(V, ins, f"pts{h}")
                sample_scores(h)
                until(f"pts{h}")
                b = A.claim()
                o = 64 * (h % 2)
                for j, (j0, rj) in enumerate(PT):
                    ins = pe.matmul(b[o:o + 64, j0:NPR], VM[:rj, j, VH * h:VH * h + VH], PTS[:rj, j, j0:NPR], start=(j == 0), stop=(j == 2))
                close(A, ins, f"yd{h}")
            b = V.claim()
            for k in range(3):
                ins = pe.matmul(b[0:64, 0:NB], QLF[0:96, k, :], C8T[0:96, k, :], start=(k == 0), stop=(k == 2))
            close(V, ins, "scur")
            pe.wait_ge(ev("ps_ready"), 1)
            b = V.claim()
            for pg in range(NPG):
                ins = pe.transpose(b[:, 64 * pg:64 * pg + 64], SCS[0:64, PAGE * pg:PAGE * pg + PAGE], ident[:64, :64])
            close(V, ins, "p8")
            b = V.claim()
            close(V, pe.transpose(b[0:NB, 0:64], SCS[0:64, PAST:PAST + NB], ident[:64, :64]), "pc")
            until("pc")
            for q in range(NB // 2):
                b = V.claim()
                for sm in (2 * q, 2 * q + 1):
                    o, f = b[0:MH, KVL * (sm % 2):KVL * (sm % 2) + KVL], slice(MH * sm, MH * sm + MH)
                    pe.matmul(o, PC[0:NB, f], CS8[0:NB, 0:KVL], start=True, stop=False)
                    for pg in range(NPG):
                        ins = pe.matmul(o, P8[:, pg, f], CK[:, sm, pg, 0:KVL], start=False, stop=(pg == NPG - 1))
                close(V, ins, "o8")
            until("o8")
            b = V.claim()
            for k in range(2):
                for sm in range(NB):
                    ins = pe.transpose(b[:, 64 * k + MH * sm:64 * k + MH * sm + MH], O8[0:MH, sm, P * k:P * k + P], ident[:MH, :MH])
            close(V, ins, "olt")
            until("olt")
            b = V.claim()
            for h in range(MH):
                o = slice(64 * (h % 2), 64 * (h % 2) + 64)
                for k in range(2):
                    ins = pe.matmul(b[o, NB * (h // 2):NB * (h // 2) + NB], uv[:, k, VH * h:VH * h + VH], OLT[:, k, h:64:MH], start=(k == 0), stop=(k == 1))
            close(V, ins, "yd_smp")
            used(ukv, V)
            until(f"yd{MH - 1}")
            out_and_moe(1, S_ODO)
            for h in range(2):
                pe.wait_ge(ev("ln_done"), KD * 3 + 4 * h + 4)
                for t, (c0, r) in enumerate(TT):
                    b = V.claim()
                    for i in range(4):
                        ins = pe.transpose(b[:r, P * i:P * i + P], XT[:, 4 * h + i, c0:c0 + r], ident)
                    close(V, ins, "y_rows")

        def odd_dve(dve, V, s, until, empty, mul, add, sub, centre, scale, out_and_moe):
            dve.wait_ge(ev("od_in"), 16 * len(od_loads))
            b = V.take()
            for m in range(RT_N):
                until(f"od{m}")
                s.mark(sub(DIF[:, m, 1:NPR], PR[:, m, 0:NPR - 1], PR[:, m, 1:NPR]), dve_step)
                s.mark(dve.tensor_scalar(DIF[:, m, 0:1], PR[:, m, 0:1], -1.0, None, ALU.mult), dve_step)
                ins = sub(DIF[:, m, NPR:NT], b[:, NB * m:NB * m + NB], PR[:, m, NPR:NT])
                s.do(ins, v_free if m == RT_N - 1 else None)
                s.mark(dve.scalar_tensor_tensor(XM[:, m, :], DIF[:, m, :], vec("rwkv_mu", m), PR[:, m, :], ALU.mult, ALU.add), ev("xm_ready"))
            dve.wait_ge(ev("xm_ready"), RT_N)
            for q in range(0, RT_N, 4):
                n = min(4, RT_N - q)
                b = V.take()
                s.do(dve.tensor_copy(SHO[0:NB + 1, P * q:P * q + P * n], b[0:NB + 1, 0:P * n]), v_free)
            v4 = lambda name, w=NT: bc(vec(name, 0, 4), [P, 4, w], 2)
            s.do(mul(KK, XK, v4("rwkv_k_k")))
            s.do(mul(E1, KK, KK), ev("kk_sq_in"))
            until("as")
            s.do(dve.tensor_scalar(E3, AS, -1.0, None, ALU.add))
            s.do(mul(E3, E3, v4("rwkv_k_a")))
            s.do(dve.scalar_tensor_tensor(K2, E3, 1.0, XK, ALU.add, ALU.mult))
            for m in range(4):
                ins = dve.tensor_tensor_scan(CS[:, m, 0:NPR], cst("scan"), SW[:, m, 0:NPR], 0.0, ALU.mult, ALU.add)
                s.do(ins, ev("cs_ready") if m == 3 else None)
            s.do(sub(ATF[:, :, 0:NPR], CS[:, :, 0:NPR], SW[:, :, 0:NPR]))
            nf = NPR // WC
            chunks = lambda v: v[:, :, 0:nf * WC].rearrange("p m (c l) -> p m c l", l=WC)
            s.do(sub(chunks(KLF), chunks(CS), chunks(CS)[:, :, :, WC - 1:WC].to_broadcast([P, 4, nf, WC])))
            s.do(sub(KLF[:, :, nf * WC:NPR], CS[:, :, nf * WC:NPR], CS[:, :, NPR - 1:NPR].to_broadcast([P, 4, NPR - nf * WC])), ev("exp_in"))
            until("kk_sq")
            s.do(dve.tensor_scalar(E2, E2, 1e-12, None, ALU.max))
            s.do(dve.reciprocal(E2, E2))
            s.do(mul(KK, KK, E2))
            s.do(mul(E1, XR, v4("rwkv_r_k")))
            s.do(mul(E1, E1, K2), ev("bonus_in"))
            s.do(mul(BTF, KK, AS))
            cols = slice(NPR, NT)
            s.mark(dve.tensor_scalar(SMP[:, 0], KK[:, :, cols], -1.0, None, ALU.mult), dve_step)
            s.mark(dve.tensor_copy(SMP[:, 2], BTF[:, :, cols]), dve_step)
            s.mark(dve.tensor_copy(SMP[:, 3], K2[:, :, cols]), dve_step)
            s.mark(dve.tensor_copy(SMP[:, 4], XR[:, :, cols]), dve_step)
            dve.wait_ge(ev("exps"), 6)
            s.do(dve.tensor_copy(SMP[:, 5], XV[:, :, cols]), ev("smp_cols"))
            for m in range(4):
                b = V.take()
                s.do(mul(BON[:, m, :], b[:, 0:NT], XV[:, m, :]), v_free)
            pc_ = slice(0, NPR)
            s.do(mul(RTF[:, :, pc_], RTF[:, :, pc_], XR[:, :, pc_]))
            s.do(dve.scalar_tensor_tensor(ATF[:, :, pc_], ATF[:, :, pc_], -1.0, KK[:, :, pc_], ALU.mult, ALU.mult))
            s.do(mul(BLF[:, :, pc_], BTF[:, :, pc_], KLF[:, :, pc_]))
            s.do(mul(KLF[:, :, pc_], K2[:, :, pc_], KLF[:, :, pc_]))
            s.do(mul(BTF[:, :, pc_], BTF[:, :, pc_], KTF[:, :, pc_]))
            s.do(mul(KTF[:, :, pc_], K2[:, :, pc_], KTF[:, :, pc_]), ev("wkv_in"))
            dve.wait_ge(ev("srow2_out"), 16)
            s.do(dve.memset(ST[:, 0], 0.0), ev("state0"))
            n_st = 0
            for tt, (c0, r) in enumerate(PT):
                for dst in (ATK, BLK, KLK, VTK):
                    empty(dst[:r, :], 512, r)

                def heads(b, n):
                    return b[:n, 0:4 * n].rearrange("p (h x) -> p h x", h=4)

                def mk(name):
                    return bc(cst(name)[:r, 0:r], [r, 4, r], 1)

                for par in range(2):
                    m_ = lambda v: v[:r, par, :, 0:r]
                    b = V.take()
                    s.do(mul(m_(NTM), heads(b, r), mk("strictT")), v_free)
                    b = V.take()
                    s.do(mul(m_(TM_), heads(b, r), mk("m2N")), v_free)
                    for dst, name in ((AKT, "strictT"), (RBT, "inclT"), (RKT, "inclT")):
                        b = V.take()
                        s.do(mul(m_(dst), heads(b, r), mk(name)), v_free)
                    s.do(add(m_(TM_), m_(TM_), mk("ident")))
                    s.do(mul(m_(TTM), m_(NTM), mk("m2T")))
                    s.do(add(m_(TTM), m_(TTM), mk("ident")), ev("t_init"))
                for lev in range(4):
                    for par in range(2):
                        b = V.take()
                        s.do(mul(XX[:r, par, :, 0:r], heads(b, r), mk(f"off{2 << lev}")), v_free)
                    for par in range(2):
                        if lev < 3:
                            b = V.take()
                            s.do(add(TM_[:r, par, :, 0:r], TM_[:r, par, :, 0:r], heads(b, r)), v_free)
                        b = V.take()
                        s.do(add(TTM[:r, par, :, 0:r], TTM[:r, par, :, 0:r], heads(b, r)), v_free)
                empty(AK[:r, :], 512, r)
                empty(TA[:r, :], 512, r)
                empty(TV[:r, :], 512, r)
                b = V.take()
                s.do(add(RE[:, :, 0:r], RTF[:, :, c0:c0 + r], b[:, 0:4 * r].rearrange("p (h x) -> p h x", h=4)), v_free)
                nch = max(1, r // WC)
                for c in range(nch):
                    s.do(mul(GTM[:, c], bc(cst("id64"), [P, 4, WD], 1), bc(PL[:, :, 4 * tt + c], [P, 4, WD], 2)))
                    b = V.take()
                    s.do(dve.tensor_copy(CCM[:, c], b[:, 256:512].rearrange("p (h x) -> p h x", h=4)))
                    s.do(add(GTM[:, c], GTM[:, c], b[:, 0:256].rearrange("p (h x) -> p h x", h=4)), v_free)
                for c in range(nch):
                    b = V.take()
                    s.do(add(ST[:, (n_st + 1) % 2], b[:, 0:256].rearrange("p (h x) -> p h x", h=4), CCM[:, c]), v_free)
                    n_st += 1
            b = V.take()
            dve.wait_ge(ev("sys_ready"), 2)
            s.do(dve.tensor_copy(SWO[0:WD], b[0:WD, :].rearrange("p (h x) -> p h x", h=WH)), v_free)
            b = V.take()
            s.do(dve.tensor_copy(YW[:, :, NPR:NT], b[:, 0:4 * NB].rearrange("p (m b) -> p m b", m=4)), v_free)
            s.do(mul(MSQ, QA, QA), ev("qa_sq"))
            until("yw")
            centre(YW, OSQ1, WD)
            until("qa_var")
            s.do(mul(MSQ[:, 0:2], CKV, CKV), ev("kv_sq"))
            s.do(dve.reciprocal(MSD[:, 0], MSD[:, 0]))
            for m in range(3):
                s.do(dve.scalar_tensor_tensor(QAN[:, m, :], QA[:, m, :], vec("mla_q_norm", m), MSD[:, 0], ALU.mult, ALU.mult), ev("qan_ready") if m == 2 else None)
            until("kv_var")
            s.do(dve.reciprocal(MSD[:, 1], MSD[:, 1]))
            for m in range(2):
                s.do(dve.scalar_tensor_tensor(CNF[:, m, :], CKV[:, m, :], vec("mla_kv_norm", m), MSD[:, 1], ALU.mult, ALU.mult), ev("cnf_ready") if m == 1 else None)
            b = V.take()
            s.do(mul(RT2, b[:, 0:NT], cst("sinr")), v_free)
            s.do(mul(RT1, KRF, cst("cosr")))
            s.do(add(KRR, RT1, RT2), ev("krr_ready"))
            for q in range(4):
                b = V.take()
                s.do(dve.tensor_copy(WUKT[0:64, 2 * q:2 * q + 2, :], b[0:64, :].rearrange("p (h c) -> p h c", h=2)), v_free)
            scale(YW, OSD1, "rwkv_gn_g", "rwkv_gn_b", YW, "hn_var1")
            s.do(add(YW, YW, BON))
            s.do(mul(MIXR1, YW, GG), ev("mix_ready"))
            dve.wait_ge(ev("wkv_out"), 16 * 2)
            s.do(dve.memset(QLP[0:96], 0.0))
            ro = slice(64, 96)
            for h in range(MH):
                b = V.take()
                s.do(mul(RT2[ro], b[ro, 0:NT], cst("sinr")[ro]))
                s.do(mul(RT1[ro], Q96[ro, h, :], cst("cosr")[ro]))
                s.do(add(Q96[ro, h, :], RT1[ro], RT2[ro]), v_free)
            s.do(dve.tensor_copy(K96[ro], bc(KRR[ro], [32, MH, NT], 1)), ev("k96_rope"))
            for t, (c0, r) in enumerate(TT):
                empty(VM[:r, t, :], 512, r)
            for t, (c0, r) in enumerate(TT):
                empty(CT9[:r, t, :], 288, r)
            empty(CS8[0:NB, :], 288, NB)
            b = V.take()
            s.do(dve.tensor_copy(C8T[0:96], b[0:96, 0:3 * NB].rearrange("p (k b) -> p k b", k=3)), v_free)
            b = V.take()
            s.do(dve.tensor_copy(QLF[0:96, 0:2, :], b[0:96, 0:128].rearrange("p (k f) -> p k f", k=2)))
            s.do(dve.tensor_copy(QLF[0:64, 2, :], b[0:64, 128:192]), v_free)
            s.do(dve.tensor_copy(QLF[ro, 2, :].rearrange("p (b h) -> p b h", b=NB), Q96[ro, :, NPR:NT].rearrange("p h b -> p b h")))
            for sm in range(NB):
                s.do(dve.tensor_copy(QLP[0:96, sm, :, 8 * sm:8 * sm + 8], QLF[0:96, :, 8 * sm:8 * sm + 8]), ev("qlp_ready") if sm == NB - 1 else None)

            def take_scores(h):
                for t, (c0, r) in enumerate(PT):
                    b = V.take()
                    if c0:
                        s.do(dve.tensor_scalar(SCM[:r, h % 2, t, 0:c0], b[:r, 0:c0], SCALE, None, ALU.mult))
                    s.do(dve.scalar_tensor_tensor(SCM[:r, h % 2, t, c0:c0 + r], b[:r, c0:c0 + r], SCALE, cst("causal")[:r, 0:r], ALU.mult, ALU.add), v_free)
                    s.do(dve.tensor_reduce(STAT[:r, h % 2, t, 0:1], SCM[:r, h % 2, t, 0:c0 + r], AX.X, ALU.max, negate=True), ev("s_ready"))

            take_scores(0)
            for h in range(MH):
                for t, (c0, r) in enumerate(PT):
                    dve.wait_ge(ev("p_exp"), 3 * h + t + 1)
                    st = STAT[:r, h % 2, t, :]
                    s.do(dve.reciprocal(st[:, 2:3], st[:, 1:2]))
                    p = SCM[:r, h % 2, t, 0:c0 + r]
                    s.do(dve.tensor_scalar(p, p, st[:, 2:3], None, ALU.mult), ev("p_ready") if t == 2 else None)
                if h < MH - 1:
                    take_scores(h + 1)
                for j, (j0, rj) in enumerate(PT):
                    b = V.take()
                    s.do(dve.tensor_copy(PTS[:rj, j, j0:NPR], b[:rj, j0:NPR]), v_free)
                for half in range(2):
                    b = V.take()
                    o = SCS[0:64, 512 * half:512 * half + 512]
                    s.do(dve.tensor_copy(o, b[0:64, :]) if h == 0 else add(o, o, b[0:64, :]), v_free)
            b = V.take()
            s.do(add(SCS[0:64, PAST:PAST + NB], b[0:64, 0:NB], cst("curmask")[0:64, :]), v_free)
            s.do(dve.tensor_reduce(STS[0:64, 0:1], SCS[0:64, :], AX.X, ALU.max, negate=True))
            s.do(dve.tensor_scalar(STS[0:64, 0:1], STS[0:64, 0:1], SCALE, None, ALU.mult), ev("ss_ready"))
            dve.wait_ge(ev("ps_exp"), 1)
            s.do(dve.reciprocal(STS[0:64, 2:3], STS[0:64, 1:2]))
            s.do(dve.tensor_scalar(SCS[0:64, :], SCS[0:64, :], STS[0:64, 2:3], None, ALU.mult), ev("ps_ready"))
            b = V.take()
            s.do(dve.tensor_copy(P8, b[:, :].rearrange("p (g f) -> p g f", g=NPG)), v_free)
            b = V.take()
            s.do(dve.tensor_copy(PC[0:NB, :], b[0:NB, 0:64]), v_free)
            for q in range(NB // 2):
                b = V.take()
                s.do(dve.tensor_copy(O8[0:MH, 2 * q:2 * q + 2, :], b[0:MH, :].rearrange("p (s c) -> p s c", s=2)), v_free)
            b = V.take()
            s.do(dve.tensor_copy(OLT, b[:, 0:128].rearrange("p (k f) -> p k f", k=2)), v_free)
            b = V.take()
            s.do(dve.tensor_copy(MIXS1[:, :, NPR:NT], b[:, 0:4 * NB].rearrange("p (m b) -> p m b", m=4)))
            s.do(dve.tensor_copy(STS[:, 3:4], b[:, 0:1]), v_free)
            s.do(dve.tensor_copy(STS[:, 3:4], MIXS1[:, 0, NPR:NPR + 1]), ev("mix_ready"))
            out_and_moe(1)
            for h in range(2):
                for t, (c0, r) in enumerate(TT):
                    empty(YOUT[:r, t, 512 * h:512 * h + 512], 512, r)

        def odd_act(act, A, s, empty, std, moe):
            for m in range(RT_N):
                empty(PR[:, m, :], NT)
            for m in range(3):
                empty(QA[:, m, :], NT)
            for m in range(2):
                empty(CKV[:, m, :], NT)
            empty(KRF, NT)
            act.wait_ge(ev("xm_ready"), RT_N)
            act.activation(TW[0:LORA, :], XM[0:LORA, 12, :], ACT.Tanh).then_inc(ev("lora_in"), 1)
            act.activation(GX, XM[:, 13, :], ACT.Sigmoid).then_inc(ev("lora_in"), 1)
            for m in range(4):
                empty(SW[:, m, :], NT, ACT.Sigmoid, bias=vec("rwkv_w0", m))
            for m in range(4):
                empty(AS[:, m, :], NT, ACT.Sigmoid, bias=vec("rwkv_a0", m))
            for m in range(4):
                empty(GG[:, m, :], NT)
            for m in range(4):
                empty(E2[:, m, :], NT, ACT.Sqrt)
            act.wait_ge(ev("exp_in"), 1)
            act.activation(ATF[:, :, 0:NPR], ATF[:, :, 0:NPR], ACT.Exp, scale=-DECAY).then_inc(ev("exps"), 1)
            act.activation(KLF[:, :, 0:NPR], KLF[:, :, 0:NPR], ACT.Exp, scale=DECAY).then_inc(ev("exps"), 1)
            act.activation(RTF[:, :, 0:NPR], CS[:, :, 0:NPR], ACT.Exp, scale=-DECAY).then_inc(ev("exps"), 1)
            act.activation(KTF[:, :, 0:NPR], CS[:, :, 0:NPR], ACT.Exp, scale=DECAY).then_inc(ev("exps"), 1)
            act.activation(PL[:, :, 0:8], CS[:, :, WC - 1:8 * WC:WC], ACT.Exp, scale=-DECAY)
            act.activation(PL[:, :, 8], CS[:, :, NPR - 1], ACT.Exp, scale=-DECAY).then_inc(ev("exps"), 1)
            act.activation(SMP[:, 1], SW[:, :, NPR:NT], ACT.Exp, scale=-DECAY).then_inc(ev("exps"), 1)
            act.wait_ge(ev("stores"), 16 * 8)
            for q in range(6):
                empty(SROW2[0:NB, 512 * q:512 * q + 512], 512, rows=NB)
            for tt, (c0, r) in enumerate(PT):
                b = A.take()
                act.activation(YW[:, :, c0:c0 + r], b[:, 0:4 * r].rearrange("p (h x) -> p h x", h=4), ACT.Copy).then_inc(a_free, 1)
            empty(MSD[:, 0, :], NT, ACT.Sqrt, scale=1.0 / QL, bias=eps[1e-6])
            std(OSD1, WD, 64e-5, 4)
            empty(MSD[:, 1, :], NT, ACT.Sqrt, scale=1.0 / KVL, bias=eps[1e-6])
            for h in range(MH):
                empty(Q96[0:96, h, :], NT, rows=96)
            for h in range(MH):
                empty(K96[0:64, h, :], NT, rows=64)

            def exps(h):
                for t, (c0, r) in enumerate(PT):
                    act.wait_ge(ev("s_ready"), 3 * h + t + 1)
                    p = SCM[:r, h % 2, t, 0:c0 + r]
                    act.activation(p, p, ACT.Exp, bias=STAT[:r, h % 2, t, 0:1], accum_out=STAT[:r, h % 2, t, 1:2]).then_inc(ev("p_exp"), 1)

            exps(0)
            for h in range(MH):
                if h < MH - 1:
                    exps(h + 1)
                for half in range(2):
                    if h:
                        act.wait_ge(*kt_read[h - 1, half])
                    for k in range(3):
                        empty(KT3[half][k][0:96, :], 512, rows=96)
                b = A.take()
                o = 64 * (h % 2)
                act.activation(MIXS1[o:o + 64, h // 2, 0:NPR], b[o:o + 64, 0:NPR], ACT.Copy).then_inc(a_free, 1)
            act.wait_ge(ev("ss_ready"), 1)
            act.activation(SCS[0:64, :], SCS[0:64, :], ACT.Exp, bias=STS[0:64, 0:1], scale=SCALE, accum_out=STS[0:64, 1:2]).then_inc(ev("ps_exp"), 1)
            moe(1)

        def odd_pool(pool, s):
            def sum_start(l):
                pool.wait_ge(ev("ln_done"), KD * (2 * l + 1))
                pool.tensor_scalar(RES[:, :, :], XT[:, :, :], ALPHA, None, ALU.mult).then_inc(ev("sum_start"), 1)

            def row_sums(dst, sem=None):
                w = WD // 2
                while w > 1:
                    s.do(pool.tensor_tensor(TS[:, :, 0:w], TS[:, :, 0:w], TS[:, :, w:2 * w], ALU.add))
                    w //= 2
                s.do(pool.tensor_tensor(dst, TS[:, :, 0], TS[:, :, 1], ALU.add), sem)

            pool.wait_ge(*mark["out0"])
            for dst, src in od_loads:
                pool.dma_start(dst, src).then_inc(ev("od_in"), 16)
            sum_start(0)
            pool.wait_ge(ev("ln_done"), KD * 2)
            pool.dma_start(WKS, a["state_wkv"][0].rearrange("b h (two i) j -> (b h two) i j", two=2)).then_inc(ev("smp2_in"), 16)
            pool.wait_ge(*mark["srow2"])
            pool.dma_start(srow2_dram, SROW2[0:NB, :]).then_inc(ev("srow2_out"), 16)
            pool.wait_ge(ev("srow2_out"), 16)
            for q in range(5):
                for ih in range(2):
                    pool.dma_start(SV5[ih:P:2, q, :], srow2_dram[:, 512 * q:512 * q + 512].rearrange("b (h d) -> b h d", d=WD)).then_inc(ev("smp2_in"), 16)
            pool.dma_start(SVV, srow2_dram[:, 2560:3072].rearrange("b (x i) -> b x i", i=32)).then_inc(ev("smp2_in"), 16)
            pool.wait_ge(ev("wkv_in"), 1)
            pool.wait_ge(ev("smp2_in"), 16 * 12)
            sh = [P, 16, WD]
            q_ = [bc(SV5[:, q, :], sh, 1) for q in range(5)]
            for half in range(2):
                hs = slice(16 * half, 16 * half + 16)
                st, tt = WKS[:, hs, :], pool.tensor_tensor
                s.do(tt(TS, st, q_[0], ALU.mult))
                row_sums(SAS[:, hs])
                s.do(tt(st, st, q_[1], ALU.mult))
                s.do(tt(TS, bc(SAS[:, hs], sh, 2), q_[2], ALU.mult))
                s.do(tt(st, st, TS, ALU.add))
                s.do(tt(TS, bc(SVV[:, hs], sh, 2), q_[3], ALU.mult))
                s.do(tt(st, st, TS, ALU.add), ev("wks_ready"))
                s.do(tt(TS, st, q_[4], ALU.mult))
                row_sums(SYS[:, hs], ev("sys_ready"))
            pool.dma_start(yrow_dram.rearrange("b (x i) -> b x i", i=32), SYS).then_inc(ev("yrow_out"), 16)
            pool.wait_ge(ev("yrow_out"), 16)
            pool.dma_start(YR8[0:NB, :], yrow_dram).then_inc(ev("yr8_in"), 16)
            pool.wait_ge(*mark["qlat"])
            pool.wait_ge(ev("wkv_out"), 16 * 2)
            for sm in range(NB):
                for pg in range(NPG):
                    i = NPG * sm + pg
                    page = pool.value_load(PTAB[0:1, i:i + 1], min_val=0, max_val=a["cache_krope"].shape[0] - 1)
                    pool.dma_start(CK[:, sm, pg, 256:288], a["cache_krope"][bass.ds(page, 1), 0].rearrange("o p c -> p (o c)")).then_inc(ev(f"cache_krope_in{sm}"), 16)
            sum_start(1)

        def odd_sp(sp, store, fill, over_capacity_sp):
            for n in range(S_OD + NSLOT, S_ODO):
                fill(n)
            sp.wait_ge(*mark["sho"])
            store(outs[10][0], SHO[0:1, :])
            store(outs[11][0], SHO[1:NB + 1, :])
            sp.wait_ge(ev("wks_ready"), 2)
            store(outs[9][0].rearrange("b h (two i) j -> (b h two) i j", two=2), WKS, "wkv_out")
            sp.wait_ge(*mark["swo"])
            store(outs[8][0, 0].rearrange("h i j -> i h j"), SWO[0:WD], "wkv_out")
            for n in range(S_ODO, S_ODO + 3):
                fill(n)
            sp.wait_ge(*mark["ct9"])
            for t, (c0, r) in enumerate(PT):
                store(outs[12][0, 0, c0:c0 + r, :], CT9[:r, t, 0:256])
                store(outs[14][0, 0, c0:c0 + r, :], CT9[:r, t, 256:288])
            sp.wait_ge(*mark["cs8"])
            store(outs[13].rearrange("b l s c -> (b l s) c"), CS8[0:NB, 0:256])
            store(outs[15].rearrange("b l s c -> (b l s) c"), CS8[0:NB, 256:288])
            sp.wait_ge(*mark["qlat"])
            sp.wait_ge(ev("wkv_out"), 16 * 2)
            for sm in range(NB):
                for pg in range(NPG):
                    i = NPG * sm + pg
                    page = sp.value_load(PTAB[0:1, i:i + 1], min_val=0, max_val=a["cache_kv"].shape[0] - 1)
                    sp.dma_start(CK[:, sm, pg, 0:256], a["cache_kv"][bass.ds(page, 1), 0].rearrange("o p c -> p (o c)")).then_inc(ev(f"cache_kv_in{sm}"), 16)
            sp.wait_ge(*mark["pc"])
            for n in range(S_ODO + 3, S_MOE[1] + 3 * NE):
                fill(n)
            over_capacity_sp(1)
            sp.wait_ge(*mark["y_rows"])
            store(outs[0][0, 0:P - NM, :], YOUT[NM:P, 0, :])
            store(outs[0][0, P - NM:2 * P - NM, :], YOUT[:, 1, :])
            store(outs[0][0, 2 * P - NM:SEQ, :], YOUT[0:NM, 2, :])
            store(outs[1].rearrange("b s d -> (b s) d"), YOUT[NM:NM + NB, 2, :])

        @block.tensor
        def _(pe):
            V, A = Ring(pe, VB, v_full, v_free), Ring(pe, AB, a_full, a_free)

            def close(ring, ins, name=None):
                ins.then_inc(ring.full, 1)
                if name:
                    mark[name] = (ring.free, ring.n)

            def until(name):
                pe.wait_ge(*mark[name])

            def slot(n):
                pe.wait_ge(w_in[n % NSLOT], landed(n))

            def used(n, ring):
                slot_done[n] = (ring.full, ring.n)

            def to_fm(src, name, r_of=TT, tiles=4):
                for m in range(tiles):
                    b = V.claim()
                    for t, (c0, r) in enumerate(r_of):
                        ins = pe.transpose(b[:, c0:c0 + r], src[:r, t, P * m:P * m + P], ident[:r, :r])
                    close(V, ins, name)

            def project(n, m2, width, src, kt, ring, name, ready=None):
                b = ring.claim()
                w = slot_view(SLOT, n, kt, width)
                for k in range(kt):
                    if ready:
                        pe.wait_ge(ready[0], ready[1] + k)
                    ins = pe.matmul(b[:, 0:NT], w[:, k, P * m2:P * m2 + P], src[:, k, :], start=(k == 0), stop=(k == kt - 1))
                close(ring, ins, name)

            pe.wait_ge(ev("x_in"), 16 * len(x_loads))
            to_fm(XTOK, "x_fm", tiles=KD)
            until("x_fm")
            for j in range(8):
                if j == 2:
                    pe.wait_ge(ev("vec_in"), 16 * len(vec_loads))
                    b = V.claim()
                    close(V, pe.transpose(b[:, 0:NVEC], VROW[:NVEC, :], ident[:NVEC, :NVEC]), "vec_cols")
                    pe.wait_ge(ev("s5_in"), 16 * len(s5_loads))
                    b = V.claim()
                    for ri in range(2):
                        for t in range(2):
                            ins = pe.transpose(b[:, P * (2 * ri + t):P * (2 * ri + t) + P], CN[:, ri, t, :], ident)
                    close(V, ins, "c_turned")
                    until("proj1")
                    for t, (c0, r) in enumerate(TT):
                        b = V.claim()
                        for m in range(4):
                            ins = pe.transpose(b[:r, P * m:P * m + P], UF[:, m, c0:c0 + r], ident)
                        close(V, ins, "u_tok")
                if j == 3:
                    pe.wait_ge(ev("s5_rows"), 1)
                    b = V.claim()
                    for j2 in range(4):
                        ins = pe.transpose(b[:, GP * j2:GP * j2 + GP], ROWS[0:GP, 11 + j2, :], ident[:GP, :GP])
                    close(V, ins, "s5_vecs")
                slot(S_EV + j)
                for m2 in range(2):
                    project(S_EV + j, m2, 256, XT, KD, A, f"proj{j}")
                used(S_EV + j, A)
            until("proj3")
            pe.wait_ge(ev("consts_in"), 16)
            for m in range(4):
                b = V.claim()
                close(V, pe.matmul(b[:, 0:NT], cst("perm64"), QK[:, m, :], start=True, stop=True), f"rope{m}")
            pe.wait_ge(ev("bi_ready"), 1)
            for j in range(2):
                for g in range(0, GP, 4):
                    b = A.claim()
                    for i in range(4):
                        ins = pe.transpose(b[:, P * i:P * i + P], BI[:, j, g + i, :, :].rearrange("p t c -> p (t c)"), ident)
                    close(A, ins, "bit")
            pe.wait_ge(ev("cp_ready"), 1)
            for q in range(8):
                b = V.claim()
                for i in range(4):
                    g = 8 * (q // 2) + 2 * i + q % 2
                    lo = SP_N * (g % 2)
                    for j in range(2):
                        ins = pe.matmul(b[0:SC_N, P * i:P * i + P], BB[lo:lo + SP_N, j, g // 2, :],
                                        CP[lo:lo + SP_N, j, g // 2, 0:CL, :].rearrange("p l c -> p (l c)"),
                                        start=(j == 0), stop=(j == 1))
                close(V, ins, "kl")
            for q in range(4):
                pe.wait_ge(ev("ucq_ready"), q + 1)
                b = V.claim()
                for i in range(8):
                    ins = pe.transpose(b[:, UCOL * i:UCOL * i + UCOL], UCQ[:UCOL, q % 2, i, :, :].rearrange("p t c -> p (t c)"), ident[:UCOL, :UCOL])
                close(V, ins, f"ug{q}")
            pe.wait_ge(ev("h0_in"), 32)
            b = V.claim()
            for j in range(2):
                ins = pe.transpose(b[:, P * j:P * j + P], H0R[:, j, :], ident)
            close(V, ins, "h0")
            until("bit")
            until("ug3")
            for j in range(2):
                for h in range(2):
                    b = V.claim()
                    for i in range(8):
                        g = 8 * h + i
                        for two in range(2):
                            lo = SP_N * two
                            ins = pe.matmul(b[lo:lo + SP_N, UCOL * i:UCOL * i + UCOL], BIT[:, j, g, lo:lo + SP_N],
                                            UG[:, 2 * g + two, :], start=True, stop=True)
                    close(V, ins, "inj")
            pe.wait_ge(ev("k_ready"), 16 * CL)

            def y_toeplitz(q, b):
                for i in range(4):
                    g = 8 * (q // 2) + 2 * i + q % 2
                    pe.matmul(b[0:HCOL, P * i:P * i + P], UG[:, g, 0:HCOL], KT_[:, g, :], start=(i == 0), stop=False, skip_group_check=True)

            held = [A.claim() for q in range(4)]
            for q in range(4):
                y_toeplitz(q, held[q])
            pe.wait_ge(ev("hs_ready"), 1)
            for q in range(8):
                if q < 4:
                    b = held[q]
                else:
                    b = A.claim()
                    y_toeplitz(q, b)
                for i in range(4):
                    g = 8 * (q // 2) + 2 * i + q % 2
                    lo = SP_N * (g % 2)
                    for j in range(2):
                        ins = pe.matmul(b[0:HCOL, P * i:P * i + P], HS[lo:lo + SP_N, j, g // 2, :], CP[lo:lo + SP_N, j, g // 2, 1:CL + 1, :].rearrange("p l c -> p (l c)"),
                                        start=False, stop=(j == 1), skip_group_check=True)
                ins.then_inc(a_full, 1)
            mark["y_chunk"] = (a_free, A.n)
            b = V.claim()
            for j in range(2):
                pe.transpose(b[:, P * j:P * j + P], HF[:, j].rearrange("p b g -> p (b g)"), ident)
            for j in range(2):
                ins = pe.transpose(b[0:GP, P * (2 + j):P * (3 + j)], HFP[:, j, :], ident)
            close(V, ins, "h_rows")
            until("rope3")
            until("proj5")
            for h in range(2):
                b = V.claim()
                for m in range(4):
                    src = QK if h == 0 else VF
                    ins = pe.transpose(b[:NB, P * m:P * m + P], src[:, m, NPR:NT], ident)
                close(V, ins, "srow")
            for t, (c0, r) in enumerate(TT):
                b = V.claim()
                for m in range(2):
                    ins = pe.transpose(b[:r, P * m:P * m + P], QK[:, 2 + m, c0:c0 + r], ident)
                close(V, ins, "k_tok")
            for t, (c0, r) in enumerate(TT):
                b = V.claim()
                for m in range(4):
                    ins = pe.transpose(b[:r, P * m:P * m + P], VF[:, m, c0:c0 + r], ident)
                close(V, ins, "v_tok")
            for h in range(RH):
                lo, m = 64 * (h % 2), h // 2
                for t, (c0, r) in enumerate(PT):
                    b = V.claim()
                    close(V, pe.matmul(b[:r, 0:NPR - c0], QK[lo:lo + 64, 2 + m, c0:c0 + r], QK[lo:lo + 64, m, c0:NPR],
                                       start=True, stop=True), f"scr{h}")
            pe.wait_ge(ev("ytok_in"), 48)
            to_fm(YTOK, "y_fm")
            slot(S_GLU)
            pe.wait_ge(ev("z_ready"), 1)
            for m in range(4):
                project(S_GLU, m, 512, ZF, 4, A, "glu")
            used(S_GLU, A)
            for h in range(RH):
                until(f"scr{h}")
                b = A.claim()
                for t, (c0, r) in enumerate(PT):
                    ins = pe.matmul(b[:, c0:NPR], VTOK[:r, t, P * h:P * h + P], SCR[:r, h, t, c0:NPR], start=(t == 0), stop=(t == 2))
                close(A, ins, "o_fm")
            pe.wait_ge(ev("kdec_ready"), 1)
            b = V.claim()
            for h in range(RH):
                for t, (c0, r) in enumerate(PT):
                    ins = pe.matmul(b[0:RDK, RDV * h:RDV * h + RDV], KDT[:r, t, RDK * h:RDK * h + RDK], VTOK[:r, t, RDV * h:RDV * h + RDV],
                                    start=(t == 0), stop=(t == 2))
            close(V, ins, "ret_state")
            pe.wait_ge(ev("parto_ready"), 1)
            b = V.claim()
            close(V, pe.matmul(b[:, 0:RH * NB], PARTO, cst("selbh"), start=True, stop=True), "o_smp")

            def fm_sums(src, kmat, tiles, together, name, ready, ring=V):
                if ready:
                    pe.wait_ge(ev(ready), fm_sums.n.setdefault(ready, 0) + 1)
                    fm_sums.n[ready] += 1
                for m in range(tiles):
                    if m == 0 or not together:
                        b = ring.claim()
                    ins = pe.matmul(b[:, 0:NT], kmat, src[:, m, :], start=(m == 0 or not together), stop=(m == tiles - 1 or not together))
                    if m == tiles - 1 or not together:
                        close(ring, ins, name)
            fm_sums.n = {}

            def ln_sums(c, free0):
                b = V.claim()
                for m in range(KD):
                    pe.wait_ge(v_free, free0 + m + 1)
                    ins = pe.matmul(b[:, 0:NT], cst("ones"), RES[:, m, :], start=(m == 0), stop=(m == KD - 1))
                close(V, ins, f"ln_mean{c}")
                b = A.claim()
                for m in range(KD):
                    pe.wait_ge(ev("ln_sq"), KD * c + m + 1)
                    ins = pe.matmul(b[:, 0:NT], cst("ones"), LSQ[:, m, :], start=(m == 0), stop=(m == KD - 1))
                close(A, ins, "ln_var")

            until("o_fm")
            until("o_smp")
            fm_sums(OT, cst("ones"), 4, False, "hn_mean", None)
            fm_sums(OSQ, cst("ones"), 4, False, "hn_var", "hn_sq", A)

            def over_capacity_pe(l):
                pe.wait_ge(ev("over_known"), l + 1)
                over = pe.value_load(OVER[0:1, l:l + 1], min_val=0, max_val=1)
                with pe.If(over > 0):
                    until(f"moe_out{l}")
                    pe.wait_ge(ev(f"x_comb{l}"), 1)
                    for t, (c0, r) in enumerate(TT):
                        ins = pe.transpose(banks[7][0:NE, c0:c0 + r], XC[:r, t, :], ident[:r, :r])
                    ins.then_inc(ev(f"x_full{l}"), 1)
                    pe.wait_ge(ev(f"x_comb{l}"), 2)
                    with pe.Fori(0, NE) as e:
                        pe.wait_ge(ev(f"x_w{l}"), e * 48 + 48)
                        pe.wait_ge(ev(f"x_row{l}"), e + 1)
                        for f in range(2):
                            for bank, j in ((4, 0), (0, 1)):
                                w = XW[:, j, :].rearrange("p (k c) -> p k c", k=KD)
                                for k in range(KD):
                                    pe.matmul(banks[bank + f][:, 0:NT], w[:, k, P * f:P * f + P], XT[:, k, :], start=(k == 0), stop=(k == KD - 1))
                        pe.matmul(banks[6][:, 0:NT], cst("ones")[0:NE, :], XROW[0:NE, :], start=True, stop=True).then_inc(ev(f"x_full{l}"), 1)
                        pe.wait_ge(ev(f"x_h{l}"), e * 2 + 2)
                        w = XW[:, 2, :].rearrange("p (k c) -> p k c", k=2)
                        for m in range(KD):
                            for f in range(2):
                                ins = pe.matmul(banks[m][:, 0:NT], w[:, f, P * m:P * m + P], XHB[:, f, :], start=(f == 0), stop=(f == 1))
                        ins.then_inc(ev(f"x_sums{l}"), 1)
                    pe.wait_ge(ev(f"x_dve{l}"), 2 * NE + 2)

            def out_and_moe(l, s_out):
                mixr, mixs = ((MIXR, MIXS), (MIXR1, MIXS1))[l]
                out0 = V.n
                halves = ((mixs, 4), (mixr, 0)) if l == 0 else ((mixr, 0), (mixs, 4))
                held = []

                def out_half(b, j, m2, which):
                    w = slot_view(SLOT, s_out + j, KD, 256)
                    src, k0 = halves[which]
                    for k in range(4):
                        ins = pe.matmul(b[:, 0:NT], w[:, k0 + k, P * m2:P * m2 + P], src[:, k, :], start=(which == 0 and k == 0), stop=(which == 1 and k == 3))
                    return ins

                pe.wait_ge(ev("mix_ready"), 2 * l + 1)
                for j in range(2):
                    slot(s_out + j)
                    for m2 in range(2):
                        held.append(V.claim())
                        out_half(held[-1], j, m2, 0)
                pe.wait_ge(ev("mix_ready"), 2 * l + 2)
                for j in range(4):
                    if j >= 2:
                        slot(s_out + j)
                    for m2 in range(2):
                        if j < 2:
                            b = held[2 * j + m2]
                        else:
                            b = V.claim()
                            out_half(b, j, m2, 0)
                        out_half(b, j, m2, 1).then_inc(v_full, 1)
                    slot_done[s_out + j] = (v_full, out0 + 2 * j + 2)
                mark[f"out{l}"] = (v_free, V.n)
                ln_sums(2 * l, out0)
                pe.wait_ge(ev("router_in"), 16 * len(router_loads))
                lg = [V.claim() for t in TT]
                for k in range(KD):
                    pe.wait_ge(ev("ln_done"), KD * 2 * l + k + 1)
                    for (c0, r), b in zip(TT, lg):
                        ins = pe.matmul(b[:r, 0:20], XT[:, k, c0:c0 + r], RW[:, l, k, :], start=(k == 0), stop=(k == KD - 1))
                        if k == KD - 1:
                            ins.then_inc(v_full, 1)
                for t, (c0, r) in enumerate(TT):
                    for h in range(2):
                        b = A.claim()
                        for i in range(4):
                            ins = pe.transpose(b[:r, P * i:P * i + P], XT[:, 4 * h + i, c0:c0 + r], ident)
                        close(A, ins, f"x_tok{l}")
                pe.wait_ge(ev("group_ready"), l + 1)
                b = V.claim()
                one = lambda t: RT[:TT[t][1], 0, t, 0:NG]
                for t, (c0, r) in enumerate(TT):
                    for u in range(t):
                        pe.matmul(b[:, NG * t:NG * t + NG], cst("ones"), one(u), start=(u == 0), stop=False)
                    pe.matmul(b[:, NG * t:NG * t + NG], cst("before")[:r, :], one(t), start=(t == 0), stop=True)
                for t, (c0, r) in enumerate(TT):
                    ins = pe.matmul(b[:, 12:16], cst("ones")[:r, :], one(t), start=(t == 0), stop=(t == 2))
                close(V, ins, "places")
                pe.wait_ge(ev("dispatch_ready"), NG * l + 1)
                until(f"x_tok{l}")

                def pack(g):
                    for kh in range(4):
                        b = V.claim()
                        for k2 in range(2):
                            k = 2 * kh + k2
                            for t, (c0, r) in enumerate(TT):
                                sel = DSP[:r, t, g, :] if isinstance(g, int) else DSP[:r, t, bass.ds(g, 1), :].rearrange("p a c -> p (a c)")
                                ins = pe.matmul(b[:, CAP * k2:CAP * k2 + CAP], XTM[:r, t, P * k:P * k + P], sel, start=(t == 0), stop=(t == 2))
                        close(V, ins)

                pack(0)
                for g in range(NG):
                    pe.wait_ge(ev("dispatch_ready"), NG * l + g + 1)
                    b = A.claim()
                    for t, (c0, r) in enumerate(TT):
                        ins = pe.transpose(b[:, c0:c0 + r], DSP[:r, t, g, :], ident[:r, :r])
                    close(A, ins, f"dspt{l}")
                s0 = S_MOE[l]

                def wait_fill(e, what, i):
                    n = s0 + 3 * e + what
                    pe.wait_ge(w_in[n % NSLOT], landed(n) + 16 * (3 * EG // NSLOT) * i)

                def gate_up(e, i):
                    wait_fill(e, 0, i)
                    wait_fill(e, 1, i)
                    n = s0 + 3 * e
                    for ring, w in ((A, slot_view(SLOT, n, KD, DE)), (V, slot_view(SLOT, n + 1, KD, DE))):
                        b = ring.claim()
                        for f in range(2):
                            for k in range(KD):
                                ins = pe.matmul(b[:, CAP * f:CAP * f + CAP], w[:, k, P * f:P * f + P], XG[:, k, :], start=(k == 0), stop=(k == KD - 1))
                        close(ring, ins)

                def down(e, i):
                    wait_fill(e, 2, i)
                    pe.wait_ge(v_free, V_UP[e] + i * V_GROUP + mark[f"moe{l}"][0])
                    w = slot_view(SLOT, s0 + 3 * e + 2, 2, D)
                    for h in range(2):
                        b = V.claim()
                        for f in range(2):
                            ins = pe.matmul(b[:, :], HB[:, e % 2, f, :], w[:, f, 512 * h:512 * h + 512], start=(f == 0), stop=(f == 1))
                        close(V, ins)

                def turn(i, last):
                    down(0, i)
                    gate_up(2, i)
                    down(1, i)
                    gate_up(3, i)
                    down(2, i)
                    if not last:
                        pack(i + 1)
                    down(3, i)
                    if not last:
                        pe.wait_ge(v_free, V.n - 2)
                        gate_up(0, i + 1)
                        gate_up(1, i + 1)

                pe.wait_ge(v_free, V.n)
                gate_up(0, 0)
                gate_up(1, 0)
                pe.wait_ge(ev("comb_ready"), l + 1)
                b = V.claim()
                for g in range(NG):
                    for t, (c0, r) in enumerate(TT):
                        ins = pe.matmul(b[:, EG * g:EG * g + EG], DSP[:r, t, g, :], RT[:r, 4, t, 0:EG], start=(t == 0), stop=(t == 2))
                close(V, ins, "weights")
                va, aa = V.n, A.n
                mark[f"moe{l}"] = (va, aa)
                for e in range(NE):
                    g, j = e // EG, e % EG
                    slot_done[s0 + 3 * e] = (a_full, aa + EG * g + A_GATE[j])
                    slot_done[s0 + 3 * e + 1] = (v_full, va + V_GROUP * g + V_UP[j])
                    slot_done[s0 + 3 * e + 2] = (v_full, va + V_GROUP * g + (V_DOWN[j] if e < NE - 1 else 10))

                with pe.Fori(0, NG - 1) as i:
                    V.n, A.n = va + i * V_GROUP, aa + i * EG
                    turn(i, False)
                V.n, A.n = va + V_GROUP * (NG - 1), aa + EG * (NG - 1)
                turn(NG - 1, True)
                assert V.n == va + V_GROUP * (NG - 1) + 10 and A.n == aa + EG * NG - 2
                moe0 = V.n
                pe.wait_ge(v_free, V.n)
                for m in range(KD):
                    b = V.claim()
                    for g in range(NG):
                        ins = pe.matmul(b[:, 0:NT], YG[:, g, P * m:P * m + P], DSPT[:, g, :], start=(g == 0), stop=(g == NG - 1))
                    close(V, ins, f"moe_out{l}")
                over_capacity_pe(l)
                ln_sums(2 * l + 1, moe0)

            out_and_moe(0, S_EVO)
            odd_pe(pe, V, A, close, until, slot, used, to_fm, project, fm_sums, out_and_moe)

        @block.vector
        def _(dve):
            V = Ring(dve, VB, v_full, v_free)
            s = Steps(dve, dve_step)

            def until(name):
                dve.wait_ge(*mark[name])

            def empty(dst, width=None, rows=P):
                b = V.take()
                src = b[:rows, 0:width or int(np.prod(dst.shape[1:]))]
                s.do(dve.tensor_copy(dst, src if len(dst.shape) == 2 else src.rearrange("p (a b) -> p a b", a=dst.shape[1])), v_free)

            def mul(o, x, y):
                return dve.tensor_tensor(o, x, y, ALU.mult)

            def add(o, x, y):
                return dve.tensor_tensor(o, x, y, ALU.add)

            def sub(o, x, y):
                return dve.tensor_tensor(o, x, y, ALU.subtract)

            for k in range(KD):
                empty(XT[:, k, :])
            empty(VC[:, 0:NVEC])
            b = V.take()
            s.do(dve.tensor_copy(CTT.rearrange("p j g c -> p (j g c)"), b[:, 0:512]), v_free)

            dve.wait_ge(ev("s5_in"), 16 * len(s5_loads))
            row = [ROWS[0:GP, i, :] for i in range(15)]
            are, aim, _, t0, t1, t2, t3, sn, cs, mag, t4, abr, abi, fr, fi = row
            dve.wait_ge(ev("dt_ready"), 1)
            dt = bc(row[2][:, 4:6], [GP, 2, SP_N], 2)
            v2 = lambda r: r.rearrange("p (a b) -> p a b", a=2)
            s.do(mul(v2(t0), v2(are), dt), ev("mag_arg"))
            s.do(mul(v2(t1), v2(aim), dt))
            MAGIC = 12582912.0
            s.do(dve.tensor_scalar(t2, t1, 1.0 / (2 * math.pi), None, ALU.mult))
            s.do(dve.tensor_scalar(t2, t2, MAGIC, None, ALU.add))
            s.do(dve.tensor_scalar(t2, t2, -MAGIC, None, ALU.add))
            c1, c2 = 6.28125, 0.0019350051879882812
            for c in (c1, c2, 2 * math.pi - c1 - c2):
                s.do(dve.scalar_tensor_tensor(t1, t2, -c, t1, ALU.mult, ALU.add))
            PI = 3.1415925
            s.do(dve.tensor_scalar(t2, t1, math.pi / 2, None, ALU.add))
            s.do(dve.tensor_scalar(t3, t2, PI, -2 * math.pi, ALU.is_gt, ALU.mult))
            s.do(add(t2, t2, t3))
            s.do(dve.tensor_scalar(t2, t2, PI, -PI, ALU.min, ALU.max))
            s.do(dve.tensor_scalar(t1, t1, PI, -PI, ALU.min, ALU.max), ev("sin_arg"))
            dve.wait_ge(ev("sin_ready"), 3)
            s.do(mul(abr, mag, cs))
            s.do(mul(abi, mag, sn))
            s.do(mul(t0, are, are))
            s.do(mul(t1, aim, aim))
            s.do(add(t0, t0, t1))
            s.do(dve.reciprocal(t4, t0))
            s.do(dve.tensor_scalar(t3, abr, -1.0, None, ALU.add))
            s.do(mul(t0, t3, are))
            s.do(mul(t1, abi, aim))
            s.do(add(t0, t0, t1))
            s.do(mul(fr, t0, t4))
            s.do(mul(t0, abi, are))
            s.do(mul(t1, t3, aim))
            s.do(sub(t0, t0, t1))
            s.do(mul(fi, t0, t4), ev("s5_rows"))
            for t, (c0, r) in enumerate(TT):
                empty(UTOK[:r, t, :], 512, r)
            b = V.take()
            s.do(dve.tensor_copy(SV.rearrange("p j g -> p (j g)"), b[:, 0:4 * GP]), v_free)
            q1, q2 = TD[:, 0].rearrange("p g l c -> p (g l c)"), TD[:, 1].rearrange("p g l c -> p (g l c)")
            s.do(dve.memset(PW[:, 0, 0, :], 1.0))
            s.do(dve.memset(PW[:, 1, 0, :], 0.0))
            s.do(dve.tensor_copy(PW[:, :, 1, :], SV[:, 0:2, :]))

            def cmul(ore, oim, xr, xi, yr, yi, last=None, q1=q1, q2=q2):
                n, sh = int(np.prod(xr.shape[1:])), xr.shape
                def shaped(q):
                    q = q[:, 0:n]
                    if len(sh) == 3:
                        return q.rearrange("p (a b) -> p a b", a=sh[1])
                    return q.rearrange("p (a b c) -> p a b c", a=sh[1], b=sh[2])
                w1, w2 = shaped(q1), shaped(q2)
                s.do(mul(w1, xr, yr))
                s.do(mul(w2, xi, yi))
                s.do(sub(ore, w1, w2))
                s.do(mul(w1, xr, yi))
                s.do(mul(w2, xi, yr))
                s.do(add(oim, w1, w2), last)

            for lo, n in ((1, 1), (1, 2), (1, 4)):
                step = [bc(PW[:, j, n, :], [P, n, GP], 1) for j in range(2)]
                cmul(PW[:, 0, n + 1:2 * n + 1, :], PW[:, 1, n + 1:2 * n + 1, :], PW[:, 0, 1:n + 1, :], PW[:, 1, 1:n + 1, :], *step)
            fb = [bc(SV[:, 2 + j, :], [P, GP, SC_N], 2) for j in range(2)]
            cmul(BB[:, 0], BB[:, 1], BRAW[:, 0], BRAW[:, 1], *fb, ev("bb_ready"))
            sh = [P, GP, CL + 1, SC_N]
            cc = [bc(CTT[:, j], sh, 2) for j in range(2)]
            pw = [bc(PW[:, j].rearrange("p l g -> p g l"), sh, 3) for j in range(2)]
            w1, w2 = TD[:, 0], TD[:, 1]
            s.do(mul(w1, cc[0], pw[0]))
            s.do(mul(w2, cc[1], pw[1]))
            s.do(sub(CP[:, 0], w1, w2))
            s.do(mul(w1, cc[0], pw[1]))
            s.do(mul(w2, cc[1], pw[0]))
            s.do(add(w1, w1, w2))
            s.do(dve.tensor_scalar(CP[:, 1], w1, -1.0, None, ALU.mult), ev("cp_ready"))
            s.do(dve.tensor_copy(PX[:, :, 0, :], PW[:, :, CL, :]))
            n = 1
            while n < HALF:
                m = min(n, HALF - n)
                step = [bc(PX[:, j, n - 1, :], [P, m, GP], 1) for j in range(2)]
                cmul(PX[:, 0, n:n + m, :], PX[:, 1, n:n + m, :], PX[:, 0, 0:m, :], PX[:, 1, 0:m, :], *step)
                n += m
            rt1, rt2 = q1[:, 0:NT], q2[:, 0:NT]
            for m in range(4):
                scale = RDK ** -0.5 if m < 2 else 1.0
                b = V.take()
                s.do(dve.scalar_tensor_tensor(rt2, b[:, 0:NT], scale, cst("sind"), ALU.mult, ALU.mult))
                s.do(dve.scalar_tensor_tensor(rt1, QK[:, m, :], scale, cst("cosd"), ALU.mult, ALU.mult))
                s.do(add(QK[:, m, :], rt1, rt2), v_free)
            dve.wait_ge(ev("u_out"), 48)
            s.do(dve.memset(KT_, 0.0), ev("k_zero"))
            for q in range(8):
                b = V.take()
                g0 = 8 * (q // 2) + q % 2
                s.do(dve.tensor_copy(KL[0:SC_N, g0:g0 + 7:2, :], b[0:SC_N, :].rearrange("p (g f) -> p g f", g=4)), v_free)
            for q in range(4):
                b = V.take()
                s.do(dve.tensor_copy(UG[:, 8 * q:8 * q + 8, :], b[:, 0:8 * UCOL].rearrange("p (g f) -> p g f", g=8)), v_free)
            b = V.take()
            s.do(dve.tensor_copy(HS[:, :, :, NCH:HCOL], b[:, 0:256].rearrange("p (j b g) -> p j g b", j=2, g=GP)), v_free)
            for j in range(2):
                for h in range(2):
                    b = V.take()
                    s.do(dve.tensor_copy(INJ[:, j, 8 * h:8 * h + 8, :], b[:, 0:8 * UCOL].rearrange("p (g f) -> p g f", g=8)), v_free)
            s.do(dve.memset(HS[:, :, :, 0:NCH:HALF], 0.0))
            sh = [P, 2, GP, 2]
            ar, ai = (PW[:, j, CL, :].unsqueeze(1).unsqueeze(3).to_broadcast(sh) for j in range(2))
            q1, q2 = part(M_BB + 512, 256), part(M_BB + 768, 256)
            w1, w2 = (q[:, 0:4 * GP].rearrange("p (j g h) -> p j g h", j=2, h=2) for q in (q1, q2))
            for c in range(HALF):
                h = HS[:, :, :, c:NCH:HALF]
                s.mark(mul(w1, h, ar), dve_step)
                s.do(mul(w2, h, ai))
                s.do(add(w1, w1, INJ[:, :, :, c:NCH:HALF]))
                if c < HALF - 1:
                    nxt = HS[:, :, :, c + 1:NCH:HALF]
                    s.mark(sub(nxt[:, 0], w1[:, 0], w2[:, 1]), dve_step)
                    s.do(add(nxt[:, 1], w1[:, 1], w2[:, 0]))
                else:
                    for k, nxt in enumerate((HS[:, :, :, HALF], HFP)):
                        s.mark(sub(nxt[:, 0], w1[:, 0, :, k], w2[:, 1, :, k]), dve_step)
                        s.do(add(nxt[:, 1], w1[:, 1, :, k], w2[:, 0, :, k]))
            last = HALF - 1
            mid = [HS[:, j, :, HALF] for j in range(2)]
            for dst, px, t1, t2 in (
                    (HS[:, :, :, HALF + 1:NCH], PX[:, :, 0:last, :].rearrange("p j k g -> p j g k"), TX[:, 0], TX[:, 1]),
                    (HFP, PX[:, :, last, :], w1[:, :, :, 0], w2[:, :, :, 0])):
                for j, t in enumerate((t1, t2)):
                    m = mid[j].unsqueeze(1) if len(px.shape) == 3 else mid[j].unsqueeze(1).unsqueeze(3)
                    s.do(mul(t, px, m.to_broadcast(list(px.shape))))
                s.do(add(dst, dst, t1))
                s.mark(sub(dst[:, 0], dst[:, 0], t2[:, 1]), dve_step)
                s.do(add(dst[:, 1], dst[:, 1], t2[:, 0]))
            h0 = [HS[:, j, :, NCH:HCOL].rearrange("p g b -> p b g") for j in range(2)]
            ab = [bc(SV[:, j, :], [P, NB, GP], 1) for j in range(2)]
            cmul(HF[:, 0], HF[:, 1], h0[0], h0[1], *ab, None, q1, q2)
            s.do(add(HF[:, :, :, :], HF[:, :, :, :], INJ[:, :, :, HCOL:UCOL].rearrange("p j g b -> p j b g")), ev("hs_ready"))
            b = V.take()
            s.do(dve.tensor_copy(HROW[:, 0:2, :], b[:, 0:256].rearrange("p (j f) -> p j f", j=2)))
            s.do(dve.tensor_copy(HROW[0:GP, 2:4, :], b[0:GP, 256:512].rearrange("p (j f) -> p j f", j=2)), v_free)
            for h in range(2):
                empty(SROW[:NB, 512 * h:512 * h + 512], 512, NB)
            for t, (c0, r) in enumerate(TT):
                empty(KTOK[:r, t, :], 256, r)
            for t, (c0, r) in enumerate(TT):
                empty(VTOK[:r, t, :], 512, r)
            kd = cst("kdec").rearrange("p (t h) -> p t h", t=3)
            for t, (c0, r) in enumerate(PT):
                ins = mul(KDT[:r, t, :].rearrange("p (h d) -> p h d", h=RH), KTOK[:r, t, :].rearrange("p (h d) -> p h d", h=RH),
                          bc(kd[:r, t, :], [r, RH, RDK], 2))
                s.do(ins, ev("kdec_ready") if t == 2 else None)
            msk = cst("retmask").rearrange("p (h x) -> p h x", h=RH)
            for h in range(RH):
                for t, (c0, r) in enumerate(PT):
                    b = V.take()
                    s.do(mul(SCR[:r, h, t, c0:NPR], b[:r, 0:NPR - c0], msk[:r, h, 0:NPR - c0]), v_free)
            for m in range(4):
                b = V.take()
                s.do(dve.scalar_tensor_tensor(YF[:, m, :], UF[:, m, :], vec("s5_d", m), b[:, 0:NT], ALU.mult, ALU.add), v_free)
            until("glu")
            s.do(mul(MIXS, ZF, YF), ev("mix_ready"))
            dve.wait_ge(ev("smp_in"), 16 * 7)
            s.do(mul(TOUT, bc(KS, [P, 16, RDV], 2), bc(VS, [P, 16, RDV], 1)))
            s.do(dve.scalar_tensor_tensor(RETS, RETS, cst("gam"), TOUT, ALU.mult, ALU.add), ev("rets_ready"))
            s.do(mul(TOUT, RETS, bc(QS, [P, 16, RDV], 2)))
            s.do(dve.tensor_reduce(PARTO, TOUT.rearrange("p d v -> p v d"), AX.X, ALU.add), ev("parto_ready"))
            b = V.take()
            s.do(dve.tensor_copy(RSTO[0:RDK], b[0:RDK, :].rearrange("p (h v) -> p h v", h=RH)), v_free)
            b = V.take()
            s.do(dve.tensor_copy(OT[:, :, NPR:NT], b[:, 0:RH * NB].rearrange("p (h b) -> p h b", h=RH)), v_free)

            def centre(x, sq, n):
                for m in range(4):
                    b = V.take()
                    s.do(dve.scalar_tensor_tensor(x[:, m, :], b[:, 0:NT], -1.0 / n, x[:, m, :], ALU.mult, ALU.add), v_free)
                s.do(mul(sq, x, x), ev("hn_sq"))

            def scale(x, sd, g, bias, out, last):
                until(last)
                s.do(dve.reciprocal(sd, sd))
                s.do(mul(x, x, sd))
                for m in range(4):
                    s.do(dve.tensor_scalar(out[:, m, :], x[:, m, :], vec(g, m), vec(bias, m), ALU.mult, ALU.add))

            until("o_fm")
            centre(OT, OSQ, RDV)
            scale(OT, OSD, "ret_gn_g", "ret_gn_b", OT, "hn_var")
            until("proj7")
            s.do(mul(MIXR, OT, GATE), ev("mix_ready"))

            def layer_norm(c):
                b = V.take()
                for m in range(KD):
                    ins = dve.scalar_tensor_tensor(RES[:, m, :], b[:, 0:NT], -1.0 / D, RES[:, m, :], ALU.mult, ALU.add)
                    s.mark(ins, ev("ln_centred") if m < KD - 1 else v_free)
                dve.wait_ge(ev("lsd_ready"), c + 1)
                s.do(dve.reciprocal(LSD, LSD))
                for m in range(KD):
                    s.mark(mul(RES[:, m, :], RES[:, m, :], LSD), ev("ln_scaled"))

            def out_and_moe(l):
                for m in range(KD):
                    b = V.take()
                    s.do(dve.scalar_tensor_tensor(RES[:, m, :], XT[:, m, :], ALPHA, b[:, 0:NT], ALU.mult, ALU.add), v_free)
                layer_norm(2 * l)
                s.do(dve.memset(LG, 0.0))
                dve.wait_ge(ev("router_in"), 16 * len(router_loads))
                for t, (c0, r) in enumerate(TT):
                    b = V.take()
                    s.do(add(LG[:r, t, :], b[:r, 0:20], RB[:r, l, :]), v_free)
                R = [RT[:, i, :, 0:4] for i in range(10)]
                r1 = [RT[:, i, :, 8:9] for i in range(10)]
                rank = bc(cst("rank"), [P, 3, 4], 1)
                b4 = lambda v: v.to_broadcast([P, 3, 4])

                def pack_taken():
                    for kh in range(4):
                        b = V.take()
                        s.do(dve.tensor_copy(XG[:, 2 * kh:2 * kh + 2, :], b[:, 0:2 * CAP].rearrange("p (k c) -> p k c", k=2)), v_free)

                def first_max(x, onehot, mx, tmp, tmp1, sem=None):
                    s.do(dve.tensor_reduce(mx, x, AX.X, ALU.max))
                    s.do(dve.tensor_tensor(tmp, x, b4(mx), ALU.is_equal))
                    s.do(mul(tmp, tmp, rank))
                    s.do(dve.tensor_reduce(tmp1, tmp, AX.X, ALU.max))
                    s.do(dve.tensor_tensor(onehot, tmp, b4(tmp1), ALU.is_equal), sem)

                lc = LG[:, :, 0:4]
                first_max(lc, R[0], r1[0], R[1], r1[1], ev("group_ready"))
                s.do(sub(R[2], lc, b4(r1[0])), ev("lc_shift"))
                b = V.take()
                s.do(mul(POS, R[0], b[:, 0:12].rearrange("p (t g) -> p t g", t=3)))
                s.do(dve.tensor_copy(CNT, b[:, 12:16]), v_free)
                s.do(dve.tensor_reduce(PLACE, POS, AX.X, ALU.add))
                s.do(dve.tensor_reduce(CNT[:, 0:1], CNT, AX.X, ALU.max))
                s.do(dve.tensor_scalar(OVER[:, l:l + 1], CNT[:, 0:1], CAP + 0.5, None, ALU.is_gt), ev("over_known"))
                for g in range(NG):
                    for t in range(3):
                        ins = dve.tensor_scalar(DSP[:, t, g, :], cst("iota"), PLACE[:, t:t + 1], R[0][:, t, g:g + 1], ALU.is_equal, ALU.mult)
                    s.mark(ins, ev("dispatch_ready"))
                pack_taken()
                dve.wait_ge(ev("lc_exp"), 2 * l + 1)
                s.do(dve.tensor_reduce(r1[2], R[2], AX.X, ALU.add))
                s.do(dve.reciprocal(r1[2], r1[2]))
                w16 = RT[:, 9, :, :]
                g4 = lambda v: v.rearrange("p t (g e) -> p t g e", g=4)
                s.do(mul(g4(w16), g4(LG[:, :, 4:20]), bc(R[0], [P, 3, 4, 4], 3)))
                s.do(dve.tensor_reduce(R[3], w16.rearrange("p t (g e) -> p t e g", g=4), AX.X, ALU.add))
                first_max(R[3], R[4], r1[3], R[1], r1[1])
                s.do(dve.scalar_tensor_tensor(R[5], R[4], -BIG, R[3], ALU.mult, ALU.add))
                first_max(R[5], R[6], r1[4], R[1], r1[1])
                s.do(sub(r1[5], r1[4], r1[3]), ev("lf_diff"))
                dve.wait_ge(ev("lc_exp"), 2 * l + 2)
                s.do(dve.tensor_scalar(r1[6], r1[5], 1.0, None, ALU.add))
                s.do(dve.reciprocal(r1[6], r1[6]))
                s.do(mul(r1[6], r1[6], r1[2]))
                s.do(mul(r1[7], r1[6], r1[5]))
                s.do(mul(R[4], R[4], b4(r1[6])))
                s.do(mul(R[6], R[6], b4(r1[7])))
                s.do(add(R[4], R[4], R[6]), ev("comb_ready"))
                va, aa = mark[f"moe{l}"]

                def at(v, g):
                    return v[:, g, :] if isinstance(g, int) else v[:, bass.ds(g, 1), :].rearrange("p a c -> p (a c)")

                def gated(e, silu_free):
                    b = V.take()
                    dve.wait_ge(a_free, silu_free)
                    s.mark(mul(HB[:, e % 2, :, :], b[:, 0:2 * CAP].rearrange("p (f c) -> p f c", f=2), SIL[:, e % 2, :, :]), v_free)

                def down_taken(e, i):
                    w = at(WG, i)[:, e:e + 1]
                    for h in range(2):
                        b = V.take()
                        y = at(YG, i)[:, 512 * h:512 * h + 512]
                        if e == 0:
                            ins = dve.tensor_scalar(y, b[:, :], w, None, ALU.mult)
                        else:
                            ins = dve.scalar_tensor_tensor(y, b[:, :], w, y, ALU.mult, ALU.add)
                        s.do(ins, v_free)

                def turn(i, last):
                    down_taken(0, i)
                    gated(2, aa + A_GATE[2] + i * EG)
                    down_taken(1, i)
                    gated(3, aa + A_GATE[3] + i * EG)
                    down_taken(2, i)
                    if not last:
                        pack_taken()
                    down_taken(3, i)
                    if not last:
                        gated(0, aa + EG + A_GATE[0] + i * EG)
                        gated(1, aa + EG + A_GATE[1] + i * EG)

                gated(0, aa + A_GATE[0])
                gated(1, aa + A_GATE[1])
                b = V.take()
                s.do(dve.tensor_copy(WG, b[:, 0:NG * EG].rearrange("p (g e) -> p g e", g=NG)), v_free)
                assert V.n == va
                free0 = s.n["v_free"]
                with dve.Fori(0, NG - 1) as i:
                    V.n = va + i * V_GROUP
                    s.n["v_free"] = free0 + i * V_GROUP
                    turn(i, False)
                V.n, s.n["v_free"] = va + V_GROUP * (NG - 1), free0 + V_GROUP * (NG - 1)
                turn(NG - 1, True)
                dve.wait_ge(ev("sum_start"), l + 1)
                for m in range(KD):
                    b = V.take()
                    s.do(add(RES[:, m, :], RES[:, m, :], b[:, 0:NT]), v_free)
                over = dve.value_load(OVER[0:1, l:l + 1], min_val=0, max_val=1)
                with dve.If(over > 0):
                    mine = ev(f"x_dve{l}")
                    t34 = [P, 3, 4]
                    dve.tensor_scalar(PLACE, PLACE, CAP - 0.5, None, ALU.is_gt).then_inc(mine, 1)
                    dve.wait_ge(mine, 1)
                    dve.tensor_tensor(R[4], R[4], bc(PLACE, t34, 2), ALU.mult).then_inc(mine, 1)
                    dve.wait_ge(mine, 2)
                    mul(g4(XC), bc(R[0], [P, 3, 4, 4], 3), bc(R[4], [P, 3, 4, 4], 2)).then_inc(ev(f"x_comb{l}"), 1)
                    dve.wait_ge(ev(f"x_full{l}"), 1)
                    dve.tensor_copy(XCT[0:NE, :], banks[7][0:NE, 0:NT]).then_inc(ev(f"x_comb{l}"), 1)
                    dve.wait_ge(ev(f"x_comb{l}"), 2)
                    with dve.Fori(0, NE) as e:
                        mul(XROW[0:NE, :], XCT[0:NE, :], ident[0:NE, bass.ds(e, 1)].to_broadcast([NE, NT])).then_inc(ev(f"x_row{l}"), 1)
                        dve.wait_ge(ev(f"x_sil{l}"), e + 1)
                        for f in range(2):
                            ins = mul(XSIL[:, f, :], banks[f][:, 0:NT], XSIL[:, f, :])
                        ins.then_inc(mine, 1)
                        dve.wait_ge(mine, e * 2 + 3)
                        for f in range(2):
                            mul(XHB[:, f, :], banks[6][:, 0:NT], XSIL[:, f, :]).then_inc(ev(f"x_h{l}"), 1)
                        dve.wait_ge(ev(f"x_sums{l}"), e + 1)
                        for m in range(KD):
                            ins = add(RES[:, m, :], RES[:, m, :], banks[m][:, 0:NT])
                        ins.then_inc(mine, 1)
                        dve.wait_ge(mine, e * 2 + 4)
                layer_norm(2 * l + 1)

            dve.wait_ge(ev("stores"), 16 * 6)
            out_and_moe(0)
            odd_dve(dve, V, s, until, empty, mul, add, sub, centre, scale, out_and_moe)

        @block.scalar
        def _(act):
            A = Ring(act, AB, a_full, a_free)
            s = Steps(act, act_step)

            for dst, src in s5_loads:
                act.dma_start(dst, src).then_inc(ev("s5_in"), 16)
            for dst, src in vec_loads:
                act.dma_start(dst, src).then_inc(ev("vec_in"), 16)
            act.dma_start(*const_load).then_inc(ev("consts_in"), 16)

            def empty(dst, width, f=ACT.Copy, rows=P, **kw):
                b = A.take()
                return act.activation(dst, b[:rows, 0:width], f, **kw).then_inc(a_free, 1)

            for m in range(4):
                empty(UF[:, m, :], NT)
            act.wait_ge(ev("s5_in"), 16 * len(s5_loads))
            act.activation(ROWS[0:GP, 2, 4:6], LDT, ACT.Exp).then_inc(ev("dt_ready"), 1)
            act.wait_ge(ev("mag_arg"), 1)
            act.activation(ROWS[0:GP, 9, :], ROWS[0:GP, 3, :], ACT.Exp).then_inc(ev("sin_ready"), 1)
            act.wait_ge(ev("sin_arg"), 1)
            act.activation(ROWS[0:GP, 7, :], ROWS[0:GP, 4, :], ACT.Sin).then_inc(ev("sin_ready"), 1)
            act.activation(ROWS[0:GP, 8, :], ROWS[0:GP, 5, :], ACT.Sin).then_inc(ev("sin_ready"), 1)
            for m in range(4):
                empty(QK[:, m, :], NT)
            for m in range(4):
                empty(VF[:, m, :], NT)
            for m in range(4):
                empty(GATE[:, m, :], NT, ACT.Silu)
            act.wait_ge(ev("bi_ready"), 1)
            for j in range(2):
                for g in range(0, GP, 4):
                    b = A.take()
                    act.activation(BIT[:, j, g:g + 4, :], b[:, :].rearrange("p (g f) -> p g f", g=4), ACT.Copy).then_inc(a_free, 1)
            act.wait_ge(ev("uc_in"), 48)
            for q in range(4):
                if q >= 2:
                    act.wait_ge(*mark[f"ug{q - 2}"])
                act.activation(UCQ[0:UCOL, q % 2], UC[0:UCOL, :, P * q:P * q + P].rearrange("p t (g c) -> p g t c", g=8), ACT.Copy).then_inc(ev("ucq_ready"), 1)
            act.wait_ge(ev("k_ready"), 16 * CL)
            for q in range(8):
                b = A.take()
                act.activation(Y[0:HCOL, :, P * (q // 2):P * (q // 2) + P].rearrange("p t (g two c) -> p two g t c", two=2, c=SC_N)[:, q % 2],
                               b[0:HCOL, :].rearrange("p (g t c) -> p g t c", g=4, t=CL), ACT.Copy).then_inc(a_free, 1)
            act.wait_ge(*mark["y_fm"])
            act.activation(ZF, YF, ACT.Gelu_apprx_tanh).then_inc(ev("z_ready"), 1)
            act.wait_ge(ev("z_ready"), 1)
            for m in range(4):
                empty(YF[:, m, :], NT, ACT.Sigmoid, bias=vec("s5_b_glu", m))
            act.wait_ge(ev("y_out"), 32)
            for h in range(RH):
                empty(OT[:, h, 0:NPR], NPR)

            def std(sd, n, e, ring_tiles):
                for m in range(ring_tiles):
                    empty(sd[:, m, :], NT, ACT.Sqrt, scale=1.0 / n, bias=eps[e])

            std(OSD, RDV, 1e-5, 4)

            def layer_norm(c, g, bias, l):
                for m in range(KD):
                    if m < KD - 1:
                        act.wait_ge(ev("ln_centred"), (KD - 1) * c + m + 1)
                    else:
                        act.wait_ge(*mark[f"ln_mean{c}"])
                    act.activation(LSQ[:, m, :], RES[:, m, :], ACT.Square).then_inc(ev("ln_sq"), 1)
                b = A.take()
                act.activation(LSD, b[:, 0:NT], ACT.Sqrt, scale=1.0 / D, bias=eps[1e-5]).then_inc(ev("lsd_ready"), 1)
                act.wait_ge(ev("lsd_ready"), c + 1)
                act.nop().then_inc(a_free, 1)
                for m in range(KD):
                    act.wait_ge(ev("ln_scaled"), KD * c + m + 1)
                    act.activation(XT[:, m, :], RES[:, m, :], ACT.Identity, scale=vec(g, KD * l + m), bias=vec(bias, KD * l + m)).then_inc(ev("ln_done"), 1)

            def moe(l):
                layer_norm(2 * l, "ln1_g", "ln1_b", l)
                for t, (c0, r) in enumerate(TT):
                    for h in range(2):
                        empty(XTM[:r, t, 512 * h:512 * h + 512], 512, rows=r)
                act.wait_ge(ev("lc_shift"), l + 1)
                act.activation(RT[:, 2, :, 0:4], RT[:, 2, :, 0:4], ACT.Exp).then_inc(ev("lc_exp"), 1)
                for g in range(NG):
                    empty(DSPT[:, g, :], NT)
                act.wait_ge(ev("lf_diff"), l + 1)
                act.activation(RT[:, 5, :, 8:9], RT[:, 5, :, 8:9], ACT.Exp).then_inc(ev("lc_exp"), 1)
                va, aa = mark[f"moe{l}"]

                def silu(e):
                    b = A.take()
                    act.activation(SIL[:, e % 2, :, :].rearrange("p f c -> p (f c)"), b[:, 0:2 * CAP], ACT.Silu).then_inc(a_free, 1)

                def turn(i, last):
                    for e, up in ((2, V_UP[0]), (3, V_UP[1])) + (() if last else ((0, V_UP[2]), (1, V_UP[3]))):
                        act.wait_ge(v_free, va + up + i * V_GROUP)
                        silu(e)

                silu(0)
                silu(1)
                assert A.n == aa
                with act.Fori(0, NG - 1) as i:
                    A.n = aa + i * EG
                    turn(i, False)
                A.n = aa + EG * (NG - 1)
                turn(NG - 1, True)
                act.wait_ge(ev("over_known"), l + 1)
                over = act.value_load(OVER[0:1, l:l + 1], min_val=0, max_val=1)
                with act.If(over > 0):
                    with act.Fori(0, NE) as e:
                        act.wait_ge(ev(f"x_full{l}"), e + 2)
                        act.activation(XSIL[:, 0, :], banks[4][:, 0:NT], ACT.Silu)
                        act.activation(XSIL[:, 1, :], banks[5][:, 0:NT], ACT.Silu).then_inc(ev(f"x_sil{l}"), 1)
                layer_norm(2 * l + 1, "ln2_g", "ln2_b", l)

            moe(0)
            odd_act(act, A, s, empty, std, moe)

        @block.gpsimd
        def _(pool):
            s = Steps(pool, pool_step)
            for dst, src in router_loads:
                pool.dma_start(dst, src).then_inc(ev("router_in"), 16)
            for j, n in enumerate(("state_s5_re", "state_s5_im")):
                pool.dma_start(H0R[:, j, :], a[n][0].rearrange("b (g two) s -> (b g) (two s)", two=2)).then_inc(ev("h0_in"), 16)
            pool.wait_ge(ev("bb_ready"), 1)
            sh = [P, GP, CL, SC_N]
            bb = [BB[:, j].unsqueeze(2).to_broadcast(sh) for j in range(2)]
            w1, w2 = TP[:, 0], TP[:, 1]

            def powers(j):
                return PW[:, j, CL - 1::-1, :].rearrange("p l g -> p g l").unsqueeze(3).to_broadcast(sh)

            for o, (x, y, op) in enumerate(((0, 0, ALU.subtract), (0, 1, ALU.add))):
                for h in range(0, GP, 8):
                    g = slice(h, h + 8)
                    s.mark(pool.tensor_tensor(w1[:, g], bb[0][:, g], powers(x if o == 0 else 1)[:, g], ALU.mult), pool_step)
                    s.do(pool.tensor_tensor(w2[:, g], bb[1][:, g], powers(1 if o == 0 else 0)[:, g], ALU.mult))
                    last = o == 1 and h == 8
                    s.do(pool.tensor_tensor(BI[:, o, g], w1[:, g], w2[:, g], op), ev("bi_ready") if last else None)
            pool.wait_ge(*mark["bit"])
            s.mark(pool.memset(UC[0:UCOL], 0.0), ev("uc_zero"))
            pool.wait_ge(*mark["srow"])
            pool.dma_start(srow_dram, SROW[0:NB, :]).then_inc(ev("srow_out"), 16)
            pool.wait_ge(ev("srow_out"), 16)
            pool.dma_start(QS, srow_dram[:, 0:256].rearrange("b (x d) -> b x d", d=16)).then_inc(ev("smp_in"), 16)
            pool.dma_start(KS, srow_dram[:, 256:512].rearrange("b (x d) -> b x d", d=16)).then_inc(ev("smp_in"), 16)
            for q in range(4):
                pool.dma_start(VS[q:P:4, :], srow_dram[:, 512:1024].rearrange("b (h v) -> b h v", v=RDV)).then_inc(ev("smp_in"), 16)
            pool.wait_ge(*mark["y_chunk"])
            pool.dma_start(RETS, a["state_ret"][0].rearrange("b h (q d) v -> (b h q) d v", q=4)).then_inc(ev("smp_in"), 16)
            odd_pool(pool, s)

        @block.sync
        def _(sp):
            out_n = {}

            def store(dst, src, sem="stores"):
                sp.dma_start(dst, src).then_inc(ev(sem), 16)
                out_n[sem] = out_n.get(sem, 0) + 16

            def fill(n):
                if n >= NSLOT:
                    sp.wait_ge(*slot_done[n - NSLOT])
                for dst, src in fills[n]:
                    sp.dma_start(dst, src).then_inc(w_in[n % NSLOT], 16)

            def over_capacity_sp(l):
                sp.wait_ge(*mark[f"moe_out{l}"])
                sp.wait_ge(ev("over_known"), l + 1)
                over = sp.value_load(OVER[0:1, l:l + 1], min_val=0, max_val=1)
                with sp.If(over > 0):
                    for e in range(NE):
                        if e:
                            sp.wait_ge(ev(f"x_sums{l}"), e)
                        for j, name in enumerate(("moe_w_gate", "moe_w_up", "moe_w_down")):
                            sp.dma_start(XW[:, j, :].rearrange("p (k c) -> p k c", k=2 if j == 2 else KD), a[name][l, e].rearrange("(k p) c -> p k c", p=P)).then_inc(ev(f"x_w{l}"), 16)
                    sp.wait_ge(ev(f"x_w{l}"), 48 * NE)

            for dst, src in x_loads:
                sp.dma_start(dst, src).then_inc(ev("x_in"), 16)
            for n in range(NSLOT):
                fill(n)
            sp.wait_ge(*mark["u_tok"])
            for t, (c0, r) in enumerate(TT):
                sp.dma_start(u_dram[c0:c0 + r, :], UTOK[:r, t, :]).then_inc(ev("u_out"), 16)
            for n in (6, 7, 8):
                fill(n)
            sp.wait_ge(ev("uc_zero"), 1)
            sp.wait_ge(ev("u_out"), 48)
            sp.dma_start(UC[0:NCH], u_dram[0:NPR, :].rearrange("(k t) f -> k t f", t=CL)).then_inc(ev("uc_in"), 16)
            sp.dma_start(UC[NCH:HCOL, 0, :], u_dram[NPR:NT, :]).then_inc(ev("uc_in"), 16)
            sp.dma_start(UC[HCOL:UCOL, CL - 1, :], u_dram[NPR:NT, :]).then_inc(ev("uc_in"), 16)
            sp.wait_ge(ev("k_zero"), 1)
            sp.wait_ge(*mark["kl"])
            for t in range(CL):
                sp.dma_start(KT_[SC_N * t:SC_N * t + SC_N, :, SC_N * t:P], KL[0:SC_N, :, 0:P - SC_N * t]).then_inc(ev("k_ready"), 16)
            sp.wait_ge(*mark["y_chunk"])
            sp.dma_start(y_dram[0:NPR, :].rearrange("(k t) f -> k t f", t=CL), Y[0:NCH]).then_inc(ev("y_out"), 16)
            sp.dma_start(y_dram[NPR:NT, :], Y[NCH:HCOL, 0, :]).then_inc(ev("y_out"), 16)
            sp.wait_ge(ev("y_out"), 32)
            for t, (c0, r) in enumerate(TT):
                sp.dma_start(YTOK[:r, t, :], y_dram[c0:c0 + r, :]).then_inc(ev("ytok_in"), 16)
            for n in range(9, S_MOE[0] + 1):
                fill(n)
            sp.wait_ge(*mark["h_rows"])
            for j, n in enumerate((5, 7)):
                store(outs[n][0].rearrange("b (g two) s -> (b g) (two s)", two=2), HROW[:, j, :])
                store(outs[n - 1][0, 0].rearrange("(g two) s -> g (two s)", two=2), HROW[0:GP, 2 + j, :])
            sp.wait_ge(ev("rets_ready"), 1)
            store(outs[3][0].rearrange("b h (q d) v -> (b h q) d v", q=4), RETS)
            sp.wait_ge(*mark["ret_state"])
            store(outs[2][0, 0].rearrange("h d v -> d h v"), RSTO[0:RDK])
            for n in range(S_MOE[0] + 1, S_OD):
                fill(n)
            for n in range(S_OD, S_OD + NSLOT):
                fill(n)
            over_capacity_sp(0)
            odd_sp(sp, store, fill, over_capacity_sp)
            for name, n in out_n.items():
                sp.wait_ge(ev(name), n)


_INS = ["x_prompt", "x_sample", "state_ret", "state_s5_re", "state_s5_im", "state_wkv", "state_shift", "cache_kv",
        "cache_krope", "page_table", "meta_tokens", "ev_w_in", "ret_gn_g", "ret_gn_b", "s5_a_re", "s5_a_im",
        "s5_log_dt", "s5_b_re", "s5_b_im", "s5_c_re", "s5_c_im", "s5_d", "s5_w_glu", "s5_b_glu", "ev_w_out",
        "od_w_in", "rwkv_mu", "rwkv_w0", "rwkv_w2", "rwkv_a0", "rwkv_a2", "rwkv_g2", "rwkv_k_k", "rwkv_k_a",
        "rwkv_r_k", "rwkv_gn_g", "rwkv_gn_b", "mla_q_norm", "mla_w_qb", "mla_kv_norm", "mla_w_uk", "mla_w_uv",
        "od_w_out", "ln1_g", "ln1_b", "ln2_g", "ln2_b", "moe_w_coarse", "moe_b_coarse", "moe_w_fine",
        "moe_b_fine", "moe_w_gate", "moe_w_up", "moe_w_down"]
_OUTS = [(1, SEQ, D), (NB, 1, D), (1, 1, RH, RDK, RDV), (1, NB, RH, RDK, RDV), (1, 1, SG_N, SP_N), (1, NB, SG_N, SP_N),
         (1, 1, SG_N, SP_N), (1, NB, SG_N, SP_N), (1, 1, WH, WD, WD), (1, NB, WH, WD, WD), (1, 1, RP), (1, NB, RP),
         (1, 1, NPR, KVL), (NB, 1, 1, KVL), (1, 1, NPR, ROPE), (NB, 1, 1, ROPE)]


def kernel(**inputs):
    import concourse.bacc as _bacc
    from concourse import mybir as _mybir
    from concourse.bass_utils import run_bass_kernel_spmd as _run

    nc = _bacc.Bacc("TRN2", target_bir_lowering=False, num_devices=1)
    arrays, args = {}, {}
    for name in _INS + ["consts"]:
        v = np.ascontiguousarray(inputs[name]) if name != "consts" else const_table()
        arrays[f"in_{name}"] = v
        args[name] = nc.dram_tensor(f"in_{name}", v.shape, _mybir.dt.from_np(v.dtype), kind="ExternalInput").ap()
    shapes = list(_OUTS)
    outs = [nc.dram_tensor(f"out_{i}", sh, F32, kind="ExternalOutput").ap() for i, sh in enumerate(shapes)]
    program(nc, args, outs)
    r = _run(nc, [arrays], core_ids=[0])
    return tuple(r.results[0][f"out_{i}"] for i in range(len(_OUTS)))
```
